# Optimizing a Trainium2 kernel written in Bass

```python
import math
import jax, jax.numpy as jnp
from jax import lax
import numpy as np

D_MODEL = 1024
BATCH = 1
SEQ = 1024
DEPTH = 1
DEC_BATCH = 1
DEC_SEQ = 32
PAST_LEN = 256

CHUNK = 64
Q_BLOCK = 128
SB_HEADS = 8
SB_HEAD_DIM = 64
SB_WIDTH = SB_HEADS * SB_HEAD_DIM
MLA_HEADS = 8
MLA_NOPE_DIM = 64
MLA_ROPE_DIM = 32
MLA_V_DIM = 64
MLA_Q_LORA = 384
MLA_KV_LORA = 256
MLA_WIDTH = MLA_HEADS * MLA_V_DIM
ROPE_THETA = 10000.0
PEER_HEADS = 8
PEER_N_KEYS = 128
PEER_N_EXPERTS = PEER_N_KEYS * PEER_N_KEYS
PEER_TOPK = 16
PEER_KEY_DIM = 256
PEER_HALF = PEER_KEY_DIM // 2
PEER_BLOCK = 128
ALPHA = (2.0 * DEPTH) ** 0.25
BETA = (8.0 * DEPTH) ** -0.25
EPS = 1e-5
NEG_INF = -1e30
IN_SIZES = (SB_WIDTH, SB_WIDTH, SB_WIDTH, MLA_Q_LORA, MLA_KV_LORA, MLA_ROPE_DIM, D_MODEL, D_MODEL)
IN_SPLITS = tuple(int(s) for s in np.cumsum(IN_SIZES)[:-1])
IN_WIDTH = int(sum(IN_SIZES))

kernel_name = "hybrid_stickbreak_mla_peer_stream_step"

def layer_norm(x, g, b):
    xf = x.astype(jnp.float32)
    mu = jnp.mean(xf, axis=-1, keepdims=True)
    var = jnp.mean(jnp.square(xf - mu), axis=-1, keepdims=True)
    return ((xf - mu) * lax.rsqrt(var + EPS) * g.astype(jnp.float32) + b.astype(jnp.float32)).astype(x.dtype)

def rms_norm(x, g):
    xf = x.astype(jnp.float32)
    ms = jnp.mean(jnp.square(xf), axis=-1, keepdims=True)
    return (xf * lax.rsqrt(ms + EPS) * g.astype(jnp.float32)).astype(x.dtype)

def rope(x, pos):
    half = x.shape[-1] // 2
    inv = ROPE_THETA ** (-jnp.arange(half, dtype=jnp.float32) / half)
    ang = pos.astype(jnp.float32)[:, None] * inv[None, :]
    shape = (ang.shape[0],) + (1,) * (x.ndim - 3) + (half,)
    cos = jnp.cos(ang).reshape(shape).astype(x.dtype)
    sin = jnp.sin(ang).reshape(shape).astype(x.dtype)
    x1, x2 = x[..., :half], x[..., half:]
    return jnp.concatenate([x1 * cos - x2 * sin, x1 * sin + x2 * cos], axis=-1)

def sweep_queries(attend, q_arrays, q_pos):
    tq = q_pos.shape[0]
    if tq <= Q_BLOCK or tq % Q_BLOCK != 0:
        return attend(*q_arrays, q_pos)
    nb = tq // Q_BLOCK

    def split(a):
        return jnp.swapaxes(a.reshape((a.shape[0], nb, Q_BLOCK) + a.shape[2:]), 0, 1)

    blocks = tuple(split(a) for a in q_arrays) + (q_pos.reshape(nb, Q_BLOCK),)
    out = lax.map(lambda args: attend(*args), blocks)
    out = jnp.swapaxes(out, 0, 1)
    return out.reshape((out.shape[0], tq) + out.shape[3:])

def stick_breaking_attend(q, k, v, q_pos, k_pos):
    z = jnp.einsum('bqhd,bkhd->bhqk', q, k, preferred_element_type=jnp.float32) * (SB_HEAD_DIM ** -0.5)
    causal = k_pos[None, :] < q_pos[:, None]
    log_beta = jax.nn.log_sigmoid(z)
    log_one_minus = jnp.where(causal, jax.nn.log_sigmoid(-z), 0.0)
    suffix = lax.cumsum(log_one_minus, axis=3, reverse=True) - log_one_minus
    a = jnp.where(causal, jnp.exp(log_beta + suffix), 0.0)
    return jnp.einsum('bhqk,bkhd->bqhd', a.astype(v.dtype), v)

def mla_attend(q_nope, q_pe, k_nope, k_pe, v, q_pos, k_pos):
    s = (jnp.einsum('bqhd,bkhd->bhqk', q_nope, k_nope, preferred_element_type=jnp.float32)
         + jnp.einsum('bqhr,bkr->bhqk', q_pe, k_pe, preferred_element_type=jnp.float32))
    s = s * ((MLA_NOPE_DIM + MLA_ROPE_DIM) ** -0.5)
    mask = (k_pos // CHUNK)[None, :] <= (q_pos // CHUNK)[:, None]
    p = jax.nn.softmax(jnp.where(mask, s, NEG_INF), axis=-1)
    return jnp.einsum('bhqk,bkhd->bqhd', p.astype(v.dtype), v)

def peer(h, peer_wq, peer_sub_keys, peer_u, peer_v):
    n = h.shape[0]
    nb = -(-n // PEER_BLOCK)
    hp = jnp.pad(h, ((0, nb * PEER_BLOCK - n), (0, 0))).reshape(nb, PEER_BLOCK, D_MODEL)

    def block(xb):
        q = (xb @ peer_wq).reshape(PEER_BLOCK, PEER_HEADS, 2, PEER_HALF)
        s = jnp.einsum('thcd,hckd->thck', q, peer_sub_keys, preferred_element_type=jnp.float32)
        s1, i1 = lax.top_k(s[:, :, 0], PEER_TOPK)
        s2, i2 = lax.top_k(s[:, :, 1], PEER_TOPK)
        cand_s = (s1[..., :, None] + s2[..., None, :]).reshape(PEER_BLOCK, PEER_HEADS, PEER_TOPK * PEER_TOPK)
        cand_i = (i1[..., :, None] * PEER_N_KEYS + i2[..., None, :]).reshape(PEER_BLOCK, PEER_HEADS, PEER_TOPK * PEER_TOPK)
        top_s, top_pos = lax.top_k(cand_s, PEER_TOPK)
        experts = jnp.take_along_axis(cand_i, top_pos, axis=-1)
        g = jax.nn.softmax(top_s, axis=-1).astype(xb.dtype)
        u = peer_u[experts]
        act = jax.nn.gelu(jnp.einsum('thkd,td->thk', u, xb), approximate=False)
        v = peer_v[experts]
        return jnp.einsum('thk,thkd->td', g * act, v)

    out = lax.map(block, hp).reshape(nb * PEER_BLOCK, D_MODEL)
    return out[:n]

def layer(x, q_pos, past, w_in, q_norm_g, w_uq, kv_norm_g, w_uk, w_uv, w_oa, w_ob, w_out,
          ln1_g, ln1_b, peer_wq, peer_sub_keys, peer_u, peer_v, ln2_g, ln2_b):
    b, t, _ = x.shape
    proj = x @ w_in
    sb_q, sb_k, sb_v, c_q, c_kv, k_r, g_a, g_b = jnp.split(proj, IN_SPLITS, axis=-1)
    sb_q = sb_q.reshape(b, t, SB_HEADS, SB_HEAD_DIM)
    sb_k = sb_k.reshape(b, t, SB_HEADS, SB_HEAD_DIM)
    sb_v = sb_v.reshape(b, t, SB_HEADS, SB_HEAD_DIM)
    q = (rms_norm(c_q, q_norm_g) @ w_uq).reshape(b, t, MLA_HEADS, MLA_NOPE_DIM + MLA_ROPE_DIM)
    q_nope = q[..., :MLA_NOPE_DIM]
    q_pe = rope(q[..., MLA_NOPE_DIM:], q_pos)
    ckv = rms_norm(c_kv, kv_norm_g)
    kpe = rope(k_r, q_pos)
    new_state = (sb_k, sb_v, ckv, kpe)
    if past is None:
        k_sb, v_sb, ckv_all, kpe_all = new_state
        k_pos = q_pos
    else:
        p_k, p_v, p_ckv, p_kpe = past
        k_sb = jnp.concatenate([p_k, sb_k], axis=1)
        v_sb = jnp.concatenate([p_v, sb_v], axis=1)
        ckv_all = jnp.concatenate([p_ckv, ckv], axis=1)
        kpe_all = jnp.concatenate([p_kpe, kpe], axis=1)
        k_pos = jnp.concatenate([jnp.arange(p_k.shape[1], dtype=jnp.int32), q_pos])
    tk = ckv_all.shape[1]
    k_nope = (ckv_all @ w_uk).reshape(b, tk, MLA_HEADS, MLA_NOPE_DIM)
    v_mla = (ckv_all @ w_uv).reshape(b, tk, MLA_HEADS, MLA_V_DIM)

    o_a = sweep_queries(lambda qb, pb: stick_breaking_attend(qb, k_sb, v_sb, pb, k_pos), (sb_q,), q_pos)
    o_b = sweep_queries(lambda qn, qe, pb: mla_attend(qn, qe, k_nope, kpe_all, v_mla, pb, k_pos),
                        (q_nope, q_pe), q_pos)
    merged = (jax.nn.sigmoid(g_a) * (o_a.reshape(b, t, SB_WIDTH) @ w_oa)
              + jax.nn.sigmoid(g_b) * (o_b.reshape(b, t, MLA_WIDTH) @ w_ob))
    h = layer_norm(ALPHA * x + merged @ w_out, ln1_g, ln1_b)
    ff = peer(h.reshape(b * t, D_MODEL), peer_wq, peer_sub_keys, peer_u, peer_v).reshape(b, t, D_MODEL)
    y = layer_norm(ALPHA * h + ff, ln2_g, ln2_b)
    return y, new_state

def setup_inputs(seed: int = 0) -> dict:
    key = jax.random.key(seed)
    ks = jax.random.split(key, 24)
    nrm = jax.random.normal
    f32 = jnp.float32
    w_in = jnp.concatenate([
        nrm(ks[0], (DEPTH, D_MODEL, 2 * SB_WIDTH), f32) * D_MODEL ** -0.5,
        nrm(ks[1], (DEPTH, D_MODEL, SB_WIDTH), f32) * (D_MODEL ** -0.5 * BETA),
        nrm(ks[2], (DEPTH, D_MODEL, IN_WIDTH - 3 * SB_WIDTH), f32) * D_MODEL ** -0.5,
    ], axis=-1)
    return {
        "x_prompt": nrm(ks[3], (BATCH, SEQ, D_MODEL), f32),
        "x_sample": nrm(ks[4], (DEC_BATCH, DEC_SEQ, D_MODEL), f32),
        "cache_sb_k": nrm(ks[5], (DEPTH, DEC_BATCH, PAST_LEN, SB_HEADS, SB_HEAD_DIM), f32),
        "cache_sb_v": nrm(ks[6], (DEPTH, DEC_BATCH, PAST_LEN, SB_HEADS, SB_HEAD_DIM), f32) * BETA,
        "cache_mla_ckv": nrm(ks[7], (DEPTH, DEC_BATCH, PAST_LEN, MLA_KV_LORA), f32),
        "cache_mla_kpe": nrm(ks[8], (DEPTH, DEC_BATCH, PAST_LEN, MLA_ROPE_DIM), f32),
        "w_in": w_in,
        "q_norm_g": 1.0 + 0.01 * nrm(ks[9], (DEPTH, MLA_Q_LORA), f32),
        "w_uq": nrm(ks[10], (DEPTH, MLA_Q_LORA, MLA_HEADS * (MLA_NOPE_DIM + MLA_ROPE_DIM)), f32) * MLA_Q_LORA ** -0.5,
        "kv_norm_g": 1.0 + 0.01 * nrm(ks[11], (DEPTH, MLA_KV_LORA), f32),
        "w_uk": nrm(ks[12], (DEPTH, MLA_KV_LORA, MLA_HEADS * MLA_NOPE_DIM), f32) * MLA_KV_LORA ** -0.5,
        "w_uv": nrm(ks[13], (DEPTH, MLA_KV_LORA, MLA_HEADS * MLA_V_DIM), f32) * (MLA_KV_LORA ** -0.5 * BETA),
        "w_oa": nrm(ks[14], (DEPTH, SB_WIDTH, D_MODEL), f32) * (SB_WIDTH ** -0.5 * BETA),
        "w_ob": nrm(ks[15], (DEPTH, MLA_WIDTH, D_MODEL), f32) * (MLA_WIDTH ** -0.5 * BETA),
        "w_out": nrm(ks[16], (DEPTH, D_MODEL, D_MODEL), f32) * (D_MODEL ** -0.5 * BETA),
        "ln1_g": 1.0 + 0.01 * nrm(ks[17], (DEPTH, D_MODEL), f32),
        "ln1_b": 0.01 * nrm(ks[18], (DEPTH, D_MODEL), f32),
        "peer_wq": nrm(ks[19], (DEPTH, D_MODEL, PEER_HEADS * PEER_KEY_DIM), f32) * D_MODEL ** -0.5,
        "peer_sub_keys": nrm(ks[20], (DEPTH, PEER_HEADS, 2, PEER_N_KEYS, PEER_HALF), f32) * PEER_HALF ** -0.5,
        "peer_u": nrm(ks[21], (DEPTH, PEER_N_EXPERTS, D_MODEL), f32) * D_MODEL ** -0.5,
        "peer_v": nrm(ks[22], (DEPTH, PEER_N_EXPERTS, D_MODEL), f32) * BETA,
        "ln2_g": 1.0 + 0.01 * nrm(ks[23], (DEPTH, D_MODEL), f32),
        "ln2_b": 0.01 * nrm(jax.random.fold_in(ks[23], 1), (DEPTH, D_MODEL), f32),
    }

def reference(x_prompt, x_sample, cache_sb_k, cache_sb_v, cache_mla_ckv, cache_mla_kpe,
              w_in, q_norm_g, w_uq, kv_norm_g, w_uk, w_uv, w_oa, w_ob, w_out, ln1_g, ln1_b,
              peer_wq, peer_sub_keys, peer_u, peer_v, ln2_g, ln2_b):
    past_len = cache_sb_k.shape[2]
    pos_prompt = jnp.arange(x_prompt.shape[1], dtype=jnp.int32)
    pos_sample = past_len + jnp.arange(x_sample.shape[1], dtype=jnp.int32)
    y_p, y_s = x_prompt, x_sample
    states_p, states_s = [], []
    for l in range(DEPTH):
        w = (w_in[l], q_norm_g[l], w_uq[l], kv_norm_g[l], w_uk[l], w_uv[l], w_oa[l], w_ob[l], w_out[l],
             ln1_g[l], ln1_b[l], peer_wq[l], peer_sub_keys[l], peer_u[l], peer_v[l], ln2_g[l], ln2_b[l])
        y_p, st_p = layer(y_p, pos_prompt, None, *w)
        past = (cache_sb_k[l], cache_sb_v[l], cache_mla_ckv[l], cache_mla_kpe[l])
        y_s, st_s = layer(y_s, pos_sample, past, *w)
        states_p.append(st_p)
        states_s.append(st_s)
    sb_k_p = jnp.stack([s[0] for s in states_p])
    sb_v_p = jnp.stack([s[1] for s in states_p])
    ckv_p = jnp.stack([s[2] for s in states_p])
    kpe_p = jnp.stack([s[3] for s in states_p])
    sb_k_s = jnp.stack([s[0] for s in states_s])
    sb_v_s = jnp.stack([s[1] for s in states_s])
    ckv_s = jnp.stack([s[2] for s in states_s])
    kpe_s = jnp.stack([s[3] for s in states_s])
    return (y_p, y_s, sb_k_p, sb_v_p, ckv_p, kpe_p, sb_k_s, sb_v_s, ckv_s, kpe_s)


_drawn_inputs = setup_inputs


def setup_inputs(seed=0):
    import zlib

    import numpy as np

    out = dict(_drawn_inputs(seed))
    spreads = {}
    factors = {'cache_sb_k': 4.814,
     'cache_sb_v': 2.985,
     'cache_mla_kpe': 2.955,
     'q_norm_g': 8.0,
     'kv_norm_g': 5.64,
     'ln2_g': 5.734,
     'ln2_b': 5.545}
    for name, (base, spread) in spreads.items():
        noise = np.random.default_rng([zlib.crc32(name.encode()), seed]).standard_normal(out[name].shape)
        drawn = base * np.exp(spread * noise) if base else spread * noise
        out[name] = __import__('jax').numpy.asarray(drawn.astype(out[name].dtype))
    for name, factor in factors.items():
        out[name] = (out[name] * factor).astype(out[name].dtype)
    return out
```

```python
from contextlib import ExitStack

import concourse.bass as bass
from concourse import mybir

F32 = mybir.dt.float32
BF16 = mybir.dt.bfloat16
U32 = mybir.dt.uint32
ALU = mybir.AluOpType
ACT = mybir.ActivationFunctionType
AX = mybir.AxisListType.X

P = 128
D = 1024
KC = D // P
SEQ, NEW, PAST = 1024, 32, 256
TOKENS = SEQ + NEW
KEYS = TOKENS + PAST
TILES = SEQ // P
SPAN = 352
SPANS = TOKENS // SPAN
HEADS, HD = 8, 64
SBW = HEADS * HD
QL, KVL, RD = 384, 256, 32
QC, VC = QL // P, KVL // P
MD = HD + RD
CHUNK = 64
PKEYS, TOPK, EXPERTS = 128, 16, 128 * 128
SLOTS = 8
LAG = 2
ALPHA = 2.0 ** 0.25
EPS = 1e-5
MLA_SCALE = float(MD) ** -0.5
FAR = -1.0e30
LOWEST = -3.0e38


def rows_of(tile):
    return P if tile < TILES else NEW


class Memory:

    BASE = 16512

    def __init__(self, nc):
        self.nc = nc

    def at(self, name, offset, shape, dtype=F32):
        return self.nc.alloc_sbuf_tensor_at(name, shape, dtype, offset=self.BASE + offset)


def hybrid_stream_step(nc, a):
    mem = Memory(nc)
    m = {}
    m["qT"] = mem.at("sb_qT", 66560, [P, 4, TOKENS])
    m["kT"] = mem.at("sb_kT", 83456, [P, 4, KEYS])
    m["v"] = mem.at("sb_v", 104448, [P, 11, SBW])
    m["oaT"] = mem.at("sb_outT", 142336, [P, 4, TOKENS])
    m["obT"] = mem.at("mla_outT", 159232, [P, 4, TOKENS])
    m["craw"] = mem.at("latents_raw", 176128, [P, QC + VC, TOKENS])
    m["kpeT"] = mem.at("kpeT", 197248, [P, KEYS])
    m["cos"] = mem.at("cosT", 202496, [P, TOKENS])
    m["sin"] = mem.at("sinT", 206720, [P, TOKENS])
    m["ident"] = mem.at("identity", 210944, [P, P])
    m["negtri"] = mem.at("minus_triangle", 211456, [P, P])
    m["negones"] = mem.at("minus_ones", 211968, [P, P])
    m["eps"] = mem.at("epsilon", 212480, [P, 1])
    m["mqT"] = mem.at("mla_qT", 0, [P, HEADS, TOKENS])
    m["mkT"] = mem.at("mla_kT", 33792, [P, HEADS, KEYS])
    m["mv"] = mem.at("mla_v", 75776, [P, 11, SBW])
    m["mergedT"] = mem.at("mergedT", 107520, [P, KC, TOKENS])
    m["hT"] = mem.at("hT", 0, [P, KC, TOKENS])
    m["h"] = mem.at("h", 33792, [P, TILES + 1, D])
    m["acc"] = mem.at("ff_sum", 70656, [P, TILES + 1, D])
    project(nc, mem, a, m)
    stick_attend(nc, mem, m)
    mla_project(nc, mem, a, m)
    mla_attend(nc, mem, m)
    merge(nc, mem, a, m)
    first_norm(nc, mem, a, m)
    experts(nc, mem, a, m)
    last_norm(nc, mem, a, m)


def sems(nc, stack, *names):
    return [stack.enter_context(nc.semaphore(n)) for n in names]


def banks(nc, stack, name, n):
    return [stack.enter_context(nc.psum_tensor(f"{name}{i}", [P, 512], F32)) for i in range(n)]


def project(nc, mem, a, m):
    with ExitStack() as s:
        xT = mem.at("xT", 0, [P, KC, TOKENS])
        w = [mem.at(f"w_in_block{i}", 33792 + 16384 * i, [P, KC, 512]) for i in range(2)]
        gate = [mem.at(f"gate_stage{i}", 126976 + 1408 * i, [P, SPAN]) for i in range(4)]
        turned = [mem.at(f"rope_part{i}", 132608 + 1408 * i, [P, SPAN]) for i in range(2)]
        NB = 8
        ps = banks(nc, s, "proj_ps", NB)
        c0 = 3 * SBW
        blocks = [(0, SBW, "q"), (SBW, SBW, "k"), (2 * SBW, SBW, "v"), (c0, QL, "c"),
                  (c0 + QL, KVL + RD, "ckr"), *[(c0 + QL + KVL + RD + 512 * i, 512, "g") for i in range(4)]]
        plan = []
        for b, (_, width, kind) in enumerate(blocks):
            if kind == "v":
                plan += [(b, "v", 0, t, 0) for t in range(TILES + 1)]
                continue
            for j in range(width // P):
                plan += [(b, kind[0], P * j, {"c": j + QC * (kind == "ckr")}.get(kind[0], j), c) for c in range(SPANS)]
            if kind == "ckr":
                plan += [(b, r, KVL + (0 if r == "r" else RD), 0, c) for c in range(SPANS) for r in "rs"]
        on_act = [kind == "g" for _, kind, *_ in plan]
        freed_by = [sum(1 for k in range(n + 1) if on_act[k] == on_act[n]) for n in range(len(plan))]

        x_in, fixed_in, filled, copied, squashed, sine_done, out_done, made = sems(
            nc, s, "x_in", "fixed_in", "p_filled", "p_copied", "p_squashed", "sine_part_done", "p_out", "const_made")
        w_in = sems(nc, s, "w_in_a", "w_in_b")
        gate_out = sems(nc, s, *[f"gate_out{i}" for i in range(4)])
        last_of = {b: max(n for n, e in enumerate(plan) if e[0] == b) for b in range(len(blocks))}
        block = s.enter_context(nc.Block())

        @block.sync
        def _(sp):
            for b, (col, width, kind) in enumerate(blocks):
                if b >= 2:
                    sp.wait_ge(filled, last_of[b - 2] + 1)
                sp.dma_start(w[b % 2][:, :, 0:width],
                             a["w_in"].rearrange("(k p) c -> p k c", p=P)[:, :, col:col + width]).then_inc(w_in[b % 2], 16)
                if kind == "ckr":
                    sp.dma_start(w[b % 2][:, :, width:width + RD],
                                 a["w_kr_swapped"].rearrange("(k p) c -> p k c", p=P)).then_inc(w_in[b % 2], 16)
                if b == 0:
                    for c in range(SPANS):
                        sp.dma_start(xT[:, :, SPAN * c:SPAN * (c + 1)],
                                     a["xT"].rearrange("(k p) t -> p k t", p=P)[:, :, SPAN * c:SPAN * (c + 1)]).then_inc(x_in, 16)
                if b == 1:
                    sp.dma_start(m["kT"][:, :, TOKENS:KEYS],
                                 a["past_sb_kT"].rearrange("(k p) t -> p k t", p=P)).then_inc(fixed_in, 16)
                    sp.dma_start(m["v"][:, TILES + 1:TILES + 3, :],
                                 a["past_sb_v"].rearrange("(k p) c -> p k c", p=P)).then_inc(fixed_in, 16)
                    sp.dma_start(m["kpeT"][HD:MD, TOKENS:KEYS], a["past_kpeT"]).then_inc(fixed_in, 16)
                    sp.dma_start(m["cos"][HD:MD, :], a["cosT"]).then_inc(fixed_in, 16)
                    sp.dma_start(m["sin"][HD:MD, :], a["sinT"]).then_inc(fixed_in, 16)
            copies = lambda b: sum(1 for n in range(last_of[b] + 1) if not on_act[n])
            sp.wait_ge(copied, copies(1))
            sp.dma_start(a["out_kT"].rearrange("(k p) t -> p k t", p=P), m["kT"][:, :, 0:TOKENS]).then_inc(out_done, 16)
            sp.wait_ge(copied, copies(2))
            sp.dma_start(a["out_v"][0:SEQ, :].rearrange("(k p) c -> p k c", p=P), m["v"][:, 0:TILES, :]).then_inc(out_done, 16)
            sp.dma_start(a["out_v"][SEQ:TOKENS, :], m["v"][0:NEW, TILES, :]).then_inc(out_done, 16)
            sp.wait_ge(copied, sum(1 for x in on_act if not x))
            sp.dma_start(a["out_kpeT"], m["kpeT"][HD:MD, 0:TOKENS]).then_inc(out_done, 16)
            for i in range(4):
                sp.wait_ge(gate_out[i], 4 * sum(on_act))
            sp.wait_ge(out_done, 64)
            sp.wait_ge(fixed_in, 80)

        @block.gpsimd
        def _(pool):
            pool.memset(m["ident"][:], 0.0).then_inc(made, 1)
            pool.memset(m["negtri"][:], -1.0).then_inc(made, 1)
            pool.memset(m["negones"][:], -1.0).then_inc(made, 1)
            pool.memset(m["eps"][:], EPS).then_inc(made, 1)
            pool.wait_ge(made, 4)
            pool.affine_select(out=m["ident"][:], in_=m["ident"][:], compare_op=ALU.not_equal, fill=1.0, base=0,
                               pattern=[[-1, P]], channel_multiplier=1).then_inc(made, 1)
            pool.affine_select(out=m["negtri"][:], in_=m["negtri"][:], compare_op=ALU.is_ge, fill=0.0, base=0,
                               pattern=[[-1, P]], channel_multiplier=1).then_inc(made, 1)
            pool.wait_ge(made, 6)

        @block.tensor
        def _(pe):
            pe.wait_ge(x_in, 16 * SPANS)
            seen = -1
            for n, (b, kind, col, j, c) in enumerate(plan):
                if b != seen:
                    seen = b
                    pe.wait_ge(w_in[b % 2], 16 * (b // 2 + 1 + (b % 2 == 0 and b >= 4)))
                if n >= NB:
                    k = n - NB
                    pe.wait_ge(squashed if on_act[k] else copied, freed_by[k])
                out = ps[n % NB]
                for k in range(KC):
                    if kind == "v":
                        r = rows_of(j)
                        mm = nc.tensor.matmul(out[0:r, :], xT[:, k, P * j:P * j + r], w[b % 2][:, k, :],
                                              start=(k == 0), stop=(k == KC - 1))
                    elif kind in "rs":
                        mm = nc.tensor.matmul(out[HD:MD, 0:SPAN], w[b % 2][:, k, col:col + RD],
                                              xT[:, k, SPAN * c:SPAN * (c + 1)], start=(k == 0), stop=(k == KC - 1))
                    else:
                        mm = nc.tensor.matmul(out[:, 0:SPAN], w[b % 2][:, k, col:col + P],
                                              xT[:, k, SPAN * c:SPAN * (c + 1)], start=(k == 0), stop=(k == KC - 1))
                mm.then_inc(filled, 1)

        @block.vector
        def _(dve):
            dve.wait_ge(fixed_in, 80)
            done = 0
            for n, (b, kind, col, j, c) in enumerate(plan):
                if kind == "g":
                    continue
                dve.wait_ge(filled, n + 1)
                cols = slice(SPAN * c, SPAN * (c + 1))
                src = ps[n % NB]
                if kind == "q":
                    nc.vector.tensor_scalar(m["qT"][:, j, cols], src[:, 0:SPAN], float(HD) ** -0.5, None, ALU.mult).then_inc(copied, 1)
                elif kind == "k":
                    nc.vector.tensor_copy(m["kT"][:, j, cols], src[:, 0:SPAN]).then_inc(copied, 1)
                elif kind == "v":
                    r = rows_of(j)
                    nc.vector.tensor_copy(m["v"][0:r, j, :], src[0:r, :]).then_inc(copied, 1)
                elif kind == "c":
                    nc.vector.tensor_copy(m["craw"][:, j, cols], src[:, 0:SPAN]).then_inc(copied, 1)
                elif kind == "r":
                    if done >= 2:
                        dve.wait_ge(copied, done)
                    nc.vector.tensor_tensor(turned[0][HD:MD, :], src[HD:MD, 0:SPAN], m["cos"][HD:MD, cols], ALU.mult).then_inc(copied, 1)
                else:
                    dve.wait_ge(copied, done)
                    nc.vector.tensor_tensor(turned[1][HD:MD, :], src[HD:MD, 0:SPAN], m["sin"][HD:MD, cols], ALU.mult).then_inc(sine_done, 1)
                    dve.wait_ge(sine_done, c + 1)
                    nc.vector.tensor_tensor(m["kpeT"][HD:MD, cols], turned[0][HD:MD, :], turned[1][HD:MD, :], ALU.add).then_inc(copied, 1)
                done += 1

        @block.scalar
        def _(act):
            n = 0
            for e, (b, kind, col, j, c) in enumerate(plan):
                if kind != "g":
                    continue
                act.wait_ge(filled, e + 1)
                if n >= 4:
                    act.wait_ge(gate_out[n % 4], 16 * (n // 4))
                nc.scalar.activation(gate[n % 4][:], ps[e % NB][:, 0:SPAN], ACT.Sigmoid).then_inc(squashed, 1)
                act.wait_ge(squashed, n + 1)
                row = 512 * (b - 5) + P * j
                act.dma_start(a["gatesT"][row:row + P, SPAN * c:SPAN * (c + 1)], gate[n % 4][:]).then_inc(gate_out[n % 4], 16)
                n += 1


def stick_attend(nc, mem, m):
    with ExitStack() as s:
        items = []
        for i in range(TILES + 1):
            nq = rows_of(i)
            tiles = [(P * j, P, j, j == i) for j in range(i, -1, -1)] if i < TILES else \
                    [(SEQ, NEW, TILES, True), (TOKENS + P, P, TILES + 2, False), (TOKENS, P, TILES + 1, False)]
            for x, (key, rows, vt, diag) in enumerate(tiles):
                for par in range(2):
                    items.append((i, nq, key, rows, vt, diag, par, x == len(tiles) - 1))
        N = len(items)
        E, S, R, A = 3, 4, 6, 3
        e = [mem.at(f"abs_exp_ln{i}", 2048 * i, [P, 512]) for i in range(E)]
        sp_ = [mem.at(f"softplus{i}", 2048 * (E + i), [P, 512]) for i in range(S)]
        rest = [mem.at(f"later_sum{i}", 2048 * (E + S + i), [P, 512]) for i in range(R)]
        w = [mem.at(f"weights{i}", 2048 * (E + S + R + i), [P, 512]) for i in range(A)]
        before = mem.at("earlier_mask", 40960, [P, P])
        far = mem.at("far_mask", 41472, [P, P])
        zb = banks(nc, s, "z_ps", 3)
        sb = banks(nc, s, "log_weight_ps", 2)
        ob = banks(nc, s, "stick_out_ps", 2)
        masks, z_done, chain, ln_done, sp_done, sp_masked, rest_done, zeroed, s_done, w_done, av_done, o_done, o_copied = sems(
            nc, s, "masks", "z_done", "act_step", "ln_done", "sp_done", "sp_masked", "rest_done", "rest_zeroed",
            "log_weight_done", "weight_done", "av_done", "stick_o_done", "stick_o_copied")
        block = s.enter_context(nc.Block())
        diag_upto = lambda n: sum(1 for k in range(n + 1) if items[k][5])
        rest_upto = lambda n: sum(1 for k in range(n + 1) if not items[k][7])

        def scores(bank, n, more):
            i, nq, key, rows, vt, diag, par, last = items[n]
            for x in range(4):
                mm = nc.tensor.matmul(bank[0:rows, nq * x:nq * (x + 1)], m["kT"][HD * par:HD * par + HD, x, key:key + rows],
                                      m["qT"][HD * par:HD * par + HD, x, P * i:P * i + nq], start=(x == 0),
                                      stop=(x == 3 and not more), skip_group_check=True)
            return mm

        @block.gpsimd
        def _(pool):
            pool.memset(before[:], 1.0).then_inc(masks, 1)
            pool.memset(far[:], 0.0).then_inc(masks, 1)
            pool.wait_ge(masks, 2)
            pool.affine_select(out=before[:], in_=before[:], compare_op=ALU.is_gt, fill=0.0, base=0,
                               pattern=[[1, P]], channel_multiplier=-1).then_inc(masks, 1)
            pool.affine_select(out=far[:], in_=far[:], compare_op=ALU.is_gt, fill=FAR, base=0,
                               pattern=[[1, P]], channel_multiplier=-1).then_inc(masks, 1)

        @block.tensor
        def _(pe):
            pe.wait_ge(masks, 4)
            for t in range(N + 4):
                if t < N:
                    if t >= 3:
                        pe.wait_ge(sp_done, t - 2)
                    scores(zb[t % 3], t, False).then_inc(z_done, 1)
                n = t - 2
                if 0 <= n < N:
                    i, nq, key, rows, vt, diag, par, last = items[n]
                    cols = slice(0, 4 * nq)
                    if n >= 2:
                        pe.wait_ge(w_done, n - 1)
                    scores(sb[n % 2], n, True)
                    if diag:
                        for x in range(4):
                            nc.tensor.matmul(sb[n % 2][0:rows, nq * x:nq * (x + 1)], m["ident"][0:rows, 0:rows], far[0:rows, 0:nq],
                                             start=False, stop=False, skip_group_check=True)
                        pe.wait_ge(sp_masked, diag_upto(n))
                    else:
                        kr = items[n - 2][3]
                        pe.wait_ge(rest_done, rest_upto(n - 2))
                        nc.tensor.matmul(sb[n % 2][0:rows, cols], m["negones"][0:P, 0:rows], rest[(n - 2) % R][:, cols],
                                         start=False, stop=False, skip_group_check=True)
                        pe.wait_ge(sp_done, n + 1)
                    nc.tensor.matmul(sb[n % 2][0:rows, cols], m["negtri"][0:rows, 0:rows], sp_[n % S][0:rows, cols],
                                     start=False, stop=True, skip_group_check=True).then_inc(s_done, 1)
                n = t - 4
                if 0 <= n < N:
                    i, nq, key, rows, vt, diag, par, last = items[n]
                    pe.wait_ge(w_done, n + 1)
                    if diag and i >= 1:
                        pe.wait_ge(o_copied, 2 * (i - 1) + par + 1)
                    for x in range(4):
                        h = 2 * x + par
                        mm = nc.tensor.matmul(ob[par][HD * par:HD * par + HD, nq * x:nq * (x + 1)], m["v"][0:rows, vt, HD * h:HD * (h + 1)],
                                              w[n % A][0:rows, nq * x:nq * (x + 1)], start=(diag and x == 0), stop=last,
                                              skip_group_check=True)
                    mm.then_inc(av_done, 1)

        @block.scalar
        def _(act):
            steps = 0
            for t in range(N + 2):
                if t < N:
                    i, nq, key, rows, vt, diag, par, last = items[t]
                    buf, src = e[t % E][0:rows, 0:4 * nq], zb[t % 3][0:rows, 0:4 * nq]
                    act.wait_ge(z_done, t + 1)
                    if t >= E:
                        act.wait_ge(sp_done, t - E + 1)
                    nc.scalar.activation(buf, src, ACT.Abs).then_inc(chain, 1)
                    act.wait_ge(chain, steps + 1)
                    nc.scalar.activation(buf, buf, ACT.Exp, scale=-1.0).then_inc(chain, 1)
                    act.wait_ge(chain, steps + 2)
                    nc.scalar.activation(buf, buf, ACT.Ln, bias=1.0).then_inc(ln_done, 1)
                    steps += 2
                n = t - 2
                if 0 <= n < N:
                    i, nq, key, rows, vt, diag, par, last = items[n]
                    act.wait_ge(s_done, n + 1)
                    if n >= A:
                        act.wait_ge(av_done, n - A + 1)
                    nc.scalar.activation(w[n % A][0:rows, 0:4 * nq], sb[n % 2][0:rows, 0:4 * nq], ACT.Exp).then_inc(w_done, 1)

        @block.vector
        def _(dve):
            dve.wait_ge(masks, 4)
            ends = [n for n in range(N) if items[n][7]]
            zeros = 0
            for t in range(N + 5):
                if t < N:
                    i, nq, key, rows, vt, diag, par, last = items[t]
                    cols = slice(0, 4 * nq)
                    dve.wait_ge(ln_done, t + 1)
                    if t >= S:
                        dve.wait_ge(s_done, t - S + 1)
                    own = sp_[t % S][0:rows, cols]
                    nc.vector.scalar_tensor_tensor(own, zb[t % 3][0:rows, cols], 0.0, e[t % E][0:rows, cols],
                                                   ALU.max, ALU.add).then_inc(sp_done, 1)
                    dve.wait_ge(sp_done, t + 1)
                    if diag:
                        v3 = own.rearrange("p (x q) -> p x q", x=4)
                        nc.vector.tensor_tensor(v3, v3, before[0:rows, 0:nq].unsqueeze(1).broadcast_to([rows, 4, nq]), ALU.mult).then_inc(sp_masked, 1)
                        dve.wait_ge(sp_masked, diag_upto(t))
                    if not last:
                        out = rest[t % R]
                        if rows < P:
                            nc.vector.memset(out[:, cols], 0.0).then_inc(zeroed, 1)
                            zeros += 1
                            dve.wait_ge(zeroed, zeros)
                        if diag:
                            nc.vector.tensor_copy(out[0:rows, cols], own).then_inc(rest_done, 1)
                        else:
                            dve.wait_ge(rest_done, rest_upto(t - 2))
                            nc.vector.tensor_tensor(out[:, cols], own, rest[(t - 2) % R][:, cols], ALU.add).then_inc(rest_done, 1)
                n = t - 5
                if n in ends:
                    i, nq, key, rows, vt, diag, par, last = items[n]
                    dve.wait_ge(av_done, n + 1)
                    nc.vector.tensor_copy(m["oaT"][HD * par:HD * par + HD, :, P * i:P * i + nq],
                                          ob[par][HD * par:HD * par + HD, 0:4 * nq].rearrange("p (x q) -> p x q", x=4)).then_inc(o_copied, 1)


def mla_project(nc, mem, a, m):
    with ExitStack() as s:
        cqT = mem.at("query_latentT", 98304, [P, QC, TOKENS])
        ckvT = mem.at("kv_latentT", 110976, [P, VC, KEYS])
        w_uq = mem.at("w_uq", 121472, [P, QC, HEADS * MD])
        w_uqs = mem.at("w_uq_swapped", 130688, [P, QC, HEADS * RD])
        w_uk = mem.at("w_uk", 133760, [P, VC, SBW])
        w_uv = mem.at("w_uv", 137856, [P, VC, SBW])
        g = mem.at("norm_gains", 141952, [P, QC + VC])
        sq = [mem.at(f"squares{i}", 159232 + 1408 * i, [P, SPAN]) for i in range(3)]
        root = [mem.at(f"roots{i}", 163456 + 1408 * i, [P, SPAN]) for i in range(2)]
        inv = [mem.at(f"inverse_roots{i}", 166272 + 1408 * i, [P, SPAN]) for i in range(2)]
        part = [mem.at(f"rope_q{i}", 169088 + 1408 * i, [P, SPAN]) for i in range(2)]
        ss = banks(nc, s, "square_sum_ps", 2)
        NB = 6
        ps = banks(nc, s, "mla_ps", NB)
        w_in, past_in, g_in, sq_done, ss_done, root_done, inv_done, normed, filled, copied, roped, kpe_in, out_done = sems(
            nc, s, "uw_in", "past_in", "gain_in", "sq_done", "ss_done", "root_done", "inv_done", "normed",
            "m_filled", "m_copied", "m_roped", "m_kpe", "m_out")
        norms = [(c, lat) for c in range(SPANS) for lat in range(2)]
        chunks = lambda lat: range(QC) if lat == 0 else range(QC, QC + VC)
        plan = []
        for c in range(SPANS):
            for h in range(HEADS):
                plan += [("q", h, c, 0), ("s", h, c, 0)]
        key_spans = [(c * SPAN, SPAN) for c in range(SPANS)] + [(TOKENS, PAST)]
        for c, width in key_spans:
            plan += [("k", h, c, width) for h in range(HEADS)]
        plan += [("v", t, 0, 0) for t in range(TILES + 3)]
        on_act = [e[0] in "kv" for e in plan]
        freed_by = [sum(1 for k in range(n + 1) if on_act[k] == on_act[n]) for n in range(len(plan))]
        squares = [(k, nn) for k, (c, lat) in enumerate(norms) for nn in chunks(lat)]
        block = s.enter_context(nc.Block())

        @block.sync
        def _(sp):
            sp.dma_start(g[:], a["norm_gains"]).then_inc(g_in, 16)
            sp.dma_start(w_uq[:], a["w_uq"].rearrange("(k p) c -> p k c", p=P)).then_inc(w_in, 16)
            sp.dma_start(w_uqs[:], a["w_uq_swapped"].rearrange("(k p) c -> p k c", p=P)).then_inc(w_in, 16)
            sp.dma_start(w_uk[:], a["w_uk"].rearrange("(k p) c -> p k c", p=P)).then_inc(w_in, 16)
            sp.dma_start(w_uv[:], a["w_uv"].rearrange("(k p) c -> p k c", p=P)).then_inc(w_in, 16)
            sp.dma_start(ckvT[:, :, TOKENS:KEYS], a["past_ckvT"].rearrange("(k p) t -> p k t", p=P)).then_inc(past_in, 16)
            sp.wait_ge(normed, len(squares))
            sp.dma_start(a["out_ckvT"].rearrange("(k p) t -> p k t", p=P), ckvT[:, :, 0:TOKENS]).then_inc(out_done, 16)
            sp.wait_ge(out_done, 16)

        @block.gpsimd
        def _(pool):
            for h in range(HEADS):
                pool.tensor_copy(m["mkT"][HD:MD, h, :], m["kpeT"][HD:MD, :]).then_inc(kpe_in, 1)
            pool.wait_ge(kpe_in, HEADS)

        @block.tensor
        def _(pe):
            for k, (c, lat) in enumerate(norms):
                if k >= 2:
                    pe.wait_ge(root_done, k - 1)
                for nn in chunks(lat):
                    at = squares.index((k, nn))
                    pe.wait_ge(sq_done, at + 1)
                    mm = nc.tensor.matmul(ss[k % 2][:, 0:SPAN], m["negones"][:], sq[at % 3][:],
                                          start=(nn == chunks(lat)[0]), stop=(nn == chunks(lat)[-1]))
                    mm.then_inc(ss_done, 1)
            pe.wait_ge(w_in, 64)
            pe.wait_ge(past_in, 16)
            pe.wait_ge(normed, len(squares))
            for n, (kind, j, c, width) in enumerate(plan):
                if n >= NB:
                    k = n - NB
                    pe.wait_ge(copied if on_act[k] else roped, freed_by[k])
                out = ps[n % NB]
                cols = slice(SPAN * c, SPAN * (c + 1))
                if kind in "qs":
                    for k in range(QC):
                        if kind == "q":
                            mm = nc.tensor.matmul(out[0:MD, 0:SPAN], w_uq[:, k, MD * j:MD * (j + 1)], cqT[:, k, cols],
                                                  start=(k == 0), stop=(k == QC - 1))
                        else:
                            mm = nc.tensor.matmul(out[HD:MD, 0:SPAN], w_uqs[:, k, RD * j:RD * (j + 1)], cqT[:, k, cols],
                                                  start=(k == 0), stop=(k == QC - 1))
                else:
                    for k in range(VC):
                        if kind == "k":
                            mm = nc.tensor.matmul(out[0:HD, 0:width], w_uk[:, k, HD * j:HD * (j + 1)], ckvT[:, k, c:c + width],
                                                  start=(k == 0), stop=(k == VC - 1))
                        else:
                            r = NEW if j == TILES else P
                            first = P * j if j <= TILES else TOKENS + P * (j - TILES - 1)
                            mm = nc.tensor.matmul(out[0:r, :], ckvT[:, k, first:first + r], w_uv[:, k, :],
                                                  start=(k == 0), stop=(k == VC - 1))
                mm.then_inc(filled, 1)

        @block.scalar
        def _(act):
            at = 0
            for k, (c, lat) in enumerate(norms):
                for nn in chunks(lat):
                    if at >= 3:
                        act.wait_ge(ss_done, at - 2)
                    nc.scalar.activation(sq[at % 3][:], m["craw"][:, nn, SPAN * c:SPAN * (c + 1)], ACT.Square).then_inc(sq_done, 1)
                    at += 1
                act.wait_ge(ss_done, at)
                if k >= 2:
                    act.wait_ge(inv_done, k - 1)
                nc.scalar.activation(root[k % 2][:], ss[k % 2][:, 0:SPAN], ACT.Sqrt, bias=m["eps"][:],
                                     scale=-1.0 / (QL if lat == 0 else KVL)).then_inc(root_done, 1)
            for n, (kind, j, c, width) in enumerate(plan):
                if not on_act[n]:
                    continue
                act.wait_ge(filled, n + 1)
                if kind == "k":
                    nc.scalar.copy(m["mkT"][0:HD, j, c:c + width], ps[n % NB][0:HD, 0:width]).then_inc(copied, 1)
                else:
                    r = NEW if j == TILES else P
                    nc.scalar.copy(m["mv"][0:r, j, :], ps[n % NB][0:r, :]).then_inc(copied, 1)

        @block.vector
        def _(dve):
            dve.wait_ge(g_in, 16)
            done = 0
            for k, (c, lat) in enumerate(norms):
                cols = slice(SPAN * c, SPAN * (c + 1))
                dve.wait_ge(root_done, k + 1)
                if k >= 2:
                    dve.wait_ge(normed, done)
                nc.vector.reciprocal(inv[k % 2][:], root[k % 2][:]).then_inc(inv_done, 1)
                dve.wait_ge(inv_done, k + 1)
                for nn in chunks(lat):
                    out = cqT[:, nn, cols] if lat == 0 else ckvT[:, nn - QC, cols]
                    nc.vector.scalar_tensor_tensor(out, m["craw"][:, nn, cols], g[:, nn:nn + 1], inv[k % 2][:],
                                                   ALU.mult, ALU.mult).then_inc(normed, 1)
                    done += 1
            pairs = 0
            for n, (kind, h, c, width) in enumerate(plan):
                if kind != "q":
                    continue
                cols = slice(SPAN * c, SPAN * (c + 1))
                dve.wait_ge(filled, n + 2)
                src, swp = ps[n % NB], ps[(n + 1) % NB]
                nc.vector.tensor_tensor(part[0][HD:MD, :], src[HD:MD, 0:SPAN], m["cos"][HD:MD, cols], ALU.mult).then_inc(inv_done, 1)
                nc.vector.tensor_tensor(part[1][HD:MD, :], swp[HD:MD, 0:SPAN], m["sin"][HD:MD, cols], ALU.mult).then_inc(inv_done, 1)
                nc.vector.tensor_copy(m["mqT"][0:HD, h, cols], src[0:HD, 0:SPAN]).then_inc(roped, 1)
                pairs += 1
                dve.wait_ge(inv_done, len(norms) + 2 * pairs)
                nc.vector.tensor_tensor(m["mqT"][HD:MD, h, cols], part[0][HD:MD, :], part[1][HD:MD, :], ALU.add).then_inc(roped, 1)
                dve.wait_ge(roped, 2 * pairs)


def mla_attend(nc, mem, m):
    with ExitStack() as s:
        items = [(i, h) for i in range(TILES + 1) for h in range(HEADS)]
        N = len(items)

        def keys_of(i):
            if i < TILES:
                return 0, P * (i + 1), [(P * j, P, j) for j in range(i + 1)]
            return SEQ, NEW + PAST, [(0, NEW, TILES), (NEW, P, TILES + 1), (NEW + P, P, TILES + 2)]

        p = [mem.at(f"probs{i}", 98304 + 4096 * i, [P, 1024]) for i in range(2)]
        pT = [mem.at(f"probsT{i}", 106496 + 4096 * i, [P, 1024]) for i in range(2)]
        on = [mem.at(f"mla_out{i}", 114688 + 2048 * i, [P, SBW]) for i in range(2)]
        mx = mem.at("row_max", 118784, [P, N])
        nm = mem.at("minus_max", 119168, [P, N])
        rs = mem.at("row_sum", 119552, [P, N])
        ri = mem.at("inverse_sum", 119936, [P, N])
        sp = [s.enter_context(nc.psum_tensor(f"score_ps{i}", [P, 1024], F32)) for i in range(2)]
        tp = s.enter_context(nc.psum_tensor("probsT_ps", [P, 1024], F32))
        op = s.enter_context(nc.psum_tensor("mla_out_ps", [P, 512], F32))
        oT = s.enter_context(nc.psum_tensor("mla_outT_ps", [P, 512], F32))
        s_done, masked, max_done, nm_done, p_done, t_done, t_copied, av_done, inv_done, on_done, oT_done, oT_copied = sems(
            nc, s, "ms_done", "ms_masked", "max_done", "nm_done", "p_done", "t_done", "t_copied", "m_av_done",
            "m_inv", "on_done", "oT_done", "oT_copied")
        block = s.enter_context(nc.Block())

        @block.tensor
        def _(pe):
            for t in range(N + 3):
                if t < N:
                    i, h = items[t]
                    r = rows_of(i)
                    first, nk, _ = keys_of(i)
                    if t >= 2:
                        pe.wait_ge(p_done, t - 1)
                    for c in range(0, nk, 512):
                        w = min(512, nk - c)
                        mm = nc.tensor.matmul(sp[t % 2][0:r, c:c + w], m["mqT"][0:MD, h, P * i:P * i + r],
                                              m["mkT"][0:MD, h, first + c:first + c + w], start=True, stop=True)
                    mm.then_inc(s_done, 1)
                n = t - 1
                if 0 <= n < N:
                    i, h = items[n]
                    r = rows_of(i)
                    pe.wait_ge(p_done, n + 1)
                    if n >= 1:
                        pe.wait_ge(t_copied, n)
                    for x, (off, rows, vt) in enumerate(keys_of(i)[2]):
                        mm = nc.tensor.transpose(tp[0:rows, P * x:P * x + r], p[n % 2][0:r, off:off + rows], m["ident"][0:r, 0:r])
                    mm.then_inc(t_done, 1)
                n = t - 2
                if 0 <= n < N:
                    i, h = items[n]
                    r = rows_of(i)
                    pe.wait_ge(t_copied, n + 1)
                    if h == 0 and i >= 1:
                        pe.wait_ge(on_done, i)
                    tiles = keys_of(i)[2]
                    for x, (off, rows, vt) in enumerate(tiles):
                        mm = nc.tensor.matmul(op[0:r, HD * h:HD * (h + 1)], pT[n % 2][0:rows, P * x:P * x + r],
                                              m["mv"][0:rows, vt, HD * h:HD * (h + 1)], start=(x == 0), stop=(x == len(tiles) - 1),
                                              skip_group_check=True)
                    mm.then_inc(av_done, 1)
                n = t - 3
                if 0 <= n < N and items[n][1] == HEADS - 1:
                    i = items[n][0]
                    r = rows_of(i)
                    pe.wait_ge(on_done, i + 1)
                    if i >= 1:
                        pe.wait_ge(oT_copied, i)
                    for x in range(4):
                        mm = nc.tensor.transpose(oT[:, P * x:P * x + r], on[i % 2][0:r, P * x:P * (x + 1)], m["ident"][0:r, 0:r])
                    mm.then_inc(oT_done, 1)

        @block.scalar
        def _(act):
            for n, (i, h) in enumerate(items):
                r = rows_of(i)
                nk = keys_of(i)[1]
                act.wait_ge(nm_done, n + 1)
                if n >= 2:
                    act.wait_ge(t_done, n - 1)
                nc.scalar.activation(p[n % 2][0:r, 0:nk], sp[n % 2][0:r, 0:nk], ACT.Exp, bias=nm[0:r, n:n + 1],
                                     scale=MLA_SCALE, accum_out=rs[0:r, n:n + 1]).then_inc(p_done, 1)

        @block.vector
        def _(dve):
            for t in range(N + 3):
                if t < N:
                    i, h = items[t]
                    r = rows_of(i)
                    nk = keys_of(i)[1]
                    dve.wait_ge(s_done, t + 1)
                    if i < TILES:
                        nc.vector.memset(sp[t % 2][0:CHUNK, nk - CHUNK:nk], FAR).then_inc(masked, 1)
                        dve.wait_ge(masked, t + 1)
                    nc.vector.reduce_max(mx[0:r, t:t + 1], sp[t % 2][0:r, 0:nk], AX).then_inc(max_done, 1)
                    dve.wait_ge(max_done, t + 1)
                    nc.vector.tensor_scalar(nm[0:r, t:t + 1], mx[0:r, t:t + 1], -MLA_SCALE, None, ALU.mult).then_inc(nm_done, 1)
                n = t - 1
                if 0 <= n < N:
                    i, h = items[n]
                    r = rows_of(i)
                    tiles = keys_of(i)[2]
                    dve.wait_ge(t_done, n + 1)
                    if n >= 2:
                        dve.wait_ge(av_done, n - 1)
                    if i < TILES:
                        nc.vector.tensor_copy(pT[n % 2][:, 0:P * len(tiles)], tp[:, 0:P * len(tiles)]).then_inc(t_copied, 1)
                    else:
                        nc.vector.tensor_copy(pT[n % 2][0:NEW, 0:r], tp[0:NEW, 0:r]).then_inc(masked, 1)
                        for x in (1, 2):
                            ins = nc.vector.tensor_copy(pT[n % 2][:, P * x:P * x + r], tp[:, P * x:P * x + r])
                            ins.then_inc(t_copied if x == 2 else masked, 1)
                n = t - 2
                if 0 <= n < N and items[n][1] == HEADS - 1:
                    i = items[n][0]
                    r = rows_of(i)
                    dve.wait_ge(av_done, n + 1)
                    dve.wait_ge(p_done, n + 1)
                    at = slice(HEADS * i, HEADS * (i + 1))
                    nc.vector.reciprocal(ri[0:r, at], rs[0:r, at]).then_inc(inv_done, 1)
                    dve.wait_ge(inv_done, i + 1)
                    nc.vector.tensor_tensor(on[i % 2][0:r, :].rearrange("p (h d) -> p h d", h=HEADS),
                                            op[0:r, :].rearrange("p (h d) -> p h d", h=HEADS),
                                            ri[0:r, at].unsqueeze(2).broadcast_to([r, HEADS, HD]), ALU.mult).then_inc(on_done, 1)
                n = t - 3
                if 0 <= n < N and items[n][1] == HEADS - 1:
                    i = items[n][0]
                    r = rows_of(i)
                    dve.wait_ge(oT_done, i + 1)
                    nc.vector.tensor_copy(m["obT"][:, :, P * i:P * i + r],
                                          oT[:].rearrange("p (x q) -> p x q", x=4)[:, :, 0:r]).then_inc(oT_copied, 1)


def merge(nc, mem, a, m):
    with ExitStack() as s:
        w_oa = mem.at("w_oa", 0, [P, 4, D])
        w_ob = mem.at("w_ob", 16384, [P, 4, D])
        sig = [mem.at(f"gates{i}", 32768 + 8448 * i, [P, 2, TOKENS]) for i in range(2)]
        part = [mem.at(f"gated{i}", 49664 + 1408 * i, [P, SPAN]) for i in range(4)]
        ps = banks(nc, s, "merge_ps", 8)
        w_in, filled, gated, merged = sems(nc, s, "wo_in", "g_filled", "g_gated", "g_merged")
        sig_in = sems(nc, s, "sig_in_a", "sig_in_b")
        plan = [(j, c) for j in range(KC) for c in range(SPANS)]
        block = s.enter_context(nc.Block())

        @block.sync
        def _(sp):
            sp.dma_start(w_oa[:], a["w_oa"].rearrange("(k p) c -> p k c", p=P)).then_inc(w_in, 16)
            sp.dma_start(w_ob[:], a["w_ob"].rearrange("(k p) c -> p k c", p=P)).then_inc(w_in, 16)
            for j in range(KC):
                if j >= 2:
                    sp.wait_ge(gated, 2 * SPANS * (j - 1))
                sp.dma_start(sig[j % 2][:], a["gatesT"].rearrange("(g k p) t -> k p g t", g=2, p=P)[j]).then_inc(sig_in[j % 2], 16)

        @block.tensor
        def _(pe):
            pe.wait_ge(w_in, 32)
            for n, (j, c) in enumerate(plan):
                if n >= 4:
                    pe.wait_ge(gated, 2 * (n - 3))
                for x, (w, o) in enumerate(((w_oa, m["oaT"]), (w_ob, m["obT"]))):
                    for k in range(4):
                        mm = nc.tensor.matmul(ps[2 * (n % 4) + x][:, 0:SPAN], w[:, k, P * j:P * (j + 1)],
                                              o[:, k, SPAN * c:SPAN * (c + 1)], start=(k == 0), stop=(k == 3))
                mm.then_inc(filled, 1)

        @block.vector
        def _(dve):
            for n, (j, c) in enumerate(plan):
                cols = slice(SPAN * c, SPAN * (c + 1))
                if c == 0:
                    dve.wait_ge(sig_in[j % 2], 16 * (j // 2 + 1))
                dve.wait_ge(filled, n + 1)
                if n >= 2:
                    dve.wait_ge(merged, n - 1)
                for x in range(2):
                    nc.vector.tensor_tensor(part[2 * (n % 2) + x][:], ps[2 * (n % 4) + x][:, 0:SPAN], sig[j % 2][:, x, cols],
                                            ALU.mult).then_inc(gated, 1)
                dve.wait_ge(gated, 2 * (n + 1))
                nc.vector.tensor_tensor(m["mergedT"][:, j, cols], part[2 * (n % 2)][:], part[2 * (n % 2) + 1][:],
                                        ALU.add).then_inc(merged, 1)


def first_norm(nc, mem, a, m):
    with ExitStack() as s:
        w_out = mem.at("w_out", 142336, [P, KC, D])
        g = mem.at("ln1_g", 175104, [P, D])
        b = mem.at("ln1_b", 179200, [P, D])
        x = [mem.at(f"x_rows{i}", 183296 + 4096 * i, [P, D]) for i in range(2)]
        r_ = [mem.at(f"residual{i}", 191488 + 4096 * i, [P, D]) for i in range(2)]
        st = [mem.at(f"stats{i}", 199680 + 64 * i, [P, 16]) for i in range(2)]
        ps = banks(nc, s, "out_ps", 4)
        tp = banks(nc, s, "hT_ps", 4)
        w_in, gb_in, filled, res_done, step, root_done, inv_done, scaled, h_done, turned, t_copied = sems(
            nc, s, "w_out_in", "gb_in", "n_filled", "n_res", "n_step", "n_root", "n_inverse", "n_scaled", "h_done", "h_turned", "hT_copied")
        x_in = sems(nc, s, "xr_in_a", "xr_in_b")
        block = s.enter_context(nc.Block())

        @block.sync
        def _(sp):
            for c in range(2):
                sp.dma_start(w_out[:, :, 512 * c:512 * (c + 1)],
                             a["w_out"].rearrange("(k p) c -> p k c", p=P)[:, :, 512 * c:512 * (c + 1)]).then_inc(w_in, 16)
            sp.dma_start(g[:], a["ln1_g"].partition_broadcast(P)).then_inc(gb_in, 16)
            sp.dma_start(b[:], a["ln1_b"].partition_broadcast(P)).then_inc(gb_in, 16)
            for t in range(TILES + 1):
                r = rows_of(t)
                if t >= 2:
                    sp.wait_ge(res_done, 2 * (t - 1))
                sp.dma_start(x[t % 2][0:r, :], a["x"][P * t:P * t + r, :]).then_inc(x_in[t % 2], 16)

        @block.tensor
        def _(pe):
            pe.wait_ge(w_in, 32)
            for t in range(TILES + 2):
                if t <= TILES:
                    r = rows_of(t)
                    if t >= 2:
                        pe.wait_ge(res_done, 2 * (t - 1))
                    for c in range(2):
                        for k in range(KC):
                            mm = nc.tensor.matmul(ps[2 * (t % 2) + c][0:r, :], m["mergedT"][:, k, P * t:P * t + r],
                                                  w_out[:, k, 512 * c:512 * (c + 1)], start=(k == 0), stop=(k == KC - 1))
                        mm.then_inc(filled, 1)
                n = t - 1
                if n >= 0:
                    r = rows_of(n)
                    pe.wait_ge(h_done, n + 1)
                    if n >= 2:
                        pe.wait_ge(t_copied, 2 * (n - 1))
                    for k in range(KC):
                        mm = nc.tensor.transpose(tp[2 * (n % 2) + k // 4][:, P * (k % 4):P * (k % 4) + r],
                                                 m["h"][0:r, n, P * k:P * (k + 1)], m["ident"][0:r, 0:r])
                        if k % 4 == 3:
                            mm.then_inc(turned, 1)

        @block.scalar
        def _(act):
            for t in range(TILES + 2):
                if t <= TILES:
                    r = rows_of(t)
                    act.wait_ge(step, 3 * t + 3)
                    nc.scalar.activation(st[t % 2][0:r, 14:15], st[t % 2][0:r, 13:14], ACT.Sqrt, bias=m["eps"][0:r, :]).then_inc(root_done, 1)
                n = t - 1
                if n >= 0:
                    r = rows_of(n)
                    for y in range(2):
                        act.wait_ge(turned, 2 * n + y + 1)
                        nc.scalar.copy(m["hT"][:, 4 * y:4 * y + 4, P * n:P * n + r],
                                       tp[2 * (n % 2) + y][:].rearrange("p (x q) -> p x q", x=4)[:, :, 0:r]).then_inc(t_copied, 1)

        @block.vector
        def _(dve):
            dve.wait_ge(gb_in, 32)
            for t in range(TILES + 1):
                r = rows_of(t)
                if t >= 2:
                    dve.wait_ge(h_done, t - 1)
                dve.wait_ge(x_in[t % 2], 16 * (t // 2 + 1))
                s_ = st[t % 2]
                for c in range(2):
                    cols = slice(512 * c, 512 * (c + 1))
                    dve.wait_ge(filled, 2 * t + c + 1)
                    nc.vector.scalar_tensor_tensor(r_[t % 2][0:r, cols], x[t % 2][0:r, cols], ALPHA, ps[2 * (t % 2) + c][0:r, :],
                                                   ALU.mult, ALU.add).then_inc(res_done, 1)
                for c in range(2):
                    dve.wait_ge(res_done, 2 * t + c + 1)
                    nc.vector.bn_stats(s_[0:r, 6 * c:6 * c + 6], r_[t % 2][0:r, 512 * c:512 * (c + 1)]).then_inc(step, 1)
                dve.wait_ge(step, 3 * t + 2)
                nc.vector.bn_aggr(s_[0:r, 12:14], s_[0:r, 0:12]).then_inc(step, 1)
                dve.wait_ge(root_done, t + 1)
                nc.vector.reciprocal(s_[0:r, 15:16], s_[0:r, 14:15]).then_inc(inv_done, 1)
                dve.wait_ge(inv_done, t + 1)
                hrow = m["h"][0:r, t, :]
                nc.vector.tensor_scalar(r_[t % 2][0:r, :], r_[t % 2][0:r, :], s_[0:r, 12:13], s_[0:r, 15:16],
                                        ALU.subtract, ALU.mult).then_inc(scaled, 1)
                dve.wait_ge(scaled, 2 * t + 1)
                nc.vector.tensor_tensor(r_[t % 2][0:r, :], r_[t % 2][0:r, :], g[0:r, :], ALU.mult).then_inc(scaled, 1)
                dve.wait_ge(scaled, 2 * t + 2)
                nc.vector.tensor_tensor(hrow, r_[t % 2][0:r, :], b[0:r, :], ALU.add).then_inc(h_done, 1)
            dve.wait_ge(h_done, TILES + 1)


def experts(nc, mem, a, m):
    with ExitStack() as s:
        T = TILES + 1
        ring = mem.at("expert_rows", 107520, [P, SLOTS, 2 * D])
        wq = mem.at("wq_head", 173056, [P, KC, 2 * PKEYS])
        qT = mem.at("peer_qT", 181248, [P, 2, TOKENS])
        sub = [mem.at(f"sub_keysT{i}", 189696 + 1024 * i, [P, 2, PKEYS]) for i in range(2)]
        junk = [mem.at(f"unused_products{i}", 191744 + 2048 * i, [P, D], BF16) for i in range(2)]
        idx = [mem.at(f"expert_index{i}", 195840 + 576 * i, [P, T, TOPK], U32) for i in range(2)]
        gate = [mem.at(f"expert_gate{i}", 196992 + 576 * i, [P, T, TOPK]) for i in range(2)]
        dots = mem.at("dots", 198144, [P, 8])
        act_ = mem.at("activated", 198208, [P, 8])
        coef = mem.at("coefficients", 198272, [P, 8])
        best = mem.at("best", 198336, [P, 2, TOPK])
        besti = mem.at("best_index", 198464, [P, 2, TOPK], U32)
        bestf = mem.at("best_index_f", 198592, [P, 2, TOPK])
        left = mem.at("scores_left", 198720, [P, 2, PKEYS])
        cand = mem.at("pair_scores", 199744, [P, TOPK * TOPK])
        cand2 = mem.at("pair_scores_left", 200768, [P, TOPK * TOPK])
        pos = mem.at("pair_position", 201792, [P, TOPK], U32)
        ab = mem.at("pair_ranks", 201856, [P, 2, TOPK], U32)
        abf = mem.at("pair_ranks_f", 201984, [P, 2, TOPK])
        iota = mem.at("rank_iota", 202112, [P, TOPK])
        hot = mem.at("one_hot", 202176, [P, 2, TOPK * TOPK])
        pick = mem.at("picked", 204224, [P, 2, TOPK])
        mx = mem.at("gate_max", 204352, [P, T])
        sm = mem.at("gate_sum", 204416, [P, T])
        iv = mem.at("gate_inverse", 204480, [P, T])
        iota_u = mem.at("rank_iota_u", 204544, [P, TOPK], U32)
        qp = banks(nc, s, "peer_q_ps", 4)
        scp = banks(nc, s, "peer_score_ps", 2)
        (cleared, fine, norm, made, acc_set, wq_in, q_filled, q_copied, scored, routed, step, exped, gated, dotted, gelud, weighed, used) = sems(
            nc, s, "gates_cleared", "route_fine_step", "gate_norm_step", "e_made", "acc_set", "wq_in", "q_filled", "q_copied", "scored", "routed", "route_step", "exp_done",
            "gates_ready", "dotted", "gelu_done", "coef_done", "row_used")
        sub_in = sems(nc, s, "sub_in_a", "sub_in_b")
        got = sems(nc, s, *[f"row_in{i}" for i in range(SLOTS)])
        block = s.enter_context(nc.Block())
        ROWS = T * TOPK
        QT = 2 * SPANS
        FINE_T = 24
        FINE = T * FINE_T

        @block.sync
        def _(sp):
            for h in range(HEADS):
                if h >= 1:
                    sp.wait_ge(q_filled, h * QT)
                sp.dma_start(wq[:], a["peer_wq"].rearrange("(k p) c -> p k c", p=P)[:, :, 2 * PKEYS * h:2 * PKEYS * (h + 1)]).then_inc(wq_in, 16)
                if h >= 2:
                    sp.wait_ge(scored, (h - 1) * T)
                sp.dma_start(sub[h % 2][:], a["sub_keysT"].rearrange("(h c p) n -> h p c n", h=HEADS, c=2)[h]).then_inc(sub_in[h % 2], 16)

        @block.gpsimd
        def _(pool):
            pool.iota(iota_u[:], pattern=[[1, TOPK]], base=0, channel_multiplier=0).then_inc(made, 1)
            pool.wait_ge(made, 1)
            pool.tensor_copy(iota[:], iota_u[:]).then_inc(made, 1)

            def gather(h, par):
                for t in range(T):
                    r = rows_of(t)
                    for k in range(TOPK):
                        x = TOPK * t + k
                        if k == 0:
                            pool.wait_ge(routed, h * T + t + 1)
                            pool.nop(nofuse=True)
                        if not (isinstance(h, int) and ROWS * h + x < SLOTS):
                            pool.wait_ge(used, h * ROWS + (x - SLOTS + 1))
                            pool.nop(nofuse=True)
                        slot = x % SLOTS
                        pool.indirect_dma_start(ring[0:r, slot, :], None, a["experts"],
                                                bass.IndirectOffsetOnAxis(ap=idx[par][0:r, t, k:k + 1], axis=0)).then_inc(got[slot], 16)

            for h in range(2):
                gather(h, h)
            with pool.Fori(1, HEADS // 2) as pair:
                for par in range(2):
                    gather(pair * 2 + par, par)

        @block.tensor
        def _(pe):
            def route(h, par):
                pe.wait_ge(wq_in, h * 16 + 16)
                for c in range(2):
                    for y in range(SPANS):
                        n = c * SPANS + y
                        if n >= 4:
                            pe.wait_ge(q_copied, h * QT + (n - 3))
                        for k in range(KC):
                            mm = nc.tensor.matmul(qp[n % 4][:, 0:SPAN], wq[:, k, PKEYS * c:PKEYS * (c + 1)],
                                                  m["hT"][:, k, SPAN * y:SPAN * (y + 1)], start=(k == 0), stop=(k == KC - 1))
                        mm.then_inc(q_filled, 1)
                if isinstance(h, int):
                    pe.wait_ge(sub_in[par], 16 * (h // 2 + 1))
                else:
                    pe.wait_ge(sub_in[par], (h - par) * 8 + 16)
                pe.wait_ge(q_copied, h * QT + QT)
                for t in range(T):
                    r = rows_of(t)
                    if not (isinstance(h, int) and h == 0 and t < 2):
                        pe.wait_ge(routed, h * T + (t - 1))
                    for c in range(2):
                        mm = nc.tensor.matmul(scp[t % 2][0:r, PKEYS * c:PKEYS * (c + 1)], qT[:, c, P * t:P * t + r],
                                              sub[par][:, c, :], start=True, stop=True)
                    mm.then_inc(scored, 1)

            for h in range(2):
                route(h, h)
            with pe.Fori(1, HEADS // 2) as pair:
                for par in range(2):
                    route(pair * 2 + par, par)

        @block.scalar
        def _(act):
            def copy_queries(h, n):
                act.wait_ge(q_filled, h * QT + (n + 1))
                if n == 0 and not (isinstance(h, int) and h == 0):
                    act.wait_ge(scored, h * T)
                nc.scalar.copy(qT[:, n // SPANS, SPAN * (n % SPANS):SPAN * (n % SPANS + 1)],
                               qp[n % 4][:, 0:SPAN]).then_inc(q_copied, 1)

            def exponentials(h, par):
                act.wait_ge(step, h * 2 + 2)
                nc.scalar.activation(gate[par][:], gate[par][:], ACT.Exp).then_inc(exped, 1)

            def weights(h, par, t, also):
                r = rows_of(t)
                for k in range(TOPK):
                    x = TOPK * t + k
                    act.wait_ge(dotted, h * ROWS + (x + 1))
                    if not (isinstance(h, int) and h == 0 and x < 8):
                        act.wait_ge(used, h * ROWS + (x - 7))
                    nc.scalar.activation(act_[0:r, k % 8:k % 8 + 1], dots[0:r, k % 8:k % 8 + 1], ACT.Gelu).then_inc(gelud, 1)
                    act.wait_ge(gelud, h * ROWS + (x + 1))
                    nc.scalar.activation(coef[0:r, k % 8:k % 8 + 1], act_[0:r, k % 8:k % 8 + 1], ACT.Copy,
                                         scale=gate[par][0:r, t, k:k + 1]).then_inc(weighed, 1)
                    if also is not None and k % 2 == 1 and k // 2 < QT:
                        copy_queries(also, k // 2)

            for t in range(T):
                nc.scalar.mul(m["acc"][0:rows_of(t), t, :], m["h"][0:rows_of(t), t, :], ALPHA).then_inc(acc_set, 1)
            for n in range(QT):
                copy_queries(0, n)
            exponentials(0, 0)

            def iteration(h, par):
                act.wait_ge(gated, h)
                for t in range(T - 1):
                    weights(h - 1, 1 - par, t, h if t == 0 else None)
                exponentials(h, par)
                weights(h - 1, 1 - par, T - 1, None)

            iteration(1, 1)
            with act.Fori(1, HEADS // 2) as pair:
                for par in range(2):
                    iteration(pair * 2 + par, par)
            act.wait_ge(gated, HEADS)
            for t in range(T):
                weights(HEADS - 1, 1, t, None)

        @block.vector
        def _(dve):
            dve.wait_ge(made, 2)

            def route(h, par, t, c):
                r = rows_of(t)
                base = h * FINE + t * FINE_T
                at = [0]

                def after(ins):
                    ins.then_inc(c, 1)
                    at[0] += 1

                def sync():
                    dve.wait_ge(c, base + at[0])
                    dve.nop(nofuse=True)

                if not (isinstance(h, int) and h == 0 and t == 0):
                    sync()
                    dve.wait_ge(routed, h * T + t)
                if not (isinstance(h, int) and h < 2):
                    dve.wait_ge(weighed, (h - 1) * ROWS)
                dve.wait_ge(scored, h * T + (t + 1))
                dve.nop(nofuse=True)
                for x in range(2):
                    sc = scp[t % 2][0:r, PKEYS * x:PKEYS * (x + 1)]
                    after(nc.vector.max(best[0:r, x, 0:8], sc))
                sync()
                for x in range(2):
                    sc = scp[t % 2][0:r, PKEYS * x:PKEYS * (x + 1)]
                    after(nc.vector.match_replace(left[0:r, x, :], best[0:r, x, 0:8], sc, LOWEST))
                    after(nc.vector.max_index(besti[0:r, x, 0:8], best[0:r, x, 0:8], sc))
                sync()
                for x in range(2):
                    after(nc.vector.max(best[0:r, x, 8:16], left[0:r, x, :]))
                sync()
                for x in range(2):
                    after(nc.vector.max_index(besti[0:r, x, 8:16], best[0:r, x, 8:16], left[0:r, x, :]))
                pair = cand[0:r, :].rearrange("p (i j) -> p i j", i=TOPK)
                after(nc.vector.tensor_tensor(pair, best[0:r, 0, :].unsqueeze(2).broadcast_to([r, TOPK, TOPK]),
                                              best[0:r, 1, :].unsqueeze(1).broadcast_to([r, TOPK, TOPK]), ALU.add))
                sync()
                g = gate[par][0:r, t, :]
                after(nc.vector.max(g[:, 0:8], cand[0:r, :]))
                after(nc.vector.tensor_copy(bestf[0:r], besti[0:r]))
                sync()
                after(nc.vector.match_replace(cand2[0:r, :], g[:, 0:8], cand[0:r, :], LOWEST))
                after(nc.vector.max_index(pos[0:r, 0:8], g[:, 0:8], cand[0:r, :]))
                sync()
                after(nc.vector.max(g[:, 8:16], cand2[0:r, :]))
                sync()
                after(nc.vector.max_index(pos[0:r, 8:16], g[:, 8:16], cand2[0:r, :]))
                sync()
                after(nc.vector.tensor_scalar(ab[0:r, 0, :], pos[0:r, :], 4, None, ALU.logical_shift_right))
                after(nc.vector.tensor_scalar(ab[0:r, 1, :], pos[0:r, :], 15, None, ALU.bitwise_and))
                sync()
                after(nc.vector.tensor_copy(abf[0:r], ab[0:r]))
                sync()
                oh = hot[0:r].rearrange("p x (k j) -> p (x k) j", j=TOPK)
                after(nc.vector.tensor_tensor(oh, abf[0:r].rearrange("p x k -> p (x k)").unsqueeze(2).broadcast_to([r, 2 * TOPK, TOPK]),
                                              iota[0:r, :].unsqueeze(1).broadcast_to([r, 2 * TOPK, TOPK]), ALU.is_equal))
                sync()
                for x in range(2):
                    o3 = hot[0:r, x, :].rearrange("p (k j) -> p k j", j=TOPK)
                    after(nc.vector.tensor_tensor(o3, o3, bestf[0:r, x, :].unsqueeze(1).broadcast_to([r, TOPK, TOPK]), ALU.mult))
                sync()
                after(nc.vector.tensor_reduce(pick[0:r].rearrange("p x k -> p (x k)"), oh, AX, ALU.add))
                sync()
                nc.vector.scalar_tensor_tensor(idx[par][0:r, t, :], pick[0:r, 0, :], float(PKEYS), pick[0:r, 1, :],
                                               ALU.mult, ALU.add).then_inc(routed, 1)
                assert at[0] == FINE_T, at[0]

            def close(h, par, c):
                dve.wait_ge(routed, h * T + T)
                dve.wait_ge(c, h * FINE + FINE)
                nc.vector.tensor_copy(mx[:, :], gate[par][:, :, 0]).then_inc(step, 1)
                dve.wait_ge(step, h * 2 + 1)
                nc.vector.tensor_tensor(gate[par][:], gate[par][:], mx[:, :].unsqueeze(2).broadcast_to([P, T, TOPK]),
                                        ALU.subtract).then_inc(step, 1)
                dve.wait_ge(exped, h + 1)
                nc.vector.tensor_reduce(sm[:, :], gate[par][:], AX, ALU.add).then_inc(norm, 1)
                dve.wait_ge(norm, h * 2 + 1)
                nc.vector.reciprocal(iv[:, :], sm[:, :]).then_inc(norm, 1)
                dve.wait_ge(norm, h * 2 + 2)
                nc.vector.tensor_tensor(gate[par][:], gate[par][:], iv[:, :].unsqueeze(2).broadcast_to([P, T, TOPK]),
                                        ALU.mult).then_inc(gated, 1)

            def rows(h, par, t):
                r = rows_of(t)
                for k in range(TOPK):
                    x = TOPK * t + k
                    slot = x % SLOTS
                    dve.wait_ge(got[slot], h * (16 * ROWS // SLOTS) + 16 * (x // SLOTS + 1))
                    if not (isinstance(h, int) and h == 0 and x < 2):
                        dve.wait_ge(dotted, h * ROWS + (x - 1))
                    if not (isinstance(h, int) and h == 0 and x < 8):
                        dve.wait_ge(gelud, h * ROWS + (x - 7))
                    nc.vector.scalar_tensor_tensor(junk[k % 2][0:r, :], ring[0:r, slot, 0:D], 1.0, m["h"][0:r, t, :],
                                                   ALU.mult, ALU.mult, accum_out=dots[0:r, k % 8:k % 8 + 1]).then_inc(dotted, 1)
                    if k >= LAG:
                        value(h, t, k - LAG)
                for k in range(TOPK - LAG, TOPK):
                    value(h, t, k)

            def value(h, t, k):
                r = rows_of(t)
                x = TOPK * t + k
                dve.wait_ge(weighed, h * ROWS + (x + 1))
                if not (isinstance(h, int) and h == 0 and x == 0):
                    dve.wait_ge(used, h * ROWS + x)
                nc.vector.scalar_tensor_tensor(m["acc"][0:r, t, :], ring[0:r, x % SLOTS, D:2 * D], coef[0:r, k % 8:k % 8 + 1],
                                               m["acc"][0:r, t, :], ALU.mult, ALU.add).then_inc(used, 1)

            def iteration(h, par):
                for t in range(T):
                    if t < T - 1:
                        rows(h - 1, 1 - par, t)
                    route(h, par, t, fine)
                close(h, par, fine)
                rows(h - 1, 1 - par, T - 1)

            nc.vector.memset(gate[0][:, T - 1, :], 0.0).then_inc(cleared, 1)
            nc.vector.memset(gate[1][:, T - 1, :], 0.0).then_inc(cleared, 1)
            dve.wait_ge(cleared, 2)
            for t in range(T):
                route(0, 0, t, fine)
            close(0, 0, fine)
            dve.wait_ge(acc_set, T)
            iteration(1, 1)
            with dve.Fori(1, HEADS // 2) as pair:
                for par in range(2):
                    iteration(pair * 2 + par, par)
            for t in range(T):
                rows(HEADS - 1, 1, t)
            dve.wait_ge(used, HEADS * ROWS)


def last_norm(nc, mem, a, m):
    with ExitStack() as s:
        T = TILES + 1
        g = mem.at("ln2_g", 107520, [P, D])
        b = mem.at("ln2_b", 111616, [P, D])
        st = mem.at("stats_y", 115712, [P, T, 16])
        gb_in, step, root_done, inv_done, scaled, y_done, out_done = sems(
            nc, s, "ln2_in", "y_step", "y_root", "y_inverse", "y_scaled", "y_done", "y_out")
        block = s.enter_context(nc.Block())

        @block.sync
        def _(sp):
            sp.dma_start(g[:], a["ln2_g"].partition_broadcast(P)).then_inc(gb_in, 16)
            sp.dma_start(b[:], a["ln2_b"].partition_broadcast(P)).then_inc(gb_in, 16)
            for t in range(T):
                r = rows_of(t)
                sp.wait_ge(y_done, t + 1)
                sp.dma_start(a["out_y"][P * t:P * t + r, :], m["acc"][0:r, t, :]).then_inc(out_done, 16)
            sp.wait_ge(out_done, 16 * T)

        @block.scalar
        def _(act):
            for t in range(T):
                r = rows_of(t)
                act.wait_ge(step, 3 * t + 3)
                nc.scalar.activation(st[0:r, t, 14:15], st[0:r, t, 13:14], ACT.Sqrt, bias=m["eps"][0:r, :]).then_inc(root_done, 1)

        @block.vector
        def _(dve):
            for t in range(T):
                r = rows_of(t)
                for c in range(2):
                    nc.vector.bn_stats(st[0:r, t, 6 * c:6 * c + 6], m["acc"][0:r, t, 512 * c:512 * (c + 1)]).then_inc(step, 1)
                dve.wait_ge(step, 3 * t + 2)
                nc.vector.bn_aggr(st[0:r, t, 12:14], st[0:r, t, 0:12]).then_inc(step, 1)
            dve.wait_ge(gb_in, 32)
            for t in range(T):
                r = rows_of(t)
                row = m["acc"][0:r, t, :]
                dve.wait_ge(root_done, t + 1)
                nc.vector.reciprocal(st[0:r, t, 15:16], st[0:r, t, 14:15]).then_inc(inv_done, 1)
                dve.wait_ge(inv_done, t + 1)
                nc.vector.tensor_scalar(row, row, st[0:r, t, 12:13], st[0:r, t, 15:16], ALU.subtract, ALU.mult).then_inc(scaled, 1)
                dve.wait_ge(scaled, 2 * t + 1)
                nc.vector.tensor_tensor(row, row, g[0:r, :], ALU.mult).then_inc(scaled, 1)
                dve.wait_ge(scaled, 2 * t + 2)
                nc.vector.tensor_tensor(row, row, b[0:r, :], ALU.add).then_inc(y_done, 1)


def kernel(x_prompt, x_sample, cache_sb_k, cache_sb_v, cache_mla_ckv, cache_mla_kpe, w_in, q_norm_g, w_uq, kv_norm_g,
           w_uk, w_uv, w_oa, w_ob, w_out, ln1_g, ln1_b, peer_wq, peer_sub_keys, peer_u, peer_v, ln2_g, ln2_b):
    import numpy as np
    import concourse.bacc as bacc
    from concourse.bass_utils import run_bass_kernel_spmd

    half = RD // 2
    swap = np.concatenate([np.arange(half, RD), np.arange(half)])
    x = np.concatenate([np.asarray(x_prompt)[0], np.asarray(x_sample)[0]], axis=0)
    w_in0, w_uq0 = np.asarray(w_in)[0], np.asarray(w_uq)[0]
    c_kr = 3 * SBW + QL + KVL
    positions = np.concatenate([np.arange(SEQ), PAST + np.arange(NEW)]).astype(np.float32)
    rates = (np.float32(10000.0) ** (-np.arange(half, dtype=np.float32) / np.float32(half))).astype(np.float32)
    angles = rates[:, None] * positions[None, :]
    cos, sin = np.cos(angles), np.sin(angles)
    arrays = {
        "x": x,
        "xT": x.T,
        "w_in": w_in0,
        "w_kr_swapped": w_in0[:, c_kr:c_kr + RD][:, swap],
        "past_sb_kT": np.asarray(cache_sb_k)[0, 0].reshape(PAST, SBW).T,
        "past_sb_v": np.asarray(cache_sb_v)[0, 0].reshape(PAST, SBW),
        "past_ckvT": np.asarray(cache_mla_ckv)[0, 0].T,
        "past_kpeT": np.asarray(cache_mla_kpe)[0, 0].T,
        "cosT": np.concatenate([cos, cos], axis=0),
        "sinT": np.concatenate([-sin, sin], axis=0),
        "norm_gains": np.concatenate([np.asarray(q_norm_g)[0], np.asarray(kv_norm_g)[0]]).reshape(QC + VC, P).T,
        "w_uq": w_uq0,
        "w_uq_swapped": w_uq0.reshape(QL, HEADS, MD)[:, :, HD:][:, :, swap].reshape(QL, HEADS * RD),
        "w_uk": np.asarray(w_uk)[0],
        "w_uv": np.asarray(w_uv)[0],
        "w_oa": np.asarray(w_oa)[0],
        "w_ob": np.asarray(w_ob)[0],
        "w_out": np.asarray(w_out)[0],
        "ln1_g": np.asarray(ln1_g)[0],
        "ln1_b": np.asarray(ln1_b)[0],
        "peer_wq": np.asarray(peer_wq)[0],
        "sub_keysT": np.asarray(peer_sub_keys)[0].transpose(0, 1, 3, 2).reshape(HEADS * 2 * PKEYS, PKEYS),
        "experts": np.concatenate([np.asarray(peer_u)[0], np.asarray(peer_v)[0]], axis=1),
        "ln2_g": np.asarray(ln2_g)[0],
        "ln2_b": np.asarray(ln2_b)[0],
    }
    arrays = {k: np.ascontiguousarray(v) for k, v in arrays.items()}
    nc = bacc.Bacc("TRN2", target_bir_lowering=False, num_devices=1)
    a = {k: nc.dram_tensor(f"in_{k}", v.shape, F32, kind="ExternalInput").ap() for k, v in arrays.items()}
    a["gatesT"] = nc.dram_tensor("gatesT", (2 * D, TOKENS), F32).ap()
    outs = {"out_y": (TOKENS, D), "out_kT": (SBW, TOKENS), "out_v": (TOKENS, SBW), "out_ckvT": (KVL, TOKENS), "out_kpeT": (RD, TOKENS)}
    for k, shape in outs.items():
        a[k] = nc.dram_tensor(k, shape, F32, kind="ExternalOutput").ap()
    hybrid_stream_step(nc, a)
    r = run_bass_kernel_spmd(nc, [{f"in_{k}": v for k, v in arrays.items()}], core_ids=[0]).results[0]
    y, v = r["out_y"], r["out_v"]
    k, ckv, kpe = (np.ascontiguousarray(r[n].T) for n in ("out_kT", "out_ckvT", "out_kpeT"))

    def state(z, rows, *tail):
        return z[rows].reshape(1, 1, -1, *tail)

    both = (slice(0, SEQ), slice(SEQ, TOKENS))
    new = [[state(k, w, HEADS, HD), state(v, w, HEADS, HD), state(ckv, w, KVL), state(kpe, w, RD)] for w in both]
    return (y[both[0]].reshape(1, SEQ, D), y[both[1]].reshape(1, NEW, D), *new[0], *new[1])
```

```python
from contextlib import ExitStack

import concourse.bass as bass
from concourse import mybir

F32 = mybir.dt.float32
BF16 = mybir.dt.bfloat16
U32 = mybir.dt.uint32
ALU = mybir.AluOpType
ACT = mybir.ActivationFunctionType
AX = mybir.AxisListType.X

P = 128
D = 1024
KC = D // P
SEQ, NEW, PAST = 1024, 32, 256
TOKENS = SEQ + NEW
KEYS = TOKENS + PAST
TILES = SEQ // P
SPAN = 352
SPANS = TOKENS // SPAN
HEADS, HD = 8, 64
SBW = HEADS * HD
QL, KVL, RD = 384, 256, 32
QC, VC = QL // P, KVL // P
MD = HD + RD
CHUNK = 64
PKEYS, TOPK, EXPERTS = 128, 16, 128 * 128
GATHER, DENSE = 4, 4
SLOTS = 8
LAG = 2
ALPHA = 2.0 ** 0.25
EPS = 1e-5
MLA_SCALE = float(MD) ** -0.5
FAR = -1.0e30
LOWEST = -3.0e38


def rows_of(tile):
    return P if tile < TILES else NEW


class Memory:

    BASE = 16512

    def __init__(self, nc):
        self.nc = nc

    def at(self, name, offset, shape, dtype=F32):
        return self.nc.alloc_sbuf_tensor_at(name, shape, dtype, offset=self.BASE + offset)


def hybrid_stream_step(nc, a):
    mem = Memory(nc)
    m = {}
    m["qT"] = mem.at("sb_qT", 66560, [P, 4, TOKENS])
    m["kT"] = mem.at("sb_kT", 83456, [P, 4, KEYS])
    m["v"] = mem.at("sb_v", 104448, [P, 11, SBW])
    m["oaT"] = mem.at("sb_outT", 142336, [P, 4, TOKENS])
    m["obT"] = mem.at("mla_outT", 159232, [P, 4, TOKENS])
    m["craw"] = mem.at("latents_raw", 176128, [P, QC + VC, TOKENS])
    m["kpeT"] = mem.at("kpeT", 197248, [P, KEYS])
    m["cos"] = mem.at("cosT", 202496, [P, TOKENS])
    m["sin"] = mem.at("sinT", 206720, [P, TOKENS])
    m["ident"] = mem.at("identity", 210944, [P, P])
    m["negtri"] = mem.at("minus_triangle", 211456, [P, P])
    m["negones"] = mem.at("minus_ones", 211968, [P, P])
    m["eps"] = mem.at("epsilon", 212480, [P, 1])
    m["mqT"] = mem.at("mla_qT", 0, [P, HEADS, TOKENS])
    m["mkT"] = mem.at("mla_kT", 33792, [P, HEADS, KEYS])
    m["mv"] = mem.at("mla_v", 75776, [P, 11, SBW])
    m["mergedT"] = mem.at("mergedT", 107520, [P, KC, TOKENS])
    m["hT"] = mem.at("hT", 0, [P, KC, TOKENS])
    m["h"] = mem.at("h", 33792, [P, TILES + 1, D])
    m["hTd"] = mem.at("dense_hT", 50176, [P, KC, P * DENSE])
    m["idx_all"] = mem.at("gathered_index", 203776, [P, HEADS, GATHER + 1, TOPK], U32)
    m["gate_all"] = mem.at("gathered_gate", 206336, [P, HEADS, GATHER + 1, TOPK])
    m["idx_s"] = mem.at("sample_index", 208896, [P, HEADS, 4], U32)
    m["gate_s"] = mem.at("sample_gate", 209024, [P, HEADS, 4])
    m["acc"] = mem.at("ff_sum", 70656, [P, TILES + 1, D])
    project(nc, mem, a, m)
    stick_attend(nc, mem, m)
    mla_project(nc, mem, a, m)
    mla_attend(nc, mem, m)
    merge(nc, mem, a, m)
    first_norm(nc, mem, a, m)
    route_experts(nc, mem, a, m)
    apply_experts(nc, mem, a, m)
    last_norm(nc, mem, a, m)


def sems(nc, stack, *names):
    return [stack.enter_context(nc.semaphore(n)) for n in names]


def banks(nc, stack, name, n):
    return [stack.enter_context(nc.psum_tensor(f"{name}{i}", [P, 512], F32)) for i in range(n)]


def project(nc, mem, a, m):
    with ExitStack() as s:
        xT = mem.at("xT", 0, [P, KC, TOKENS])
        w = [mem.at(f"w_in_block{i}", 33792 + 16384 * i, [P, KC, 512]) for i in range(2)]
        gate = [mem.at(f"gate_stage{i}", 126976 + 1408 * i, [P, SPAN]) for i in range(4)]
        turned = [mem.at(f"rope_part{i}", 132608 + 1408 * i, [P, SPAN]) for i in range(2)]
        zero = mem.at("zeros", 135424, [P, 1024])
        NB = 8
        ps = banks(nc, s, "proj_ps", NB)
        c0 = 3 * SBW
        blocks = [(0, SBW, "q"), (SBW, SBW, "k"), (2 * SBW, SBW, "v"), (c0, QL, "c"),
                  (c0 + QL, KVL + RD, "ckr"), *[(c0 + QL + KVL + RD + 512 * i, 512, "g") for i in range(4)]]
        plan = []
        for b, (_, width, kind) in enumerate(blocks):
            if kind == "v":
                plan += [(b, "v", 0, t, 0) for t in range(TILES + 1)]
                continue
            for j in range(width // P):
                plan += [(b, kind[0], P * j, {"c": j + QC * (kind == "ckr")}.get(kind[0], j), c) for c in range(SPANS)]
            if kind == "ckr":
                plan += [(b, r, KVL + (0 if r == "r" else RD), 0, c) for c in range(SPANS) for r in "rs"]
        on_act = [kind == "g" for _, kind, *_ in plan]
        freed_by = [sum(1 for k in range(n + 1) if on_act[k] == on_act[n]) for n in range(len(plan))]

        x_in, fixed_in, filled, copied, squashed, sine_done, out_done, made, zeroed, zero_done = sems(
            nc, s, "x_in", "fixed_in", "p_filled", "p_copied", "p_squashed", "sine_part_done", "p_out", "const_made", "zeros_set", "dense_gates_zeroed")
        w_in = sems(nc, s, "w_in_a", "w_in_b")
        gate_out = sems(nc, s, *[f"gate_out{i}" for i in range(4)])
        last_of = {b: max(n for n, e in enumerate(plan) if e[0] == b) for b in range(len(blocks))}
        block = s.enter_context(nc.Block())

        @block.sync
        def _(sp):
            for b, (col, width, kind) in enumerate(blocks):
                if b >= 2:
                    sp.wait_ge(filled, last_of[b - 2] + 1)
                sp.dma_start(w[b % 2][:, :, 0:width],
                             a["w_in"].rearrange("(k p) c -> p k c", p=P)[:, :, col:col + width]).then_inc(w_in[b % 2], 16)
                if kind == "ckr":
                    sp.dma_start(w[b % 2][:, :, width:width + RD],
                                 a["w_kr_swapped"].rearrange("(k p) c -> p k c", p=P)).then_inc(w_in[b % 2], 16)
                if b == 0:
                    for c in range(SPANS):
                        sp.dma_start(xT[:, :, SPAN * c:SPAN * (c + 1)],
                                     a["xT"].rearrange("(k p) t -> p k t", p=P)[:, :, SPAN * c:SPAN * (c + 1)]).then_inc(x_in, 16)
                if b == 1:
                    sp.dma_start(m["kT"][:, :, TOKENS:KEYS],
                                 a["past_sb_kT"].rearrange("(k p) t -> p k t", p=P)).then_inc(fixed_in, 16)
                    sp.dma_start(m["v"][:, TILES + 1:TILES + 3, :],
                                 a["past_sb_v"].rearrange("(k p) c -> p k c", p=P)).then_inc(fixed_in, 16)
                    sp.dma_start(m["kpeT"][HD:MD, TOKENS:KEYS], a["past_kpeT"]).then_inc(fixed_in, 16)
                    sp.dma_start(m["cos"][HD:MD, :], a["cosT"]).then_inc(fixed_in, 16)
                    sp.dma_start(m["sin"][HD:MD, :], a["sinT"]).then_inc(fixed_in, 16)
            sp.wait_ge(zeroed, 1)
            cells = a["gates_by_expert"].rearrange("(n p r c) o -> n p r (c o)", p=P, r=8, c=1024)
            for n in range(EXPERTS * DENSE // 8192):
                sp.dma_start(cells[n], zero[:].unsqueeze(1).broadcast_to([P, 8, 1024])).then_inc(zero_done, 16)
            copies = lambda b: sum(1 for n in range(last_of[b] + 1) if not on_act[n])
            sp.wait_ge(copied, copies(1))
            sp.dma_start(a["out_kT"].rearrange("(k p) t -> p k t", p=P), m["kT"][:, :, 0:TOKENS]).then_inc(out_done, 16)
            sp.wait_ge(copied, copies(2))
            sp.dma_start(a["out_v"][0:SEQ, :].rearrange("(k p) c -> p k c", p=P), m["v"][:, 0:TILES, :]).then_inc(out_done, 16)
            sp.dma_start(a["out_v"][SEQ:TOKENS, :], m["v"][0:NEW, TILES, :]).then_inc(out_done, 16)
            sp.wait_ge(copied, sum(1 for x in on_act if not x))
            sp.dma_start(a["out_kpeT"], m["kpeT"][HD:MD, 0:TOKENS]).then_inc(out_done, 16)
            for i in range(4):
                sp.wait_ge(gate_out[i], 4 * sum(on_act))
            sp.wait_ge(out_done, 64)
            sp.wait_ge(zero_done, 2 * EXPERTS * DENSE // 1024)
            sp.wait_ge(fixed_in, 80)

        @block.gpsimd
        def _(pool):
            pool.memset(zero[:], 0.0).then_inc(zeroed, 1)
            pool.memset(m["ident"][:], 0.0).then_inc(made, 1)
            pool.memset(m["negtri"][:], -1.0).then_inc(made, 1)
            pool.memset(m["negones"][:], -1.0).then_inc(made, 1)
            pool.memset(m["eps"][:], EPS).then_inc(made, 1)
            pool.wait_ge(made, 4)
            pool.affine_select(out=m["ident"][:], in_=m["ident"][:], compare_op=ALU.not_equal, fill=1.0, base=0,
                               pattern=[[-1, P]], channel_multiplier=1).then_inc(made, 1)
            pool.affine_select(out=m["negtri"][:], in_=m["negtri"][:], compare_op=ALU.is_ge, fill=0.0, base=0,
                               pattern=[[-1, P]], channel_multiplier=1).then_inc(made, 1)
            pool.wait_ge(made, 6)

        @block.tensor
        def _(pe):
            pe.wait_ge(x_in, 16 * SPANS)
            seen = -1
            for n, (b, kind, col, j, c) in enumerate(plan):
                if b != seen:
                    seen = b
                    pe.wait_ge(w_in[b % 2], 16 * (b // 2 + 1 + (b % 2 == 0 and b >= 4)))
                if n >= NB:
                    k = n - NB
                    pe.wait_ge(squashed if on_act[k] else copied, freed_by[k])
                out = ps[n % NB]
                for k in range(KC):
                    if kind == "v":
                        r = rows_of(j)
                        mm = nc.tensor.matmul(out[0:r, :], xT[:, k, P * j:P * j + r], w[b % 2][:, k, :],
                                              start=(k == 0), stop=(k == KC - 1))
                    elif kind in "rs":
                        mm = nc.tensor.matmul(out[HD:MD, 0:SPAN], w[b % 2][:, k, col:col + RD],
                                              xT[:, k, SPAN * c:SPAN * (c + 1)], start=(k == 0), stop=(k == KC - 1))
                    else:
                        mm = nc.tensor.matmul(out[:, 0:SPAN], w[b % 2][:, k, col:col + P],
                                              xT[:, k, SPAN * c:SPAN * (c + 1)], start=(k == 0), stop=(k == KC - 1))
                mm.then_inc(filled, 1)

        @block.vector
        def _(dve):
            dve.wait_ge(fixed_in, 80)
            done = 0
            for n, (b, kind, col, j, c) in enumerate(plan):
                if kind == "g":
                    continue
                dve.wait_ge(filled, n + 1)
                cols = slice(SPAN * c, SPAN * (c + 1))
                src = ps[n % NB]
                if kind == "q":
                    nc.vector.tensor_scalar(m["qT"][:, j, cols], src[:, 0:SPAN], float(HD) ** -0.5, None, ALU.mult).then_inc(copied, 1)
                elif kind == "k":
                    nc.vector.tensor_copy(m["kT"][:, j, cols], src[:, 0:SPAN]).then_inc(copied, 1)
                elif kind == "v":
                    r = rows_of(j)
                    nc.vector.tensor_copy(m["v"][0:r, j, :], src[0:r, :]).then_inc(copied, 1)
                elif kind == "c":
                    nc.vector.tensor_copy(m["craw"][:, j, cols], src[:, 0:SPAN]).then_inc(copied, 1)
                elif kind == "r":
                    if done >= 2:
                        dve.wait_ge(copied, done)
                    nc.vector.tensor_tensor(turned[0][HD:MD, :], src[HD:MD, 0:SPAN], m["cos"][HD:MD, cols], ALU.mult).then_inc(copied, 1)
                else:
                    dve.wait_ge(copied, done)
                    nc.vector.tensor_tensor(turned[1][HD:MD, :], src[HD:MD, 0:SPAN], m["sin"][HD:MD, cols], ALU.mult).then_inc(sine_done, 1)
                    dve.wait_ge(sine_done, c + 1)
                    nc.vector.tensor_tensor(m["kpeT"][HD:MD, cols], turned[0][HD:MD, :], turned[1][HD:MD, :], ALU.add).then_inc(copied, 1)
                done += 1

        @block.scalar
        def _(act):
            n = 0
            for e, (b, kind, col, j, c) in enumerate(plan):
                if kind != "g":
                    continue
                act.wait_ge(filled, e + 1)
                if n >= 4:
                    act.wait_ge(gate_out[n % 4], 16 * (n // 4))
                nc.scalar.activation(gate[n % 4][:], ps[e % NB][:, 0:SPAN], ACT.Sigmoid).then_inc(squashed, 1)
                act.wait_ge(squashed, n + 1)
                row = 512 * (b - 5) + P * j
                act.dma_start(a["gatesT"][row:row + P, SPAN * c:SPAN * (c + 1)], gate[n % 4][:]).then_inc(gate_out[n % 4], 16)
                n += 1


def stick_attend(nc, mem, m):
    with ExitStack() as s:
        items = []
        for i in range(TILES + 1):
            nq = rows_of(i)
            tiles = [(P * j, P, j, j == i) for j in range(i, -1, -1)] if i < TILES else \
                    [(SEQ, NEW, TILES, True), (TOKENS + P, P, TILES + 2, False), (TOKENS, P, TILES + 1, False)]
            for x, (key, rows, vt, diag) in enumerate(tiles):
                for par in range(2):
                    items.append((i, nq, key, rows, vt, diag, par, x == len(tiles) - 1))
        N = len(items)
        E, S, R, A = 3, 4, 6, 3
        e = [mem.at(f"abs_exp_ln{i}", 2048 * i, [P, 512]) for i in range(E)]
        sp_ = [mem.at(f"softplus{i}", 2048 * (E + i), [P, 512]) for i in range(S)]
        rest = [mem.at(f"later_sum{i}", 2048 * (E + S + i), [P, 512]) for i in range(R)]
        w = [mem.at(f"weights{i}", 2048 * (E + S + R + i), [P, 512]) for i in range(A)]
        before = mem.at("earlier_mask", 40960, [P, P])
        far = mem.at("far_mask", 41472, [P, P])
        zb = banks(nc, s, "z_ps", 3)
        sb = banks(nc, s, "log_weight_ps", 2)
        ob = banks(nc, s, "stick_out_ps", 2)
        masks, z_done, chain, ln_done, sp_done, sp_masked, rest_done, zeroed, s_done, w_done, av_done, o_done, o_copied = sems(
            nc, s, "masks", "z_done", "act_step", "ln_done", "sp_done", "sp_masked", "rest_done", "rest_zeroed",
            "log_weight_done", "weight_done", "av_done", "stick_o_done", "stick_o_copied")
        block = s.enter_context(nc.Block())
        diag_upto = lambda n: sum(1 for k in range(n + 1) if items[k][5])
        rest_upto = lambda n: sum(1 for k in range(n + 1) if not items[k][7])

        def scores(bank, n, more):
            i, nq, key, rows, vt, diag, par, last = items[n]
            for x in range(4):
                mm = nc.tensor.matmul(bank[0:rows, nq * x:nq * (x + 1)], m["kT"][HD * par:HD * par + HD, x, key:key + rows],
                                      m["qT"][HD * par:HD * par + HD, x, P * i:P * i + nq], start=(x == 0),
                                      stop=(x == 3 and not more), skip_group_check=True)
            return mm

        @block.gpsimd
        def _(pool):
            pool.memset(before[:], 1.0).then_inc(masks, 1)
            pool.memset(far[:], 0.0).then_inc(masks, 1)
            pool.wait_ge(masks, 2)
            pool.affine_select(out=before[:], in_=before[:], compare_op=ALU.is_gt, fill=0.0, base=0,
                               pattern=[[1, P]], channel_multiplier=-1).then_inc(masks, 1)
            pool.affine_select(out=far[:], in_=far[:], compare_op=ALU.is_gt, fill=FAR, base=0,
                               pattern=[[1, P]], channel_multiplier=-1).then_inc(masks, 1)

        @block.tensor
        def _(pe):
            pe.wait_ge(masks, 4)
            for t in range(N + 4):
                if t < N:
                    if t >= 3:
                        pe.wait_ge(sp_done, t - 2)
                    scores(zb[t % 3], t, False).then_inc(z_done, 1)
                n = t - 2
                if 0 <= n < N:
                    i, nq, key, rows, vt, diag, par, last = items[n]
                    cols = slice(0, 4 * nq)
                    if n >= 2:
                        pe.wait_ge(w_done, n - 1)
                    scores(sb[n % 2], n, True)
                    if diag:
                        for x in range(4):
                            nc.tensor.matmul(sb[n % 2][0:rows, nq * x:nq * (x + 1)], m["ident"][0:rows, 0:rows], far[0:rows, 0:nq],
                                             start=False, stop=False, skip_group_check=True)
                        pe.wait_ge(sp_masked, diag_upto(n))
                    else:
                        kr = items[n - 2][3]
                        pe.wait_ge(rest_done, rest_upto(n - 2))
                        nc.tensor.matmul(sb[n % 2][0:rows, cols], m["negones"][0:P, 0:rows], rest[(n - 2) % R][:, cols],
                                         start=False, stop=False, skip_group_check=True)
                        pe.wait_ge(sp_done, n + 1)
                    nc.tensor.matmul(sb[n % 2][0:rows, cols], m["negtri"][0:rows, 0:rows], sp_[n % S][0:rows, cols],
                                     start=False, stop=True, skip_group_check=True).then_inc(s_done, 1)
                n = t - 4
                if 0 <= n < N:
                    i, nq, key, rows, vt, diag, par, last = items[n]
                    pe.wait_ge(w_done, n + 1)
                    if diag and i >= 1:
                        pe.wait_ge(o_copied, 2 * (i - 1) + par + 1)
                    for x in range(4):
                        h = 2 * x + par
                        mm = nc.tensor.matmul(ob[par][HD * par:HD * par + HD, nq * x:nq * (x + 1)], m["v"][0:rows, vt, HD * h:HD * (h + 1)],
                                              w[n % A][0:rows, nq * x:nq * (x + 1)], start=(diag and x == 0), stop=last,
                                              skip_group_check=True)
                    mm.then_inc(av_done, 1)

        @block.scalar
        def _(act):
            steps = 0
            for t in range(N + 2):
                if t < N:
                    i, nq, key, rows, vt, diag, par, last = items[t]
                    buf, src = e[t % E][0:rows, 0:4 * nq], zb[t % 3][0:rows, 0:4 * nq]
                    act.wait_ge(z_done, t + 1)
                    if t >= E:
                        act.wait_ge(sp_done, t - E + 1)
                    nc.scalar.activation(buf, src, ACT.Abs).then_inc(chain, 1)
                    act.wait_ge(chain, steps + 1)
                    nc.scalar.activation(buf, buf, ACT.Exp, scale=-1.0).then_inc(chain, 1)
                    act.wait_ge(chain, steps + 2)
                    nc.scalar.activation(buf, buf, ACT.Ln, bias=1.0).then_inc(ln_done, 1)
                    steps += 2
                n = t - 2
                if 0 <= n < N:
                    i, nq, key, rows, vt, diag, par, last = items[n]
                    act.wait_ge(s_done, n + 1)
                    if n >= A:
                        act.wait_ge(av_done, n - A + 1)
                    nc.scalar.activation(w[n % A][0:rows, 0:4 * nq], sb[n % 2][0:rows, 0:4 * nq], ACT.Exp).then_inc(w_done, 1)

        @block.vector
        def _(dve):
            dve.wait_ge(masks, 4)
            ends = [n for n in range(N) if items[n][7]]
            zeros = 0
            for t in range(N + 5):
                if t < N:
                    i, nq, key, rows, vt, diag, par, last = items[t]
                    cols = slice(0, 4 * nq)
                    dve.wait_ge(ln_done, t + 1)
                    if t >= S:
                        dve.wait_ge(s_done, t - S + 1)
                    own = sp_[t % S][0:rows, cols]
                    nc.vector.scalar_tensor_tensor(own, zb[t % 3][0:rows, cols], 0.0, e[t % E][0:rows, cols],
                                                   ALU.max, ALU.add).then_inc(sp_done, 1)
                    dve.wait_ge(sp_done, t + 1)
                    if diag:
                        v3 = own.rearrange("p (x q) -> p x q", x=4)
                        nc.vector.tensor_tensor(v3, v3, before[0:rows, 0:nq].unsqueeze(1).broadcast_to([rows, 4, nq]), ALU.mult).then_inc(sp_masked, 1)
                        dve.wait_ge(sp_masked, diag_upto(t))
                    if not last:
                        out = rest[t % R]
                        if rows < P:
                            nc.vector.memset(out[:, cols], 0.0).then_inc(zeroed, 1)
                            zeros += 1
                            dve.wait_ge(zeroed, zeros)
                        if diag:
                            nc.vector.tensor_copy(out[0:rows, cols], own).then_inc(rest_done, 1)
                        else:
                            dve.wait_ge(rest_done, rest_upto(t - 2))
                            nc.vector.tensor_tensor(out[:, cols], own, rest[(t - 2) % R][:, cols], ALU.add).then_inc(rest_done, 1)
                n = t - 5
                if n in ends:
                    i, nq, key, rows, vt, diag, par, last = items[n]
                    dve.wait_ge(av_done, n + 1)
                    nc.vector.tensor_copy(m["oaT"][HD * par:HD * par + HD, :, P * i:P * i + nq],
                                          ob[par][HD * par:HD * par + HD, 0:4 * nq].rearrange("p (x q) -> p x q", x=4)).then_inc(o_copied, 1)


def mla_project(nc, mem, a, m):
    with ExitStack() as s:
        cqT = mem.at("query_latentT", 98304, [P, QC, TOKENS])
        ckvT = mem.at("kv_latentT", 110976, [P, VC, KEYS])
        w_uq = mem.at("w_uq", 121472, [P, QC, HEADS * MD])
        w_uqs = mem.at("w_uq_swapped", 130688, [P, QC, HEADS * RD])
        w_uk = mem.at("w_uk", 133760, [P, VC, SBW])
        w_uv = mem.at("w_uv", 137856, [P, VC, SBW])
        g = mem.at("norm_gains", 141952, [P, QC + VC])
        sq = [mem.at(f"squares{i}", 159232 + 1408 * i, [P, SPAN]) for i in range(3)]
        root = [mem.at(f"roots{i}", 163456 + 1408 * i, [P, SPAN]) for i in range(2)]
        inv = [mem.at(f"inverse_roots{i}", 166272 + 1408 * i, [P, SPAN]) for i in range(2)]
        part = [mem.at(f"rope_q{i}", 169088 + 1408 * i, [P, SPAN]) for i in range(2)]
        ss = banks(nc, s, "square_sum_ps", 2)
        NB = 6
        ps = banks(nc, s, "mla_ps", NB)
        w_in, past_in, g_in, sq_done, ss_done, root_done, inv_done, normed, filled, copied, roped, kpe_in, out_done = sems(
            nc, s, "uw_in", "past_in", "gain_in", "sq_done", "ss_done", "root_done", "inv_done", "normed",
            "m_filled", "m_copied", "m_roped", "m_kpe", "m_out")
        norms = [(c, lat) for c in range(SPANS) for lat in range(2)]
        chunks = lambda lat: range(QC) if lat == 0 else range(QC, QC + VC)
        plan = []
        for c in range(SPANS):
            for h in range(HEADS):
                plan += [("q", h, c, 0), ("s", h, c, 0)]
        key_spans = [(c * SPAN, SPAN) for c in range(SPANS)] + [(TOKENS, PAST)]
        for c, width in key_spans:
            plan += [("k", h, c, width) for h in range(HEADS)]
        plan += [("v", t, 0, 0) for t in range(TILES + 3)]
        on_act = [e[0] in "kv" for e in plan]
        freed_by = [sum(1 for k in range(n + 1) if on_act[k] == on_act[n]) for n in range(len(plan))]
        squares = [(k, nn) for k, (c, lat) in enumerate(norms) for nn in chunks(lat)]
        block = s.enter_context(nc.Block())

        @block.sync
        def _(sp):
            sp.dma_start(g[:], a["norm_gains"]).then_inc(g_in, 16)
            sp.dma_start(w_uq[:], a["w_uq"].rearrange("(k p) c -> p k c", p=P)).then_inc(w_in, 16)
            sp.dma_start(w_uqs[:], a["w_uq_swapped"].rearrange("(k p) c -> p k c", p=P)).then_inc(w_in, 16)
            sp.dma_start(w_uk[:], a["w_uk"].rearrange("(k p) c -> p k c", p=P)).then_inc(w_in, 16)
            sp.dma_start(w_uv[:], a["w_uv"].rearrange("(k p) c -> p k c", p=P)).then_inc(w_in, 16)
            sp.dma_start(ckvT[:, :, TOKENS:KEYS], a["past_ckvT"].rearrange("(k p) t -> p k t", p=P)).then_inc(past_in, 16)
            sp.wait_ge(normed, len(squares))
            sp.dma_start(a["out_ckvT"].rearrange("(k p) t -> p k t", p=P), ckvT[:, :, 0:TOKENS]).then_inc(out_done, 16)
            sp.wait_ge(out_done, 16)

        @block.gpsimd
        def _(pool):
            for h in range(HEADS):
                pool.tensor_copy(m["mkT"][HD:MD, h, :], m["kpeT"][HD:MD, :]).then_inc(kpe_in, 1)
            pool.wait_ge(kpe_in, HEADS)

        @block.tensor
        def _(pe):
            for k, (c, lat) in enumerate(norms):
                if k >= 2:
                    pe.wait_ge(root_done, k - 1)
                for nn in chunks(lat):
                    at = squares.index((k, nn))
                    pe.wait_ge(sq_done, at + 1)
                    mm = nc.tensor.matmul(ss[k % 2][:, 0:SPAN], m["negones"][:], sq[at % 3][:],
                                          start=(nn == chunks(lat)[0]), stop=(nn == chunks(lat)[-1]))
                    mm.then_inc(ss_done, 1)
            pe.wait_ge(w_in, 64)
            pe.wait_ge(past_in, 16)
            pe.wait_ge(normed, len(squares))
            for n, (kind, j, c, width) in enumerate(plan):
                if n >= NB:
                    k = n - NB
                    pe.wait_ge(copied if on_act[k] else roped, freed_by[k])
                out = ps[n % NB]
                cols = slice(SPAN * c, SPAN * (c + 1))
                if kind in "qs":
                    for k in range(QC):
                        if kind == "q":
                            mm = nc.tensor.matmul(out[0:MD, 0:SPAN], w_uq[:, k, MD * j:MD * (j + 1)], cqT[:, k, cols],
                                                  start=(k == 0), stop=(k == QC - 1))
                        else:
                            mm = nc.tensor.matmul(out[HD:MD, 0:SPAN], w_uqs[:, k, RD * j:RD * (j + 1)], cqT[:, k, cols],
                                                  start=(k == 0), stop=(k == QC - 1))
                else:
                    for k in range(VC):
                        if kind == "k":
                            mm = nc.tensor.matmul(out[0:HD, 0:width], w_uk[:, k, HD * j:HD * (j + 1)], ckvT[:, k, c:c + width],
                                                  start=(k == 0), stop=(k == VC - 1))
                        else:
                            r = NEW if j == TILES else P
                            first = P * j if j <= TILES else TOKENS + P * (j - TILES - 1)
                            mm = nc.tensor.matmul(out[0:r, :], ckvT[:, k, first:first + r], w_uv[:, k, :],
                                                  start=(k == 0), stop=(k == VC - 1))
                mm.then_inc(filled, 1)

        @block.scalar
        def _(act):
            at = 0
            for k, (c, lat) in enumerate(norms):
                for nn in chunks(lat):
                    if at >= 3:
                        act.wait_ge(ss_done, at - 2)
                    nc.scalar.activation(sq[at % 3][:], m["craw"][:, nn, SPAN * c:SPAN * (c + 1)], ACT.Square).then_inc(sq_done, 1)
                    at += 1
                act.wait_ge(ss_done, at)
                if k >= 2:
                    act.wait_ge(inv_done, k - 1)
                nc.scalar.activation(root[k % 2][:], ss[k % 2][:, 0:SPAN], ACT.Sqrt, bias=m["eps"][:],
                                     scale=-1.0 / (QL if lat == 0 else KVL)).then_inc(root_done, 1)
            for n, (kind, j, c, width) in enumerate(plan):
                if not on_act[n]:
                    continue
                act.wait_ge(filled, n + 1)
                if kind == "k":
                    nc.scalar.copy(m["mkT"][0:HD, j, c:c + width], ps[n % NB][0:HD, 0:width]).then_inc(copied, 1)
                else:
                    r = NEW if j == TILES else P
                    nc.scalar.copy(m["mv"][0:r, j, :], ps[n % NB][0:r, :]).then_inc(copied, 1)

        @block.vector
        def _(dve):
            dve.wait_ge(g_in, 16)
            done = 0
            for k, (c, lat) in enumerate(norms):
                cols = slice(SPAN * c, SPAN * (c + 1))
                dve.wait_ge(root_done, k + 1)
                if k >= 2:
                    dve.wait_ge(normed, done)
                nc.vector.reciprocal(inv[k % 2][:], root[k % 2][:]).then_inc(inv_done, 1)
                dve.wait_ge(inv_done, k + 1)
                for nn in chunks(lat):
                    out = cqT[:, nn, cols] if lat == 0 else ckvT[:, nn - QC, cols]
                    nc.vector.scalar_tensor_tensor(out, m["craw"][:, nn, cols], g[:, nn:nn + 1], inv[k % 2][:],
                                                   ALU.mult, ALU.mult).then_inc(normed, 1)
                    done += 1
            pairs = 0
            for n, (kind, h, c, width) in enumerate(plan):
                if kind != "q":
                    continue
                cols = slice(SPAN * c, SPAN * (c + 1))
                dve.wait_ge(filled, n + 2)
                src, swp = ps[n % NB], ps[(n + 1) % NB]
                nc.vector.tensor_tensor(part[0][HD:MD, :], src[HD:MD, 0:SPAN], m["cos"][HD:MD, cols], ALU.mult).then_inc(inv_done, 1)
                nc.vector.tensor_tensor(part[1][HD:MD, :], swp[HD:MD, 0:SPAN], m["sin"][HD:MD, cols], ALU.mult).then_inc(inv_done, 1)
                nc.vector.tensor_copy(m["mqT"][0:HD, h, cols], src[0:HD, 0:SPAN]).then_inc(roped, 1)
                pairs += 1
                dve.wait_ge(inv_done, len(norms) + 2 * pairs)
                nc.vector.tensor_tensor(m["mqT"][HD:MD, h, cols], part[0][HD:MD, :], part[1][HD:MD, :], ALU.add).then_inc(roped, 1)
                dve.wait_ge(roped, 2 * pairs)


def mla_attend(nc, mem, m):
    with ExitStack() as s:
        items = [(i, h) for i in range(TILES + 1) for h in range(HEADS)]
        N = len(items)

        def keys_of(i):
            if i < TILES:
                return 0, P * (i + 1), [(P * j, P, j) for j in range(i + 1)]
            return SEQ, NEW + PAST, [(0, NEW, TILES), (NEW, P, TILES + 1), (NEW + P, P, TILES + 2)]

        p = [mem.at(f"probs{i}", 98304 + 4096 * i, [P, 1024]) for i in range(2)]
        pT = [mem.at(f"probsT{i}", 106496 + 4096 * i, [P, 1024]) for i in range(2)]
        on = [mem.at(f"mla_out{i}", 114688 + 2048 * i, [P, SBW]) for i in range(2)]
        mx = mem.at("row_max", 118784, [P, N])
        nm = mem.at("minus_max", 119168, [P, N])
        rs = mem.at("row_sum", 119552, [P, N])
        ri = mem.at("inverse_sum", 119936, [P, N])
        sp = [s.enter_context(nc.psum_tensor(f"score_ps{i}", [P, 1024], F32)) for i in range(2)]
        tp = s.enter_context(nc.psum_tensor("probsT_ps", [P, 1024], F32))
        op = s.enter_context(nc.psum_tensor("mla_out_ps", [P, 512], F32))
        oT = s.enter_context(nc.psum_tensor("mla_outT_ps", [P, 512], F32))
        s_done, masked, max_done, nm_done, p_done, t_done, t_copied, av_done, inv_done, on_done, oT_done, oT_copied = sems(
            nc, s, "ms_done", "ms_masked", "max_done", "nm_done", "p_done", "t_done", "t_copied", "m_av_done",
            "m_inv", "on_done", "oT_done", "oT_copied")
        block = s.enter_context(nc.Block())

        @block.tensor
        def _(pe):
            for t in range(N + 3):
                if t < N:
                    i, h = items[t]
                    r = rows_of(i)
                    first, nk, _ = keys_of(i)
                    if t >= 2:
                        pe.wait_ge(p_done, t - 1)
                    for c in range(0, nk, 512):
                        w = min(512, nk - c)
                        mm = nc.tensor.matmul(sp[t % 2][0:r, c:c + w], m["mqT"][0:MD, h, P * i:P * i + r],
                                              m["mkT"][0:MD, h, first + c:first + c + w], start=True, stop=True)
                    mm.then_inc(s_done, 1)
                n = t - 1
                if 0 <= n < N:
                    i, h = items[n]
                    r = rows_of(i)
                    pe.wait_ge(p_done, n + 1)
                    if n >= 1:
                        pe.wait_ge(t_copied, n)
                    for x, (off, rows, vt) in enumerate(keys_of(i)[2]):
                        mm = nc.tensor.transpose(tp[0:rows, P * x:P * x + r], p[n % 2][0:r, off:off + rows], m["ident"][0:r, 0:r])
                    mm.then_inc(t_done, 1)
                n = t - 2
                if 0 <= n < N:
                    i, h = items[n]
                    r = rows_of(i)
                    pe.wait_ge(t_copied, n + 1)
                    if h == 0 and i >= 1:
                        pe.wait_ge(on_done, i)
                    tiles = keys_of(i)[2]
                    for x, (off, rows, vt) in enumerate(tiles):
                        mm = nc.tensor.matmul(op[0:r, HD * h:HD * (h + 1)], pT[n % 2][0:rows, P * x:P * x + r],
                                              m["mv"][0:rows, vt, HD * h:HD * (h + 1)], start=(x == 0), stop=(x == len(tiles) - 1),
                                              skip_group_check=True)
                    mm.then_inc(av_done, 1)
                n = t - 3
                if 0 <= n < N and items[n][1] == HEADS - 1:
                    i = items[n][0]
                    r = rows_of(i)
                    pe.wait_ge(on_done, i + 1)
                    if i >= 1:
                        pe.wait_ge(oT_copied, i)
                    for x in range(4):
                        mm = nc.tensor.transpose(oT[:, P * x:P * x + r], on[i % 2][0:r, P * x:P * (x + 1)], m["ident"][0:r, 0:r])
                    mm.then_inc(oT_done, 1)

        @block.scalar
        def _(act):
            for n, (i, h) in enumerate(items):
                r = rows_of(i)
                nk = keys_of(i)[1]
                act.wait_ge(nm_done, n + 1)
                if n >= 2:
                    act.wait_ge(t_done, n - 1)
                nc.scalar.activation(p[n % 2][0:r, 0:nk], sp[n % 2][0:r, 0:nk], ACT.Exp, bias=nm[0:r, n:n + 1],
                                     scale=MLA_SCALE, accum_out=rs[0:r, n:n + 1]).then_inc(p_done, 1)

        @block.vector
        def _(dve):
            for t in range(N + 3):
                if t < N:
                    i, h = items[t]
                    r = rows_of(i)
                    nk = keys_of(i)[1]
                    dve.wait_ge(s_done, t + 1)
                    if i < TILES:
                        nc.vector.memset(sp[t % 2][0:CHUNK, nk - CHUNK:nk], FAR).then_inc(masked, 1)
                        dve.wait_ge(masked, t + 1)
                    nc.vector.reduce_max(mx[0:r, t:t + 1], sp[t % 2][0:r, 0:nk], AX).then_inc(max_done, 1)
                    dve.wait_ge(max_done, t + 1)
                    nc.vector.tensor_scalar(nm[0:r, t:t + 1], mx[0:r, t:t + 1], -MLA_SCALE, None, ALU.mult).then_inc(nm_done, 1)
                n = t - 1
                if 0 <= n < N:
                    i, h = items[n]
                    r = rows_of(i)
                    tiles = keys_of(i)[2]
                    dve.wait_ge(t_done, n + 1)
                    if n >= 2:
                        dve.wait_ge(av_done, n - 1)
                    if i < TILES:
                        nc.vector.tensor_copy(pT[n % 2][:, 0:P * len(tiles)], tp[:, 0:P * len(tiles)]).then_inc(t_copied, 1)
                    else:
                        nc.vector.tensor_copy(pT[n % 2][0:NEW, 0:r], tp[0:NEW, 0:r]).then_inc(masked, 1)
                        for x in (1, 2):
                            ins = nc.vector.tensor_copy(pT[n % 2][:, P * x:P * x + r], tp[:, P * x:P * x + r])
                            ins.then_inc(t_copied if x == 2 else masked, 1)
                n = t - 2
                if 0 <= n < N and items[n][1] == HEADS - 1:
                    i = items[n][0]
                    r = rows_of(i)
                    dve.wait_ge(av_done, n + 1)
                    dve.wait_ge(p_done, n + 1)
                    at = slice(HEADS * i, HEADS * (i + 1))
                    nc.vector.reciprocal(ri[0:r, at], rs[0:r, at]).then_inc(inv_done, 1)
                    dve.wait_ge(inv_done, i + 1)
                    nc.vector.tensor_tensor(on[i % 2][0:r, :].rearrange("p (h d) -> p h d", h=HEADS),
                                            op[0:r, :].rearrange("p (h d) -> p h d", h=HEADS),
                                            ri[0:r, at].unsqueeze(2).broadcast_to([r, HEADS, HD]), ALU.mult).then_inc(on_done, 1)
                n = t - 3
                if 0 <= n < N and items[n][1] == HEADS - 1:
                    i = items[n][0]
                    r = rows_of(i)
                    dve.wait_ge(oT_done, i + 1)
                    nc.vector.tensor_copy(m["obT"][:, :, P * i:P * i + r],
                                          oT[:].rearrange("p (x q) -> p x q", x=4)[:, :, 0:r]).then_inc(oT_copied, 1)


def merge(nc, mem, a, m):
    with ExitStack() as s:
        w_oa = mem.at("w_oa", 0, [P, 4, D])
        w_ob = mem.at("w_ob", 16384, [P, 4, D])
        sig = [mem.at(f"gates{i}", 32768 + 8448 * i, [P, 2, TOKENS]) for i in range(2)]
        part = [mem.at(f"gated{i}", 49664 + 1408 * i, [P, SPAN]) for i in range(4)]
        ps = banks(nc, s, "merge_ps", 8)
        w_in, filled, gated, merged = sems(nc, s, "wo_in", "g_filled", "g_gated", "g_merged")
        sig_in = sems(nc, s, "sig_in_a", "sig_in_b")
        plan = [(j, c) for j in range(KC) for c in range(SPANS)]
        block = s.enter_context(nc.Block())

        @block.sync
        def _(sp):
            sp.dma_start(w_oa[:], a["w_oa"].rearrange("(k p) c -> p k c", p=P)).then_inc(w_in, 16)
            sp.dma_start(w_ob[:], a["w_ob"].rearrange("(k p) c -> p k c", p=P)).then_inc(w_in, 16)
            for j in range(KC):
                if j >= 2:
                    sp.wait_ge(gated, 2 * SPANS * (j - 1))
                sp.dma_start(sig[j % 2][:], a["gatesT"].rearrange("(g k p) t -> k p g t", g=2, p=P)[j]).then_inc(sig_in[j % 2], 16)

        @block.tensor
        def _(pe):
            pe.wait_ge(w_in, 32)
            for n, (j, c) in enumerate(plan):
                if n >= 4:
                    pe.wait_ge(gated, 2 * (n - 3))
                for x, (w, o) in enumerate(((w_oa, m["oaT"]), (w_ob, m["obT"]))):
                    for k in range(4):
                        mm = nc.tensor.matmul(ps[2 * (n % 4) + x][:, 0:SPAN], w[:, k, P * j:P * (j + 1)],
                                              o[:, k, SPAN * c:SPAN * (c + 1)], start=(k == 0), stop=(k == 3))
                mm.then_inc(filled, 1)

        @block.vector
        def _(dve):
            for n, (j, c) in enumerate(plan):
                cols = slice(SPAN * c, SPAN * (c + 1))
                if c == 0:
                    dve.wait_ge(sig_in[j % 2], 16 * (j // 2 + 1))
                dve.wait_ge(filled, n + 1)
                if n >= 2:
                    dve.wait_ge(merged, n - 1)
                for x in range(2):
                    nc.vector.tensor_tensor(part[2 * (n % 2) + x][:], ps[2 * (n % 4) + x][:, 0:SPAN], sig[j % 2][:, x, cols],
                                            ALU.mult).then_inc(gated, 1)
                dve.wait_ge(gated, 2 * (n + 1))
                nc.vector.tensor_tensor(m["mergedT"][:, j, cols], part[2 * (n % 2)][:], part[2 * (n % 2) + 1][:],
                                        ALU.add).then_inc(merged, 1)


def first_norm(nc, mem, a, m):
    with ExitStack() as s:
        w_out = mem.at("w_out", 142336, [P, KC, D])
        g = mem.at("ln1_g", 175104, [P, D])
        b = mem.at("ln1_b", 179200, [P, D])
        x = [mem.at(f"x_rows{i}", 183296 + 4096 * i, [P, D]) for i in range(2)]
        r_ = [mem.at(f"residual{i}", 191488 + 4096 * i, [P, D]) for i in range(2)]
        st = [mem.at(f"stats{i}", 199680 + 64 * i, [P, 16]) for i in range(2)]
        ps = banks(nc, s, "out_ps", 4)
        tp = banks(nc, s, "hT_ps", 4)
        w_in, gb_in, filled, res_done, step, root_done, inv_done, scaled, h_done, turned, t_copied = sems(
            nc, s, "w_out_in", "gb_in", "n_filled", "n_res", "n_step", "n_root", "n_inverse", "n_scaled", "h_done", "h_turned", "hT_copied")
        x_in = sems(nc, s, "xr_in_a", "xr_in_b")
        block = s.enter_context(nc.Block())

        @block.sync
        def _(sp):
            for c in range(2):
                sp.dma_start(w_out[:, :, 512 * c:512 * (c + 1)],
                             a["w_out"].rearrange("(k p) c -> p k c", p=P)[:, :, 512 * c:512 * (c + 1)]).then_inc(w_in, 16)
            sp.dma_start(g[:], a["ln1_g"].partition_broadcast(P)).then_inc(gb_in, 16)
            sp.dma_start(b[:], a["ln1_b"].partition_broadcast(P)).then_inc(gb_in, 16)
            for t in range(TILES + 1):
                r = rows_of(t)
                if t >= 2:
                    sp.wait_ge(res_done, 2 * (t - 1))
                sp.dma_start(x[t % 2][0:r, :], a["x"][P * t:P * t + r, :]).then_inc(x_in[t % 2], 16)

        @block.tensor
        def _(pe):
            pe.wait_ge(w_in, 32)
            for t in range(TILES + 2):
                if t <= TILES:
                    r = rows_of(t)
                    if t >= 2:
                        pe.wait_ge(res_done, 2 * (t - 1))
                    for c in range(2):
                        for k in range(KC):
                            mm = nc.tensor.matmul(ps[2 * (t % 2) + c][0:r, :], m["mergedT"][:, k, P * t:P * t + r],
                                                  w_out[:, k, 512 * c:512 * (c + 1)], start=(k == 0), stop=(k == KC - 1))
                        mm.then_inc(filled, 1)
                n = t - 1
                if n >= 0:
                    r = rows_of(n)
                    pe.wait_ge(h_done, n + 1)
                    if n >= 2:
                        pe.wait_ge(t_copied, 2 * (n - 1))
                    for k in range(KC):
                        mm = nc.tensor.transpose(tp[2 * (n % 2) + k // 4][:, P * (k % 4):P * (k % 4) + r],
                                                 m["h"][0:r, n, P * k:P * (k + 1)], m["ident"][0:r, 0:r])
                        if k % 4 == 3:
                            mm.then_inc(turned, 1)

        @block.scalar
        def _(act):
            for t in range(TILES + 2):
                if t <= TILES:
                    r = rows_of(t)
                    act.wait_ge(step, 3 * t + 3)
                    nc.scalar.activation(st[t % 2][0:r, 14:15], st[t % 2][0:r, 13:14], ACT.Sqrt, bias=m["eps"][0:r, :]).then_inc(root_done, 1)
                n = t - 1
                if n >= 0:
                    r = rows_of(n)
                    for y in range(2):
                        act.wait_ge(turned, 2 * n + y + 1)
                        nc.scalar.copy(m["hT"][:, 4 * y:4 * y + 4, P * n:P * n + r],
                                       tp[2 * (n % 2) + y][:].rearrange("p (x q) -> p x q", x=4)[:, :, 0:r]).then_inc(t_copied, 1)

        @block.vector
        def _(dve):
            dve.wait_ge(gb_in, 32)
            for t in range(TILES + 1):
                r = rows_of(t)
                if t >= 2:
                    dve.wait_ge(h_done, t - 1)
                dve.wait_ge(x_in[t % 2], 16 * (t // 2 + 1))
                s_ = st[t % 2]
                for c in range(2):
                    cols = slice(512 * c, 512 * (c + 1))
                    dve.wait_ge(filled, 2 * t + c + 1)
                    nc.vector.scalar_tensor_tensor(r_[t % 2][0:r, cols], x[t % 2][0:r, cols], ALPHA, ps[2 * (t % 2) + c][0:r, :],
                                                   ALU.mult, ALU.add).then_inc(res_done, 1)
                for c in range(2):
                    dve.wait_ge(res_done, 2 * t + c + 1)
                    nc.vector.bn_stats(s_[0:r, 6 * c:6 * c + 6], r_[t % 2][0:r, 512 * c:512 * (c + 1)]).then_inc(step, 1)
                dve.wait_ge(step, 3 * t + 2)
                nc.vector.bn_aggr(s_[0:r, 12:14], s_[0:r, 0:12]).then_inc(step, 1)
                dve.wait_ge(root_done, t + 1)
                nc.vector.reciprocal(s_[0:r, 15:16], s_[0:r, 14:15]).then_inc(inv_done, 1)
                dve.wait_ge(inv_done, t + 1)
                hrow = m["h"][0:r, t, :]
                nc.vector.tensor_scalar(r_[t % 2][0:r, :], r_[t % 2][0:r, :], s_[0:r, 12:13], s_[0:r, 15:16],
                                        ALU.subtract, ALU.mult).then_inc(scaled, 1)
                dve.wait_ge(scaled, 2 * t + 1)
                nc.vector.tensor_tensor(r_[t % 2][0:r, :], r_[t % 2][0:r, :], g[0:r, :], ALU.mult).then_inc(scaled, 1)
                dve.wait_ge(scaled, 2 * t + 2)
                nc.vector.tensor_tensor(hrow, r_[t % 2][0:r, :], b[0:r, :], ALU.add).then_inc(h_done, 1)
            dve.wait_ge(h_done, TILES + 1)


def route_experts(nc, mem, a, m):
    with ExitStack() as s:
        T = TILES + 1
        wq = [mem.at(f"wq_head{i}", 107520 + 8192 * i, [P, KC, 2 * PKEYS]) for i in range(2)]
        qT = [mem.at(f"peer_qT{i}", 123904 + 8448 * i, [P, 2, TOKENS]) for i in range(2)]
        sub = [mem.at(f"sub_keysT{i}", 140800 + 1024 * i, [P, 2, PKEYS]) for i in range(2)]
        gate = [mem.at(f"expert_gate{i}", 142848 + 576 * i, [P, T, TOPK]) for i in range(2)]
        flat = [mem.at(f"gate_address{i}", 144000 + 256 * i, [P, DENSE, TOPK], U32) for i in range(2)]
        best = mem.at("best", 144512, [P, 2, TOPK])
        besti = mem.at("best_index", 144640, [P, 2, TOPK], U32)
        bestf = mem.at("best_index_f", 144768, [P, 2, TOPK])
        pos = mem.at("pair_position", 144896, [P, TOPK], U32)
        ab = mem.at("pair_ranks", 144960, [P, 2, TOPK], U32)
        abf = mem.at("pair_ranks_f", 145088, [P, 2, TOPK])
        pick = mem.at("picked", 145216, [P, 2, TOPK])
        expert = mem.at("expert_f", 145344, [P, TOPK])
        iota_u = mem.at("rank_iota_u", 145408, [P, TOPK], U32)
        iota = mem.at("rank_iota", 145472, [P, TOPK])
        token_u = mem.at("dense_token_u", 145536, [P, DENSE], U32)
        token = mem.at("dense_token", 145568, [P, DENSE])
        mx = mem.at("gate_max", 145600, [P, T])
        sm = mem.at("gate_sum", 145664, [P, T])
        iv = mem.at("gate_inverse", 145728, [P, T])
        left = mem.at("scores_left", 146432, [P, 2, PKEYS])
        cand = mem.at("pair_scores", 147456, [P, TOPK * TOPK])
        cand2 = mem.at("pair_scores_left", 148480, [P, TOPK * TOPK])
        hot = mem.at("one_hot", 149504, [P, 2, TOPK * TOPK])
        idx_all, gate_all = m["idx_all"], m["gate_all"]
        qp = banks(nc, s, "peer_q_ps", 4)
        scp = banks(nc, s, "peer_score_ps", 2)
        (cleared, fine, norm, made, acc_set, q_filled, q_copied, scored, routed, step, exped, gated, kept, added,
         compacted, packed) = sems(
            nc, s, "gates_cleared", "route_fine_step", "gate_norm_step", "r_made", "acc_set", "q_filled", "q_copied", "scored",
            "routed", "route_step", "exp_done", "gates_ready", "gates_kept", "gates_added", "hT_compacted", "packed_in")
        wq_in = sems(nc, s, "wq_in_a", "wq_in_b")
        sub_in = sems(nc, s, "sub_in_a", "sub_in_b")
        block = s.enter_context(nc.Block())
        QT = 2 * SPANS
        SCATTERS = DENSE * TOPK
        FINE_T = 25
        FINE = T * FINE_T

        def over_heads(eng, body):
            body(0, 0)
            body(1, 1)
            with eng.Fori(1, HEADS // 2 - 1) as pair:
                for par in range(2):
                    body(pair * 2 + par, par)
            body(HEADS - 2, 0)
            body(HEADS - 1, 1)

        @block.sync
        def _(sp):
            for h in range(HEADS):
                if h >= 2:
                    sp.wait_ge(q_filled, (h - 1) * QT)
                sp.dma_start(wq[h % 2][:], a["peer_wq"].rearrange("(k p) c -> p k c", p=P)[:, :, 2 * PKEYS * h:2 * PKEYS * (h + 1)]).then_inc(wq_in[h % 2], 16)
                if h >= 2:
                    sp.wait_ge(scored, (h - 1) * T)
                sp.dma_start(sub[h % 2][:], a["sub_keysT"].rearrange("(h c p) n -> h p c n", h=HEADS, c=2)[h]).then_inc(sub_in[h % 2], 16)
            sp.wait_ge(acc_set, T)
            sp.wait_ge(kept, 2 * HEADS)
            sp.wait_ge(routed, HEADS * T)
            for q in range(4):
                part = slice(NEW * q, NEW * (q + 1))
                sp.dma_start(m["idx_s"][part, :, :], idx_all[0:NEW, :, GATHER, 4 * q:4 * q + 4]).then_inc(packed, 16)
                sp.dma_start(m["gate_s"][part, :, :], gate_all[0:NEW, :, GATHER, 4 * q:4 * q + 4]).then_inc(packed, 16)
                if q >= 1:
                    sp.dma_start(m["h"][part, TILES, :], m["h"][0:NEW, TILES, :]).then_inc(packed, 16)
            sp.wait_ge(packed, 16 * 11)

        @block.gpsimd
        def _(pool):
            pool.iota(iota_u[:], pattern=[[1, TOPK]], base=0, channel_multiplier=0).then_inc(made, 1)
            pool.iota(token_u[:], pattern=[[P, DENSE]], base=0, channel_multiplier=1).then_inc(made, 1)
            pool.wait_ge(made, 2)
            pool.tensor_copy(iota[:], iota_u[:]).then_inc(made, 1)
            pool.tensor_copy(token[:], token_u[:]).then_inc(made, 1)

            def scatter(h, par):
                pool.wait_ge(gated, h + 1)
                pool.nop(nofuse=True)
                if not (isinstance(h, int) and h == 0):
                    pool.wait_ge(added, h * (16 * SCATTERS))
                    pool.nop(nofuse=True)
                for t in range(DENSE):
                    for k in range(TOPK):
                        pool.indirect_dma_start(a["gates_by_expert"], bass.IndirectOffsetOnAxis(ap=flat[par][:, t, k:k + 1], axis=0),
                                                gate[par][:, GATHER + t, k:k + 1], None, compute_op=ALU.add).then_inc(added, 16)

            over_heads(pool, scatter)
            pool.wait_ge(added, HEADS * 16 * SCATTERS)

        @block.tensor
        def _(pe):
            def queries(h, par):
                pe.wait_ge(wq_in[par], 16 * (h // 2 + 1) if isinstance(h, int) else (h - par) * 8 + 16)
                for n in range(QT):
                    if n >= 4 or not (isinstance(h, int) and h == 0):
                        pe.wait_ge(q_copied, h * QT + (n - 3 if n >= 4 else 0))
                    c, y = n // SPANS, n % SPANS
                    for k in range(KC):
                        mm = nc.tensor.matmul(qp[n % 4][:, 0:SPAN], wq[par][:, k, PKEYS * c:PKEYS * (c + 1)],
                                              m["hT"][:, k, SPAN * y:SPAN * (y + 1)], start=(k == 0), stop=(k == KC - 1))
                    mm.then_inc(q_filled, 1)

            def route(h, par):
                if not (isinstance(h, int) and h == HEADS - 1):
                    queries(h + 1, 1 - par)
                pe.wait_ge(sub_in[par], 16 * (h // 2 + 1) if isinstance(h, int) else (h - par) * 8 + 16)
                pe.wait_ge(q_copied, h * QT + QT)
                for t in range(T):
                    r = rows_of(t)
                    if not (isinstance(h, int) and h == 0 and t < 2):
                        pe.wait_ge(routed, h * T + (t - 1))
                    for c in range(2):
                        mm = nc.tensor.matmul(scp[(t + par) % 2][0:r, PKEYS * c:PKEYS * (c + 1)], qT[par][:, c, P * t:P * t + r],
                                              sub[par][:, c, :], start=True, stop=True)
                    mm.then_inc(scored, 1)

            queries(0, 0)
            over_heads(pe, route)

        @block.scalar
        def _(act):
            def copy_queries(h, par):
                if not (isinstance(h, int) and h < 2):
                    act.wait_ge(scored, (h - 1) * T)
                for n in range(QT):
                    act.wait_ge(q_filled, h * QT + (n + 1))
                    nc.scalar.copy(qT[par][:, n // SPANS, SPAN * (n % SPANS):SPAN * (n % SPANS + 1)],
                                   qp[n % 4][:, 0:SPAN]).then_inc(q_copied, 1)

            def route(h, par):
                if not (isinstance(h, int) and h == HEADS - 1):
                    copy_queries(h + 1, 1 - par)
                act.wait_ge(step, h * 2 + 2)
                nc.scalar.activation(gate[par][:], gate[par][:], ACT.Exp).then_inc(exped, 1)
                act.wait_ge(gated, h + 1)
                nc.scalar.activation(gate_all[:, h, 0:GATHER, :] if isinstance(h, int) else
                                     gate_all[:, bass.ds(h, 1), 0:GATHER, :].rearrange("p o t k -> p (o t) k"),
                                     gate[par][:, 0:GATHER, :], ACT.Copy).then_inc(kept, 1)
                nc.scalar.activation(gate_all[:, h, GATHER, :] if isinstance(h, int) else
                                     gate_all[:, bass.ds(h, 1), GATHER, :].rearrange("p o k -> p (o k)"),
                                     gate[par][:, TILES, :], ACT.Copy).then_inc(kept, 1)

            for t in range(TILES):
                nc.scalar.mul(m["acc"][:, t, :], m["h"][:, t, :], ALPHA).then_inc(acc_set, 1)
            act.wait_ge(cleared, 3)
            nc.scalar.mul(m["acc"][0:NEW, TILES, :], m["h"][0:NEW, TILES, :], ALPHA).then_inc(acc_set, 1)
            act.wait_ge(acc_set, T)
            for k in range(KC):
                nc.scalar.copy(m["hTd"][:, k, :], m["hT"][:, k, P * GATHER:SEQ]).then_inc(compacted, 1)
            act.wait_ge(compacted, KC)
            copy_queries(0, 0)
            over_heads(act, route)
            act.wait_ge(kept, 2 * HEADS)

        @block.vector
        def _(dve):
            nc.vector.memset(gate[0][:, T - 1, :], 0.0).then_inc(cleared, 1)
            nc.vector.memset(gate[1][:, T - 1, :], 0.0).then_inc(cleared, 1)
            nc.vector.memset(m["acc"][:, TILES, :], 0.0).then_inc(cleared, 1)
            dve.wait_ge(cleared, 3)
            dve.wait_ge(made, 4)

            def route(h, par, t):
                r = rows_of(t)
                base = h * FINE + t * FINE_T
                at = [0]

                def after(ins):
                    ins.then_inc(fine, 1)
                    at[0] += 1

                def sync():
                    dve.wait_ge(fine, base + at[0])
                    dve.nop(nofuse=True)

                if not (isinstance(h, int) and h == 0 and t == 0):
                    sync()
                dve.wait_ge(scored, h * T + (t + 1))
                dve.nop(nofuse=True)
                for x in range(2):
                    sc = scp[(t + par) % 2][0:r, PKEYS * x:PKEYS * (x + 1)]
                    after(nc.vector.max(best[0:r, x, 0:8], sc))
                sync()
                for x in range(2):
                    sc = scp[(t + par) % 2][0:r, PKEYS * x:PKEYS * (x + 1)]
                    after(nc.vector.match_replace(left[0:r, x, :], best[0:r, x, 0:8], sc, LOWEST))
                    after(nc.vector.max_index(besti[0:r, x, 0:8], best[0:r, x, 0:8], sc))
                sync()
                for x in range(2):
                    after(nc.vector.max(best[0:r, x, 8:16], left[0:r, x, :]))
                sync()
                for x in range(2):
                    after(nc.vector.max_index(besti[0:r, x, 8:16], best[0:r, x, 8:16], left[0:r, x, :]))
                pair = cand[0:r, :].rearrange("p (i j) -> p i j", i=TOPK)
                after(nc.vector.tensor_tensor(pair, best[0:r, 0, :].unsqueeze(2).broadcast_to([r, TOPK, TOPK]),
                                              best[0:r, 1, :].unsqueeze(1).broadcast_to([r, TOPK, TOPK]), ALU.add))
                sync()
                g = gate[par][0:r, t, :]
                after(nc.vector.max(g[:, 0:8], cand[0:r, :]))
                after(nc.vector.tensor_copy(bestf[0:r], besti[0:r]))
                sync()
                after(nc.vector.match_replace(cand2[0:r, :], g[:, 0:8], cand[0:r, :], LOWEST))
                after(nc.vector.max_index(pos[0:r, 0:8], g[:, 0:8], cand[0:r, :]))
                sync()
                after(nc.vector.max(g[:, 8:16], cand2[0:r, :]))
                sync()
                after(nc.vector.max_index(pos[0:r, 8:16], g[:, 8:16], cand2[0:r, :]))
                sync()
                after(nc.vector.tensor_scalar(ab[0:r, 0, :], pos[0:r, :], 4, None, ALU.logical_shift_right))
                after(nc.vector.tensor_scalar(ab[0:r, 1, :], pos[0:r, :], 15, None, ALU.bitwise_and))
                sync()
                after(nc.vector.tensor_copy(abf[0:r], ab[0:r]))
                sync()
                oh = hot[0:r].rearrange("p x (k j) -> p (x k) j", j=TOPK)
                after(nc.vector.tensor_tensor(oh, abf[0:r].rearrange("p x k -> p (x k)").unsqueeze(2).broadcast_to([r, 2 * TOPK, TOPK]),
                                              iota[0:r, :].unsqueeze(1).broadcast_to([r, 2 * TOPK, TOPK]), ALU.is_equal))
                sync()
                for x in range(2):
                    o3 = hot[0:r, x, :].rearrange("p (k j) -> p k j", j=TOPK)
                    after(nc.vector.tensor_tensor(o3, o3, bestf[0:r, x, :].unsqueeze(1).broadcast_to([r, TOPK, TOPK]), ALU.mult))
                sync()
                after(nc.vector.tensor_reduce(pick[0:r].rearrange("p x k -> p (x k)"), oh, AX, ALU.add))
                sync()
                after(nc.vector.scalar_tensor_tensor(expert[0:r, :], pick[0:r, 0, :], float(PKEYS), pick[0:r, 1, :],
                                                     ALU.mult, ALU.add))
                sync()
                assert at[0] == FINE_T, at[0]
                if GATHER <= t < TILES:
                    nc.vector.tensor_scalar(flat[par][:, t - GATHER, :], expert[:], float(P * DENSE),
                                            token[:, t - GATHER:t - GATHER + 1], ALU.mult, ALU.add).then_inc(routed, 1)
                else:
                    u = min(t, GATHER)
                    nc.vector.tensor_copy(idx_all[0:r, h, u, :] if isinstance(h, int) else
                                          idx_all[0:r, bass.ds(h, 1), u, :].rearrange("p o k -> p (o k)"),
                                          expert[0:r, :]).then_inc(routed, 1)

            def route_head(h, par):
                if not (isinstance(h, int) and h < 2):
                    dve.wait_ge(kept, h * 2 - 2)
                    dve.wait_ge(added, (h - 1) * (16 * SCATTERS))
                for t in range(T):
                    route(h, par, t)
                dve.wait_ge(routed, h * T + T)
                if not (isinstance(h, int) and h == 0):
                    dve.wait_ge(gated, h)
                nc.vector.tensor_copy(mx[:, :], gate[par][:, :, 0]).then_inc(step, 1)
                dve.wait_ge(step, h * 2 + 1)
                nc.vector.tensor_tensor(gate[par][:], gate[par][:], mx[:, :].unsqueeze(2).broadcast_to([P, T, TOPK]),
                                        ALU.subtract).then_inc(step, 1)
                dve.wait_ge(exped, h + 1)
                nc.vector.tensor_reduce(sm[:, :], gate[par][:], AX, ALU.add).then_inc(norm, 1)
                dve.wait_ge(norm, h * 2 + 1)
                nc.vector.reciprocal(iv[:, :], sm[:, :]).then_inc(norm, 1)
                dve.wait_ge(norm, h * 2 + 2)
                nc.vector.tensor_tensor(gate[par][:], gate[par][:], iv[:, :].unsqueeze(2).broadcast_to([P, T, TOPK]),
                                        ALU.mult).then_inc(gated, 1)

            over_heads(dve, route_head)
            dve.wait_ge(gated, HEADS)


def apply_experts(nc, mem, a, m):
    with ExitStack() as s:
        vals = mem.at("value_rows", 0, [P, 8, D])
        ring = mem.at("expert_rows", 107520, [P, SLOTS, 2 * D])
        keys = mem.at("key_columns", 173056, [P, 2, KC, P])
        gts = mem.at("dense_gates", 181248, [P, 2, P * DENSE])
        w = mem.at("dense_weights", 185344, [P, 8, P * DENSE])
        junk = mem.at("unused_products", 201728, [P, D], BF16)
        cur = mem.at("head_index", 209920, [P, GATHER, TOPK], U32)
        curg = mem.at("head_gate", 210176, [P, GATHER, TOPK])
        dots = mem.at("dots", 210432, [P, 8])
        gel = mem.at("activated", 210464, [P, 8])
        coef = mem.at("coefficients", 210496, [P, 8])
        up = banks(nc, s, "dense_act_ps", 2)
        vp = [s.enter_context(nc.psum_tensor(f"dense_out_ps{i}", [P, D], F32)) for i in range(2)]
        ss = s.enter_context(nc.psum_tensor("sample_sum_ps", [P, D], F32))
        (cur_set, dotted, gelud, weighed, used, act_filled, act_gelud, act_gated, v_filled, v_added, summed) = sems(
            nc, s, "head_index_set", "dotted", "gelu_done", "coef_done", "row_used", "dense_filled", "dense_gelu",
            "dense_weighed", "dense_out_filled", "dense_out_added", "sample_summed")
        got = sems(nc, s, *[f"row_in{i}" for i in range(SLOTS)])
        keys_in = sems(nc, s, "key_columns_in_a", "key_columns_in_b")
        gts_in = sems(nc, s, "dense_gates_in_a", "dense_gates_in_b")
        vals_in = sems(nc, s, *[f"value_rows_in{i}" for i in range(8)])
        block = s.enter_context(nc.Block())
        SROWS = HEADS * 4
        ROWS = GATHER * TOPK
        ET = 16
        PER = ROWS // ET
        GRP = 4

        def iterations(eng, body):
            body(0)
            with eng.Fori(1, HEADS) as i:
                body(i)

        def first(i):
            return isinstance(i, int) and i == 0

        @block.sync
        def _(sp):
            keysT = a["key_columns"]
            table = a["experts"].rearrange("(n p) c -> n p c", p=P)
            dgates = a["gates_by_expert"].rearrange("(n p t) o -> n p (t o)", p=P, t=P * DENSE)

            def tile(src, n):
                return src[n] if isinstance(n, int) else src[bass.ds(n, 1)]

            def flatten(x, n, dims):
                return x if isinstance(n, int) else x.rearrange(f"o {dims} -> (o p) {dims[2:]}")

            def loads(i):
                for e in range(ET):
                    n = i * ET + e
                    if not (first(i) and e < 2):
                        sp.wait_ge(act_filled, n - 1)
                    sp.dma_start(keys[:, e % 2, :, :], flatten(tile(keysT, n), n, "p k e")).then_inc(keys_in[e % 2], 16)
                    if not (first(i) and e < 2):
                        sp.wait_ge(act_gated, n - 1)
                    sp.dma_start(gts[:, e % 2, :], flatten(tile(dgates, n), n, "p t")).then_inc(gts_in[e % 2], 16)
                    if not (first(i) and e < 8):
                        sp.wait_ge(v_filled, i * ET + (e - e % GRP - GRP))
                    sp.dma_start(vals[:, e % 8, :], flatten(tile(table, n), n, "p c")[:, D:2 * D]).then_inc(vals_in[e % 8], 16)

            iterations(sp, loads)

        @block.gpsimd
        def _(pool):
            def gather(slot, source):
                pool.indirect_dma_start(ring[:, slot, :], None, a["experts"],
                                        bass.IndirectOffsetOnAxis(ap=source, axis=0)).then_inc(got[slot], 16)

            for x in range(SROWS):
                if x >= SLOTS:
                    pool.wait_ge(used, x - SLOTS + 1)
                gather(x % SLOTS, m["idx_s"][:, x // 4, x % 4:x % 4 + 1])

            def head(i):
                for t in range(GATHER):
                    for k in range(TOPK):
                        x = SROWS + TOPK * t + k
                        pool.wait_ge(used, i * ROWS + (x - SLOTS + 1))
                        pool.nop(nofuse=True)
                        if k == 0:
                            for src, dst in ((m["idx_all"], cur), (m["gate_all"], curg)):
                                pool.tensor_copy(dst[:, t, :], src[:, i, t, :] if isinstance(i, int) else
                                                 src[:, bass.ds(i, 1), t, :].rearrange("p o k -> p (o k)")).then_inc(cur_set, 1)
                            pool.wait_ge(cur_set, i * (2 * GATHER) + 2 * (t + 1))
                            pool.nop(nofuse=True)
                        gather(x % SLOTS, cur[:, t, k:k + 1])

            iterations(pool, head)

        @block.tensor
        def _(pe):
            def add_values(i, e):
                tt = e % GRP
                g0 = (e - tt - GRP) % 8
                n = i * ET + e
                if tt == 0:
                    pe.wait_ge(act_gated, n)
                    for y in range(GRP):
                        b = g0 + y
                        pe.wait_ge(vals_in[b], i * (ET // 8 * 16) + 16 * ((e - GRP + y) // 8 + 1))
                if not (first(i) and e < GRP + 2):
                    pe.wait_ge(v_added, i * (2 * ET) + 2 * (e - GRP - 1))
                for half in range(2):
                    for y in range(GRP):
                        mm = nc.tensor.matmul(vp[tt % 2][:, 512 * half:512 * (half + 1)], w[:, g0 + y, P * tt:P * (tt + 1)],
                                              vals[:, g0 + y, 512 * half:512 * (half + 1)], start=(y == 0), stop=(y == GRP - 1))
                mm.then_inc(v_filled, 1)

            def tiles(i):
                for e in range(ET):
                    n = i * ET + e
                    pe.wait_ge(keys_in[e % 2], i * (ET // 2 * 16) + 16 * (e // 2 + 1))
                    if not (first(i) and e < 2):
                        pe.wait_ge(act_gelud, n - 1)
                    for k in range(KC):
                        mm = nc.tensor.matmul(up[e % 2][:], keys[:, e % 2, k, :], m["hTd"][:, k, :], start=(k == 0), stop=(k == KC - 1))
                    mm.then_inc(act_filled, 1)
                    if not (first(i) and e < GRP):
                        add_values(i, e)

            iterations(pe, tiles)
            for e in range(GRP):
                add_values(HEADS, e)
            pe.wait_ge(used, SROWS)
            for half in range(2):
                for q in range(4):
                    mm = nc.tensor.matmul(ss[0:NEW, 512 * half:512 * (half + 1)], m["ident"][:, NEW * q:NEW * (q + 1)],
                                          m["acc"][:, TILES, 512 * half:512 * (half + 1)], start=(q == 0), stop=(q == 3))
            mm.then_inc(summed, 1)

        @block.scalar
        def _(act):
            def weight(i, x, gate):
                c = x % 8
                act.wait_ge(dotted, i * ROWS + (x + 1))
                if x >= 8:
                    act.wait_ge(used, i * ROWS + (x - 7))
                nc.scalar.activation(gel[:, c:c + 1], dots[:, c:c + 1], ACT.Gelu).then_inc(gelud, 1)
                act.wait_ge(gelud, i * ROWS + (x + 1))
                nc.scalar.activation(coef[:, c:c + 1], gel[:, c:c + 1], ACT.Copy, scale=gate).then_inc(weighed, 1)

            for x in range(SROWS):
                weight(0, x, m["gate_s"][:, x // 4, x % 4:x % 4 + 1])

            def tiles(i):
                for e in range(ET):
                    n = i * ET + e
                    act.wait_ge(act_filled, n + 1)
                    if not (first(i) and e < 8):
                        act.wait_ge(v_filled, i * ET + (e - e % GRP - GRP))
                    nc.scalar.activation(w[:, e % 8, :], up[e % 2][:], ACT.Gelu).then_inc(act_gelud, 1)
                    for y in range(PER):
                        x = PER * e + y
                        weight(i, SROWS + x, curg[:, x // TOPK, x % TOPK:x % TOPK + 1])

            iterations(act, tiles)

        @block.vector
        def _(dve):
            def dot(i, x, h):
                slot = x % SLOTS
                dve.wait_ge(got[slot], i * (16 * ROWS // SLOTS) + 16 * (x // SLOTS + 1))
                if x >= 1:
                    dve.wait_ge(dotted, i * ROWS + x)
                if x >= 8:
                    dve.wait_ge(gelud, i * ROWS + (x - 7))
                nc.vector.scalar_tensor_tensor(junk[:], ring[:, slot, 0:D], 1.0, h, ALU.mult, ALU.mult,
                                               accum_out=dots[:, x % 8:x % 8 + 1]).then_inc(dotted, 1)

            def value(i, x, sum_):
                dve.wait_ge(weighed, i * ROWS + (x + 1))
                if x >= 1:
                    dve.wait_ge(used, i * ROWS + x)
                nc.vector.scalar_tensor_tensor(sum_, ring[:, x % SLOTS, D:2 * D], coef[:, x % 8:x % 8 + 1], sum_,
                                               ALU.mult, ALU.add).then_inc(used, 1)

            for x in range(SROWS + LAG):
                if x < SROWS:
                    dot(0, x, m["h"][:, TILES, :])
                if x >= LAG:
                    value(0, x - LAG, m["acc"][:, TILES, :])

            def add_dense(i, e):
                tt = e % GRP
                dve.wait_ge(v_filled, i * ET + (e - GRP + 1))
                for half in range(2):
                    cols = slice(512 * half, 512 * (half + 1))
                    sum_ = m["acc"][:, GATHER + tt, cols]
                    nc.vector.tensor_tensor(sum_, sum_, vp[tt % 2][:, cols], ALU.add).then_inc(v_added, 1)

            def tiles(i):
                for e in range(ET):
                    n = i * ET + e
                    dve.wait_ge(gts_in[e % 2], i * (ET // 2 * 16) + 16 * (e // 2 + 1))
                    dve.wait_ge(act_gelud, n + 1)
                    nc.vector.tensor_tensor(w[:, e % 8, :], w[:, e % 8, :], gts[:, e % 2, :], ALU.mult).then_inc(act_gated, 1)
                    for y in range(PER):
                        x = PER * e + y
                        dot(i, SROWS + x, m["h"][:, x // TOPK, :])
                        if x % TOPK >= LAG:
                            value(i, SROWS + x - LAG, m["acc"][:, x // TOPK, :])
                        if x % TOPK == TOPK - 1:
                            for z in range(x - LAG + 1, x + 1):
                                value(i, SROWS + z, m["acc"][:, x // TOPK, :])
                    if not (first(i) and e < GRP):
                        if not (first(i) and e < 2 * GRP):
                            dve.wait_ge(v_added, i * (2 * ET) + 2 * (e - 2 * GRP + 1))
                        add_dense(i, e)

            iterations(dve, tiles)
            for e in range(GRP):
                dve.wait_ge(v_added, HEADS * 2 * ET + 2 * (e - 2 * GRP + 1))
                add_dense(HEADS, e)
            dve.wait_ge(summed, 1)
            nc.vector.tensor_copy(m["acc"][0:NEW, TILES, :], ss[0:NEW, :]).then_inc(used, 1)
            dve.wait_ge(used, SROWS + HEADS * ROWS + 1)
            dve.wait_ge(v_added, 2 * HEADS * ET)


def last_norm(nc, mem, a, m):
    with ExitStack() as s:
        T = TILES + 1
        g = mem.at("ln2_g", 107520, [P, D])
        b = mem.at("ln2_b", 111616, [P, D])
        st = mem.at("stats_y", 115712, [P, T, 16])
        gb_in, step, root_done, inv_done, scaled, y_done, out_done = sems(
            nc, s, "ln2_in", "y_step", "y_root", "y_inverse", "y_scaled", "y_done", "y_out")
        block = s.enter_context(nc.Block())

        @block.sync
        def _(sp):
            sp.dma_start(g[:], a["ln2_g"].partition_broadcast(P)).then_inc(gb_in, 16)
            sp.dma_start(b[:], a["ln2_b"].partition_broadcast(P)).then_inc(gb_in, 16)
            for t in range(T):
                r = rows_of(t)
                sp.wait_ge(y_done, t + 1)
                sp.dma_start(a["out_y"][P * t:P * t + r, :], m["acc"][0:r, t, :]).then_inc(out_done, 16)
            sp.wait_ge(out_done, 16 * T)

        @block.scalar
        def _(act):
            for t in range(T):
                r = rows_of(t)
                act.wait_ge(step, 3 * t + 3)
                nc.scalar.activation(st[0:r, t, 14:15], st[0:r, t, 13:14], ACT.Sqrt, bias=m["eps"][0:r, :]).then_inc(root_done, 1)

        @block.vector
        def _(dve):
            for t in range(T):
                r = rows_of(t)
                for c in range(2):
                    nc.vector.bn_stats(st[0:r, t, 6 * c:6 * c + 6], m["acc"][0:r, t, 512 * c:512 * (c + 1)]).then_inc(step, 1)
                dve.wait_ge(step, 3 * t + 2)
                nc.vector.bn_aggr(st[0:r, t, 12:14], st[0:r, t, 0:12]).then_inc(step, 1)
            dve.wait_ge(gb_in, 32)
            for t in range(T):
                r = rows_of(t)
                row = m["acc"][0:r, t, :]
                dve.wait_ge(root_done, t + 1)
                nc.vector.reciprocal(st[0:r, t, 15:16], st[0:r, t, 14:15]).then_inc(inv_done, 1)
                dve.wait_ge(inv_done, t + 1)
                nc.vector.tensor_scalar(row, row, st[0:r, t, 12:13], st[0:r, t, 15:16], ALU.subtract, ALU.mult).then_inc(scaled, 1)
                dve.wait_ge(scaled, 2 * t + 1)
                nc.vector.tensor_tensor(row, row, g[0:r, :], ALU.mult).then_inc(scaled, 1)
                dve.wait_ge(scaled, 2 * t + 2)
                nc.vector.tensor_tensor(row, row, b[0:r, :], ALU.add).then_inc(y_done, 1)


def kernel(x_prompt, x_sample, cache_sb_k, cache_sb_v, cache_mla_ckv, cache_mla_kpe, w_in, q_norm_g, w_uq, kv_norm_g,
           w_uk, w_uv, w_oa, w_ob, w_out, ln1_g, ln1_b, peer_wq, peer_sub_keys, peer_u, peer_v, ln2_g, ln2_b):
    import numpy as np
    import concourse.bacc as bacc
    from concourse.bass_utils import run_bass_kernel_spmd

    half = RD // 2
    swap = np.concatenate([np.arange(half, RD), np.arange(half)])
    x = np.concatenate([np.asarray(x_prompt)[0], np.asarray(x_sample)[0]], axis=0)
    w_in0, w_uq0 = np.asarray(w_in)[0], np.asarray(w_uq)[0]
    c_kr = 3 * SBW + QL + KVL
    positions = np.concatenate([np.arange(SEQ), PAST + np.arange(NEW)]).astype(np.float32)
    rates = (np.float32(10000.0) ** (-np.arange(half, dtype=np.float32) / np.float32(half))).astype(np.float32)
    angles = rates[:, None] * positions[None, :]
    cos, sin = np.cos(angles), np.sin(angles)
    arrays = {
        "x": x,
        "xT": x.T,
        "w_in": w_in0,
        "w_kr_swapped": w_in0[:, c_kr:c_kr + RD][:, swap],
        "past_sb_kT": np.asarray(cache_sb_k)[0, 0].reshape(PAST, SBW).T,
        "past_sb_v": np.asarray(cache_sb_v)[0, 0].reshape(PAST, SBW),
        "past_ckvT": np.asarray(cache_mla_ckv)[0, 0].T,
        "past_kpeT": np.asarray(cache_mla_kpe)[0, 0].T,
        "cosT": np.concatenate([cos, cos], axis=0),
        "sinT": np.concatenate([-sin, sin], axis=0),
        "norm_gains": np.concatenate([np.asarray(q_norm_g)[0], np.asarray(kv_norm_g)[0]]).reshape(QC + VC, P).T,
        "w_uq": w_uq0,
        "w_uq_swapped": w_uq0.reshape(QL, HEADS, MD)[:, :, HD:][:, :, swap].reshape(QL, HEADS * RD),
        "w_uk": np.asarray(w_uk)[0],
        "w_uv": np.asarray(w_uv)[0],
        "w_oa": np.asarray(w_oa)[0],
        "w_ob": np.asarray(w_ob)[0],
        "w_out": np.asarray(w_out)[0],
        "ln1_g": np.asarray(ln1_g)[0],
        "ln1_b": np.asarray(ln1_b)[0],
        "peer_wq": np.asarray(peer_wq)[0],
        "sub_keysT": np.asarray(peer_sub_keys)[0].transpose(0, 1, 3, 2).reshape(HEADS * 2 * PKEYS, PKEYS),
        "experts": np.concatenate([np.asarray(peer_u)[0], np.asarray(peer_v)[0]], axis=1),
        "key_columns": np.asarray(peer_u)[0].reshape(EXPERTS // P, P, KC, P).transpose(0, 3, 2, 1),
        "ln2_g": np.asarray(ln2_g)[0],
        "ln2_b": np.asarray(ln2_b)[0],
    }
    arrays = {k: np.ascontiguousarray(v) for k, v in arrays.items()}
    nc = bacc.Bacc("TRN2", target_bir_lowering=False, num_devices=1)
    a = {k: nc.dram_tensor(f"in_{k}", v.shape, F32, kind="ExternalInput").ap() for k, v in arrays.items()}
    a["gates_by_expert"] = nc.dram_tensor("gates_by_expert", (EXPERTS * P * DENSE, 1), F32).ap()
    a["gatesT"] = nc.dram_tensor("gatesT", (2 * D, TOKENS), F32).ap()
    outs = {"out_y": (TOKENS, D), "out_kT": (SBW, TOKENS), "out_v": (TOKENS, SBW), "out_ckvT": (KVL, TOKENS), "out_kpeT": (RD, TOKENS)}
    for k, shape in outs.items():
        a[k] = nc.dram_tensor(k, shape, F32, kind="ExternalOutput").ap()
    hybrid_stream_step(nc, a)
    r = run_bass_kernel_spmd(nc, [{f"in_{k}": v for k, v in arrays.items()}], core_ids=[0]).results[0]
    y, v = r["out_y"], r["out_v"]
    k, ckv, kpe = (np.ascontiguousarray(r[n].T) for n in ("out_kT", "out_ckvT", "out_kpeT"))

    def state(z, rows, *tail):
        return z[rows].reshape(1, 1, -1, *tail)

    both = (slice(0, SEQ), slice(SEQ, TOKENS))
    new = [[state(k, w, HEADS, HD), state(v, w, HEADS, HD), state(ckv, w, KVL), state(kpe, w, RD)] for w in both]
    return (y[both[0]].reshape(1, SEQ, D), y[both[1]].reshape(1, NEW, D), *new[0], *new[1])
```

```python
from contextlib import ExitStack

import concourse.bass as bass
from concourse import mybir

F32 = mybir.dt.float32
BF16 = mybir.dt.bfloat16
U32 = mybir.dt.uint32
ALU = mybir.AluOpType
ACT = mybir.ActivationFunctionType
AX = mybir.AxisListType.X

P = 128
D = 1024
KC = D // P
SEQ, NEW, PAST = 1024, 32, 256
TOKENS = SEQ + NEW
KEYS = TOKENS + PAST
TILES = SEQ // P
SPAN = 352
SPANS = TOKENS // SPAN
HEADS, HD = 8, 64
SBW = HEADS * HD
QL, KVL, RD = 384, 256, 32
QC, VC = QL // P, KVL // P
MD = HD + RD
CHUNK = 64
PKEYS, TOPK, EXPERTS = 128, 16, 128 * 128
GATHER, DENSE = 4, 4
EARLY = 2
SLOTS = 8
LAG = 3
ALPHA = 2.0 ** 0.25
EPS = 1e-5
MLA_SCALE = float(MD) ** -0.5
FAR = -1.0e30
LOWEST = -3.0e38


def rows_of(tile):
    return P if tile < TILES else NEW


class Memory:

    BASE = 16512

    def __init__(self, nc):
        self.nc = nc

    def at(self, name, offset, shape, dtype=F32):
        return self.nc.alloc_sbuf_tensor_at(name, shape, dtype, offset=self.BASE + offset)


def hybrid_stream_step(nc, a):
    mem = Memory(nc)
    m = {}
    m["qT"] = mem.at("sb_qT", 66560, [P, 4, TOKENS])
    m["kT"] = mem.at("sb_kT", 83456, [P, 4, KEYS])
    m["v"] = mem.at("sb_v", 104448, [P, 11, SBW])
    m["oaT"] = mem.at("sb_outT", 142336, [P, 4, TOKENS])
    m["obT"] = mem.at("mla_outT", 159232, [P, 4, TOKENS])
    m["craw"] = mem.at("latents_raw", 176128, [P, QC + VC, TOKENS])
    m["kpeT"] = mem.at("kpeT", 197248, [P, KEYS])
    m["cos"] = mem.at("cosT", 202496, [P, TOKENS])
    m["sin"] = mem.at("sinT", 206720, [P, TOKENS])
    m["ident"] = mem.at("identity", 210944, [P, P])
    m["negtri"] = mem.at("minus_triangle", 211456, [P, P])
    m["negones"] = mem.at("minus_ones", 211968, [P, P])
    m["eps"] = mem.at("epsilon", 212480, [P, 1])
    m["mqT"] = mem.at("mla_qT", 0, [P, HEADS, TOKENS])
    m["mkT"] = mem.at("mla_kT", 33792, [P, HEADS, KEYS])
    m["mv"] = mem.at("mla_v", 75776, [P, 11, SBW])
    m["mergedT"] = mem.at("mergedT", 107520, [P, KC, TOKENS])
    m["hT"] = mem.at("hT", 0, [P, KC, TOKENS])
    m["h"] = mem.at("h", 33792, [P, TILES + 1, D])
    m["idx_all"] = mem.at("gathered_index", 203776, [P, HEADS, GATHER - EARLY, TOPK], U32)
    m["gate_all"] = mem.at("gathered_gate", 204800, [P, HEADS, GATHER - EARLY, TOPK])
    m["acc"] = mem.at("ff_sum", 70656, [P, TILES + 1, D])
    m["w_oa"] = mem.at("w_oa", 176128, [P, 4, D])
    m["w_ob"] = mem.at("w_ob", 192512, [P, 4, D])
    m["w_out"] = mem.at("w_out", 70656, [P, KC, D])
    m["ln1_g"] = mem.at("ln1_g", 103424, [P, D])
    project(nc, mem, a, m)
    stick_attend(nc, mem, m)
    mla_project(nc, mem, a, m)
    mla_attend(nc, mem, a, m)
    merge(nc, mem, a, m)
    first_norm(nc, mem, a, m)
    route_experts(nc, mem, a, m)
    with ExitStack() as s:
        norm = LastNorm(nc, mem, s, m)
        apply_experts(nc, mem, a, m, norm)
        last_norm(nc, mem, a, m, norm)


def sems(nc, stack, *names):
    return [stack.enter_context(nc.semaphore(n)) for n in names]


def banks(nc, stack, name, n):
    return [stack.enter_context(nc.psum_tensor(f"{name}{i}", [P, 512], F32)) for i in range(n)]


def project(nc, mem, a, m):
    with ExitStack() as s:
        xT = mem.at("xT", 0, [P, KC, TOKENS])
        w = [mem.at(f"w_in_block{i}", 33792 + 16384 * i, [P, KC, 512]) for i in range(2)]
        gate = [mem.at(f"gate_stage{i}", 126976 + 1408 * i, [P, SPAN]) for i in range(4)]
        turned = [mem.at(f"rope_part{i}", 132608 + 1408 * i, [P, SPAN]) for i in range(2)]
        zero = mem.at("zeros", 135424, [P, 1024])
        NB = 8
        ps = banks(nc, s, "proj_ps", NB)
        c0 = 3 * SBW
        blocks = [(0, SBW, "q"), (SBW, SBW, "k"), (2 * SBW, SBW, "v"), (c0, QL, "c"),
                  (c0 + QL, KVL + RD, "ckr"), *[(c0 + QL + KVL + RD + 512 * i, 512, "g") for i in range(4)]]
        plan = []
        for b, (_, width, kind) in enumerate(blocks):
            if kind == "v":
                plan += [(b, "v", 0, t, 0) for t in range(TILES + 1)]
                continue
            for j in range(width // P):
                plan += [(b, kind[0], P * j, {"c": j + QC * (kind == "ckr")}.get(kind[0], j), c) for c in range(SPANS)]
            if kind == "ckr":
                plan += [(b, r, KVL + (0 if r == "r" else RD), 0, c) for c in range(SPANS) for r in "rs"]
        on_act = [kind == "g" for _, kind, *_ in plan]
        freed_by = [sum(1 for k in range(n + 1) if on_act[k] == on_act[n]) for n in range(len(plan))]

        fixed_in, filled, copied, squashed, sine_done, out_done, made, zeroed, zero_done = sems(
            nc, s, "fixed_in", "p_filled", "p_copied", "p_squashed", "sine_part_done", "p_out", "const_made", "zeros_set", "dense_gates_zeroed")
        w_in = sems(nc, s, "w_in_a", "w_in_b")
        x_in = sems(nc, s, *[f"x_in{c}" for c in range(SPANS)])
        first_w_in = sems(nc, s, "first_w_in", "rest_of_first_w_in")
        gate_out = sems(nc, s, *[f"gate_out{i}" for i in range(4)])
        last_of = {b: max(n for n, e in enumerate(plan) if e[0] == b) for b in range(len(blocks))}
        block = s.enter_context(nc.Block())

        @block.sync
        def _(sp):
            for b, (col, width, kind) in enumerate(blocks):
                if b >= 2:
                    sp.wait_ge(filled, last_of[b - 2] + 1)
                w_rows = a["w_in"].rearrange("(k p) c -> p k c", p=P)
                if b == 0:
                    for x in range(width // P):
                        sp.dma_start(w[0][:, :, P * x:P * (x + 1)], w_rows[:, :, P * x:P * (x + 1)]).then_inc(first_w_in[x > 0], 16)
                        if x < SPANS:
                            sp.dma_start(xT[:, :, SPAN * x:SPAN * (x + 1)],
                                         a["xT"].rearrange("(k p) t -> p k t", p=P)[:, :, SPAN * x:SPAN * (x + 1)]).then_inc(x_in[x], 16)
                    continue
                sp.dma_start(w[b % 2][:, :, 0:width], w_rows[:, :, col:col + width]).then_inc(w_in[b % 2], 16)
                if kind == "ckr":
                    sp.dma_start(w[b % 2][:, :, width:width + RD],
                                 a["w_kr_swapped"].rearrange("(k p) c -> p k c", p=P)).then_inc(w_in[b % 2], 16)
                if b == 1:
                    sp.dma_start(m["kT"][:, :, TOKENS:KEYS],
                                 a["past_sb_kT"].rearrange("(k p) t -> p k t", p=P)).then_inc(fixed_in, 16)
                    sp.dma_start(m["v"][:, TILES + 1:TILES + 3, :],
                                 a["past_sb_v"].rearrange("(k p) c -> p k c", p=P)).then_inc(fixed_in, 16)
                    sp.dma_start(m["kpeT"][HD:MD, TOKENS:KEYS], a["past_kpeT"]).then_inc(fixed_in, 16)
                    sp.dma_start(m["cos"][HD:MD, :], a["cosT"]).then_inc(fixed_in, 16)
                    sp.dma_start(m["sin"][HD:MD, :], a["sinT"]).then_inc(fixed_in, 16)
            copies = lambda b: sum(1 for n in range(last_of[b] + 1) if not on_act[n])
            sp.wait_ge(copied, copies(1))
            sp.dma_start(a["out_kT"].rearrange("(k p) t -> p k t", p=P), m["kT"][:, :, 0:TOKENS]).then_inc(out_done, 16)
            sp.wait_ge(copied, copies(2))
            sp.dma_start(a["out_v"][0:SEQ, :].rearrange("(k p) c -> p k c", p=P), m["v"][:, 0:TILES, :]).then_inc(out_done, 16)
            sp.dma_start(a["out_v"][SEQ:TOKENS, :], m["v"][0:NEW, TILES, :]).then_inc(out_done, 16)
            sp.wait_ge(copied, sum(1 for x in on_act if not x))
            sp.dma_start(a["out_kpeT"], m["kpeT"][HD:MD, 0:TOKENS]).then_inc(out_done, 16)
            for i in range(4):
                sp.wait_ge(gate_out[i], 4 * sum(on_act))
            sp.wait_ge(out_done, 64)
            sp.wait_ge(fixed_in, 80)

        @block.gpsimd
        def _(pool):
            pool.memset(zero[:], 0.0).then_inc(zeroed, 1)
            pool.memset(m["ident"][:], 0.0).then_inc(made, 1)
            pool.memset(m["negtri"][:], -1.0).then_inc(made, 1)
            pool.memset(m["negones"][:], -1.0).then_inc(made, 1)
            pool.memset(m["eps"][:], EPS).then_inc(made, 1)
            pool.wait_ge(made, 4)
            pool.affine_select(out=m["ident"][:], in_=m["ident"][:], compare_op=ALU.not_equal, fill=1.0, base=0,
                               pattern=[[-1, P]], channel_multiplier=1).then_inc(made, 1)
            pool.affine_select(out=m["negtri"][:], in_=m["negtri"][:], compare_op=ALU.is_ge, fill=0.0, base=0,
                               pattern=[[-1, P]], channel_multiplier=1).then_inc(made, 1)
            pool.wait_ge(made, 6)
            pool.wait_ge(zeroed, 1)
            FILLS = EXPERTS * P * DENSE // (P * 4096)
            cells = a["gates_by_expert"].rearrange("(n p r c) o -> n p r (c o)", p=P, r=4, c=1024)
            for n in range(FILLS):
                pool.wait_ge(filled, len(plan) * (n + 1) // (FILLS + 1))
                pool.dma_start(cells[n], zero[:].unsqueeze(1).broadcast_to([P, 4, 1024])).then_inc(zero_done, 16)
            pool.wait_ge(zero_done, 16 * FILLS)

        @block.tensor
        def _(pe):
            seen = 0
            for n, (b, kind, col, j, c) in enumerate(plan):
                if b != seen:
                    seen = b
                    pe.wait_ge(w_in[b % 2], 16 * ((b + 1) // 2 + (b % 2 == 0 and b >= 4)))
                if n < SPANS:
                    pe.wait_ge(first_w_in[0], 16)
                    pe.wait_ge(x_in[c], 16)
                elif n == SPANS:
                    pe.wait_ge(first_w_in[1], 16 * (SBW // P - 1))
                if n >= NB:
                    k = n - NB
                    pe.wait_ge(squashed if on_act[k] else copied, freed_by[k])
                out = ps[n % NB]
                for k in range(KC):
                    if kind == "v":
                        r = rows_of(j)
                        mm = nc.tensor.matmul(out[0:r, :], xT[:, k, P * j:P * j + r], w[b % 2][:, k, :],
                                              start=(k == 0), stop=(k == KC - 1))
                    elif kind in "rs":
                        mm = nc.tensor.matmul(out[HD:MD, 0:SPAN], w[b % 2][:, k, col:col + RD],
                                              xT[:, k, SPAN * c:SPAN * (c + 1)], start=(k == 0), stop=(k == KC - 1))
                    else:
                        mm = nc.tensor.matmul(out[:, 0:SPAN], w[b % 2][:, k, col:col + P],
                                              xT[:, k, SPAN * c:SPAN * (c + 1)], start=(k == 0), stop=(k == KC - 1))
                mm.then_inc(filled, 1)

        @block.vector
        def _(dve):
            dve.wait_ge(fixed_in, 80)
            done = 0
            for n, (b, kind, col, j, c) in enumerate(plan):
                if kind == "g":
                    continue
                dve.wait_ge(filled, n + 1)
                cols = slice(SPAN * c, SPAN * (c + 1))
                src = ps[n % NB]
                if kind == "q":
                    nc.vector.tensor_scalar(m["qT"][:, j, cols], src[:, 0:SPAN], float(HD) ** -0.5, None, ALU.mult).then_inc(copied, 1)
                elif kind == "k":
                    nc.vector.tensor_copy(m["kT"][:, j, cols], src[:, 0:SPAN]).then_inc(copied, 1)
                elif kind == "v":
                    r = rows_of(j)
                    nc.vector.tensor_copy(m["v"][0:r, j, :], src[0:r, :]).then_inc(copied, 1)
                elif kind == "c":
                    nc.vector.tensor_copy(m["craw"][:, j, cols], src[:, 0:SPAN]).then_inc(copied, 1)
                elif kind == "r":
                    if done >= 2:
                        dve.wait_ge(copied, done)
                    nc.vector.tensor_tensor(turned[0][HD:MD, :], src[HD:MD, 0:SPAN], m["cos"][HD:MD, cols], ALU.mult).then_inc(copied, 1)
                else:
                    dve.wait_ge(copied, done)
                    nc.vector.tensor_tensor(turned[1][HD:MD, :], src[HD:MD, 0:SPAN], m["sin"][HD:MD, cols], ALU.mult).then_inc(sine_done, 1)
                    dve.wait_ge(sine_done, c + 1)
                    nc.vector.tensor_tensor(m["kpeT"][HD:MD, cols], turned[0][HD:MD, :], turned[1][HD:MD, :], ALU.add).then_inc(copied, 1)
                done += 1

        @block.scalar
        def _(act):
            n = 0
            for e, (b, kind, col, j, c) in enumerate(plan):
                if kind != "g":
                    continue
                act.wait_ge(filled, e + 1)
                if n >= 4:
                    act.wait_ge(gate_out[n % 4], 16 * (n // 4))
                nc.scalar.activation(gate[n % 4][:], ps[e % NB][:, 0:SPAN], ACT.Sigmoid).then_inc(squashed, 1)
                act.wait_ge(squashed, n + 1)
                row = 512 * (b - 5) + P * j
                act.dma_start(a["gatesT"][row:row + P, SPAN * c:SPAN * (c + 1)], gate[n % 4][:]).then_inc(gate_out[n % 4], 16)
                n += 1


def stick_attend(nc, mem, m):
    with ExitStack() as s:
        items = []
        for i in range(TILES + 1):
            nq = rows_of(i)
            tiles = [(P * j, P, j, j == i) for j in range(i, -1, -1)] if i < TILES else \
                    [(SEQ, NEW, TILES, True), (TOKENS + P, P, TILES + 2, False), (TOKENS, P, TILES + 1, False)]
            for x, (key, rows, vt, diag) in enumerate(tiles):
                for par in range(2):
                    items.append((i, nq, key, rows, vt, diag, par, x == len(tiles) - 1))
        N = len(items)
        LATE = 3
        E, S, R, A = 4, 6, 8, 4
        e = [mem.at(f"abs_exp_ln{i}", 2048 * i, [P, 512]) for i in range(E)]
        sp_ = [mem.at(f"softplus{i}", 2048 * (E + i), [P, 512]) for i in range(S)]
        rest = [mem.at(f"later_sum{i}", 2048 * (E + S + i), [P, 512]) for i in range(R)]
        w = [mem.at(f"weights{i}", 2048 * (E + S + R + i), [P, 512]) for i in range(A)]
        before = mem.at("earlier_mask", 45056, [P, P])
        far = mem.at("far_mask", 45568, [P, P])
        Z = 6
        zb = banks(nc, s, "log_weight_ps", Z)
        ob = banks(nc, s, "stick_out_ps", 2)
        masks, z_done, abs_done, exp_done, ln_done, sp_done, sp_masked, rest_done, zeroed, s_done, w_done, av_done, o_done, o_copied = sems(
            nc, s, "masks", "z_done", "abs_done", "exp_neg_abs_done", "ln_done", "sp_done", "sp_masked", "rest_done", "rest_zeroed",
            "log_weight_done", "weight_done", "av_done", "stick_o_done", "stick_o_copied")
        block = s.enter_context(nc.Block())
        diag_upto = lambda n: sum(1 for k in range(n + 1) if items[k][5])
        rest_upto = lambda n: sum(1 for k in range(n + 1) if not items[k][7])

        def scores(bank, n):
            i, nq, key, rows, vt, diag, par, last = items[n]
            for x in range(4):
                mm = nc.tensor.matmul(bank[0:rows, nq * x:nq * (x + 1)], m["kT"][HD * par:HD * par + HD, x, key:key + rows],
                                      m["qT"][HD * par:HD * par + HD, x, P * i:P * i + nq], start=(x == 0),
                                      stop=(x == 3), skip_group_check=True)
            return mm

        @block.gpsimd
        def _(pool):
            pool.memset(before[:], 1.0).then_inc(masks, 1)
            pool.memset(far[:], 0.0).then_inc(masks, 1)
            pool.wait_ge(masks, 2)
            pool.affine_select(out=before[:], in_=before[:], compare_op=ALU.is_gt, fill=0.0, base=0,
                               pattern=[[1, P]], channel_multiplier=-1).then_inc(masks, 1)
            pool.affine_select(out=far[:], in_=far[:], compare_op=ALU.is_gt, fill=FAR, base=0,
                               pattern=[[1, P]], channel_multiplier=-1).then_inc(masks, 1)

        @block.tensor
        def _(pe):
            pe.wait_ge(masks, 4)
            for t in range(N + LATE + 2):
                if t < N:
                    if t >= Z:
                        pe.wait_ge(w_done, t - Z + 1)
                    scores(zb[t % Z], t).then_inc(z_done, 1)
                n = t - LATE
                if 0 <= n < N:
                    i, nq, key, rows, vt, diag, par, last = items[n]
                    cols = slice(0, 4 * nq)
                    pe.wait_ge(sp_done, n + 1)
                    if diag:
                        for x in range(4):
                            nc.tensor.matmul(zb[n % Z][0:rows, nq * x:nq * (x + 1)], m["ident"][0:rows, 0:rows], far[0:rows, 0:nq],
                                             start=False, stop=False, skip_group_check=True)
                        pe.wait_ge(sp_masked, diag_upto(n))
                    else:
                        kr = items[n - 2][3]
                        pe.wait_ge(rest_done, rest_upto(n - 2))
                        nc.tensor.matmul(zb[n % Z][0:rows, cols], m["negones"][0:P, 0:rows], rest[(n - 2) % R][:, cols],
                                         start=False, stop=False, skip_group_check=True)
                    nc.tensor.matmul(zb[n % Z][0:rows, cols], m["negtri"][0:rows, 0:rows], sp_[n % S][0:rows, cols],
                                     start=False, stop=True, skip_group_check=True).then_inc(s_done, 1)
                n = t - LATE - 2
                if 0 <= n < N:
                    i, nq, key, rows, vt, diag, par, last = items[n]
                    pe.wait_ge(w_done, n + 1)
                    if diag and i >= 1:
                        pe.wait_ge(o_copied, 2 * (i - 1) + par + 1)
                    for x in range(4):
                        h = 2 * x + par
                        mm = nc.tensor.matmul(ob[par][HD * par:HD * par + HD, nq * x:nq * (x + 1)], m["v"][0:rows, vt, HD * h:HD * (h + 1)],
                                              w[n % A][0:rows, nq * x:nq * (x + 1)], start=(diag and x == 0), stop=last,
                                              skip_group_check=True)
                    mm.then_inc(av_done, 1)

        @block.scalar
        def _(act):
            def of(n):
                return slice(0, items[n][3]), slice(0, 4 * items[n][1])

            for t in range(0, N + LATE, 2):
                pair = [n for n in (t, t + 1) if n < N]
                for n in pair:
                    buf = e[n % E][of(n)]
                    act.wait_ge(z_done, n + 1)
                    if n >= E:
                        act.wait_ge(sp_done, n - E + 1)
                    nc.scalar.activation(buf, zb[n % Z][of(n)], ACT.Abs).then_inc(abs_done, 1)
                for n in pair:
                    buf = e[n % E][of(n)]
                    act.wait_ge(abs_done, n + 1)
                    nc.scalar.activation(buf, buf, ACT.Exp, scale=-1.0).then_inc(exp_done, 1)
                for n in (t - LATE, t - LATE + 1):
                    if not 0 <= n < N:
                        continue
                    act.wait_ge(s_done, n + 1)
                    if n >= A:
                        act.wait_ge(av_done, n - A + 1)
                    nc.scalar.activation(w[n % A][of(n)], zb[n % Z][of(n)], ACT.Exp).then_inc(w_done, 1)
                for n in pair:
                    buf = e[n % E][of(n)]
                    act.wait_ge(exp_done, n + 1)
                    nc.scalar.activation(buf, buf, ACT.Ln, bias=1.0).then_inc(ln_done, 1)

        @block.vector
        def _(dve):
            dve.wait_ge(masks, 4)
            ends = [n for n in range(N) if items[n][7]]
            zeros = 0
            for t in range(N + LATE + 3):
                n = t - LATE - 3
                if n in ends:
                    i, nq, key, rows, vt, diag, par, last = items[n]
                    dve.wait_ge(av_done, n + 1)
                    nc.vector.tensor_copy(m["oaT"][HD * par:HD * par + HD, :, P * i:P * i + nq],
                                          ob[par][HD * par:HD * par + HD, 0:4 * nq].rearrange("p (x q) -> p x q", x=4)).then_inc(o_copied, 1)
                if t < N:
                    i, nq, key, rows, vt, diag, par, last = items[t]
                    cols = slice(0, 4 * nq)
                    dve.wait_ge(ln_done, t + 1)
                    if t >= S:
                        dve.wait_ge(s_done, t - S + 1)
                    own = sp_[t % S][0:rows, cols]
                    nc.vector.scalar_tensor_tensor(own, zb[t % Z][0:rows, cols], 0.0, e[t % E][0:rows, cols],
                                                   ALU.max, ALU.add).then_inc(sp_done, 1)
                    dve.wait_ge(sp_done, t + 1)
                    if diag:
                        v3 = own.rearrange("p (x q) -> p x q", x=4)
                        nc.vector.tensor_tensor(v3, v3, before[0:rows, 0:nq].unsqueeze(1).broadcast_to([rows, 4, nq]), ALU.mult).then_inc(sp_masked, 1)
                        dve.wait_ge(sp_masked, diag_upto(t))
                    if not last:
                        out = rest[t % R]
                        if rows < P:
                            nc.vector.memset(out[:, cols], 0.0).then_inc(zeroed, 1)
                            zeros += 1
                            dve.wait_ge(zeroed, zeros)
                        if diag:
                            nc.vector.tensor_copy(out[0:rows, cols], own).then_inc(rest_done, 1)
                        else:
                            dve.wait_ge(rest_done, rest_upto(t - 2))
                            nc.vector.tensor_tensor(out[:, cols], own, rest[(t - 2) % R][:, cols], ALU.add).then_inc(rest_done, 1)


def mla_project(nc, mem, a, m):
    with ExitStack() as s:
        cqT = mem.at("query_latentT", 98304, [P, QC, TOKENS])
        ckvT = mem.at("kv_latentT", 110976, [P, VC, KEYS])
        w_uq = mem.at("w_uq", 121472, [P, QC, HEADS * MD])
        w_uqs = mem.at("w_uq_swapped", 130688, [P, QC, HEADS * RD])
        w_uk = mem.at("w_uk", 133760, [P, VC, SBW])
        w_uv = mem.at("w_uv", 137856, [P, VC, SBW])
        g = mem.at("norm_gains", 141952, [P, QC + VC])
        sq = [mem.at(f"squares{i}", 159232 + 1408 * i, [P, SPAN]) for i in range(3)]
        root = [mem.at(f"roots{i}", 163456 + 1408 * i, [P, SPAN]) for i in range(2)]
        inv = [mem.at(f"inverse_roots{i}", 166272 + 1408 * i, [P, SPAN]) for i in range(2)]
        part = [mem.at(f"rope_q{i}", 169088 + 1408 * i, [P, SPAN]) for i in range(2)]
        ss = banks(nc, s, "square_sum_ps", 2)
        NB = 6
        ps = banks(nc, s, "mla_ps", NB)
        w_in, past_in, g_in, sq_done, ss_done, root_done, inv_done, normed, filled, copied, roped, kpe_in, out_done = sems(
            nc, s, "uw_in", "past_in", "gain_in", "sq_done", "ss_done", "root_done", "inv_done", "normed",
            "m_filled", "m_copied", "m_roped", "m_kpe", "m_out")
        norms = [(c, lat) for c in range(SPANS) for lat in range(2)]
        chunks = lambda lat: range(QC) if lat == 0 else range(QC, QC + VC)
        plan = []
        for c in range(SPANS):
            for h in range(HEADS):
                plan += [("q", h, c, 0), ("s", h, c, 0)]
        key_spans = [(c * SPAN, SPAN) for c in range(SPANS)] + [(TOKENS, PAST)]
        for c, width in key_spans:
            plan += [("k", h, c, width) for h in range(HEADS)]
        plan += [("v", t, 0, 0) for t in range(TILES + 3)]
        on_act = [e[0] in "kv" for e in plan]
        freed_by = [sum(1 for k in range(n + 1) if on_act[k] == on_act[n]) for n in range(len(plan))]
        squares = [(k, nn) for k, (c, lat) in enumerate(norms) for nn in chunks(lat)]
        block = s.enter_context(nc.Block())

        @block.sync
        def _(sp):
            sp.dma_start(g[:], a["norm_gains"]).then_inc(g_in, 16)
            sp.dma_start(w_uq[:], a["w_uq"].rearrange("(k p) c -> p k c", p=P)).then_inc(w_in, 16)
            sp.dma_start(w_uqs[:], a["w_uq_swapped"].rearrange("(k p) c -> p k c", p=P)).then_inc(w_in, 16)
            sp.dma_start(w_uk[:], a["w_uk"].rearrange("(k p) c -> p k c", p=P)).then_inc(w_in, 16)
            sp.dma_start(w_uv[:], a["w_uv"].rearrange("(k p) c -> p k c", p=P)).then_inc(w_in, 16)
            sp.dma_start(ckvT[:, :, TOKENS:KEYS], a["past_ckvT"].rearrange("(k p) t -> p k t", p=P)).then_inc(past_in, 16)
            sp.wait_ge(normed, len(squares))
            sp.dma_start(a["out_ckvT"].rearrange("(k p) t -> p k t", p=P), ckvT[:, :, 0:TOKENS]).then_inc(out_done, 16)
            sp.wait_ge(out_done, 16)

        @block.gpsimd
        def _(pool):
            for h in range(HEADS):
                pool.tensor_copy(m["mkT"][HD:MD, h, :], m["kpeT"][HD:MD, :]).then_inc(kpe_in, 1)
            pool.wait_ge(kpe_in, HEADS)

        @block.tensor
        def _(pe):
            for k, (c, lat) in enumerate(norms):
                if k >= 2:
                    pe.wait_ge(root_done, k - 1)
                for nn in chunks(lat):
                    at = squares.index((k, nn))
                    pe.wait_ge(sq_done, at + 1)
                    mm = nc.tensor.matmul(ss[k % 2][:, 0:SPAN], m["negones"][:], sq[at % 3][:],
                                          start=(nn == chunks(lat)[0]), stop=(nn == chunks(lat)[-1]))
                    mm.then_inc(ss_done, 1)
            pe.wait_ge(w_in, 64)
            pe.wait_ge(past_in, 16)
            pe.wait_ge(normed, len(squares))
            for n, (kind, j, c, width) in enumerate(plan):
                if n >= NB:
                    k = n - NB
                    pe.wait_ge(copied if on_act[k] else roped, freed_by[k])
                out = ps[n % NB]
                cols = slice(SPAN * c, SPAN * (c + 1))
                if kind in "qs":
                    for k in range(QC):
                        if kind == "q":
                            mm = nc.tensor.matmul(out[0:MD, 0:SPAN], w_uq[:, k, MD * j:MD * (j + 1)], cqT[:, k, cols],
                                                  start=(k == 0), stop=(k == QC - 1))
                        else:
                            mm = nc.tensor.matmul(out[HD:MD, 0:SPAN], w_uqs[:, k, RD * j:RD * (j + 1)], cqT[:, k, cols],
                                                  start=(k == 0), stop=(k == QC - 1))
                else:
                    for k in range(VC):
                        if kind == "k":
                            mm = nc.tensor.matmul(out[0:HD, 0:width], w_uk[:, k, HD * j:HD * (j + 1)], ckvT[:, k, c:c + width],
                                                  start=(k == 0), stop=(k == VC - 1))
                        else:
                            r = NEW if j == TILES else P
                            first = P * j if j <= TILES else TOKENS + P * (j - TILES - 1)
                            mm = nc.tensor.matmul(out[0:r, :], ckvT[:, k, first:first + r], w_uv[:, k, :],
                                                  start=(k == 0), stop=(k == VC - 1))
                mm.then_inc(filled, 1)

        @block.scalar
        def _(act):
            at = 0
            for k, (c, lat) in enumerate(norms):
                for nn in chunks(lat):
                    if at >= 3:
                        act.wait_ge(ss_done, at - 2)
                    nc.scalar.activation(sq[at % 3][:], m["craw"][:, nn, SPAN * c:SPAN * (c + 1)], ACT.Square).then_inc(sq_done, 1)
                    at += 1
                act.wait_ge(ss_done, at)
                if k >= 2:
                    act.wait_ge(inv_done, k - 1)
                nc.scalar.activation(root[k % 2][:], ss[k % 2][:, 0:SPAN], ACT.Sqrt, bias=m["eps"][:],
                                     scale=-1.0 / (QL if lat == 0 else KVL)).then_inc(root_done, 1)
            for n, (kind, j, c, width) in enumerate(plan):
                if not on_act[n]:
                    continue
                act.wait_ge(filled, n + 1)
                if kind == "k":
                    nc.scalar.copy(m["mkT"][0:HD, j, c:c + width], ps[n % NB][0:HD, 0:width]).then_inc(copied, 1)
                else:
                    r = NEW if j == TILES else P
                    nc.scalar.copy(m["mv"][0:r, j, :], ps[n % NB][0:r, :]).then_inc(copied, 1)

        @block.vector
        def _(dve):
            dve.wait_ge(g_in, 16)
            done = 0
            for k, (c, lat) in enumerate(norms):
                cols = slice(SPAN * c, SPAN * (c + 1))
                dve.wait_ge(root_done, k + 1)
                if k >= 2:
                    dve.wait_ge(normed, done)
                nc.vector.reciprocal(inv[k % 2][:], root[k % 2][:]).then_inc(inv_done, 1)
                dve.wait_ge(inv_done, k + 1)
                for nn in chunks(lat):
                    out = cqT[:, nn, cols] if lat == 0 else ckvT[:, nn - QC, cols]
                    nc.vector.scalar_tensor_tensor(out, m["craw"][:, nn, cols], g[:, nn:nn + 1], inv[k % 2][:],
                                                   ALU.mult, ALU.mult).then_inc(normed, 1)
                    done += 1
            pairs = 0
            for n, (kind, h, c, width) in enumerate(plan):
                if kind != "q":
                    continue
                cols = slice(SPAN * c, SPAN * (c + 1))
                dve.wait_ge(filled, n + 2)
                src, swp = ps[n % NB], ps[(n + 1) % NB]
                nc.vector.tensor_tensor(part[0][HD:MD, :], src[HD:MD, 0:SPAN], m["cos"][HD:MD, cols], ALU.mult).then_inc(inv_done, 1)
                nc.vector.tensor_tensor(part[1][HD:MD, :], swp[HD:MD, 0:SPAN], m["sin"][HD:MD, cols], ALU.mult).then_inc(inv_done, 1)
                nc.vector.tensor_copy(m["mqT"][0:HD, h, cols], src[0:HD, 0:SPAN]).then_inc(roped, 1)
                pairs += 1
                dve.wait_ge(inv_done, len(norms) + 2 * pairs)
                nc.vector.tensor_tensor(m["mqT"][HD:MD, h, cols], part[0][HD:MD, :], part[1][HD:MD, :], ALU.add).then_inc(roped, 1)
                dve.wait_ge(roped, 2 * pairs)


def mla_attend(nc, mem, a, m):
    with ExitStack() as s:
        items = [(i, h) for i in range(TILES + 1) for h in range(HEADS)]
        N = len(items)

        def keys_of(i):
            if i < TILES:
                return 0, P * (i + 1), [(P * j, P, j) for j in range(i + 1)]
            return SEQ, NEW + PAST, [(0, NEW, TILES), (NEW, P, TILES + 1), (NEW + P, P, TILES + 2)]

        p = [mem.at(f"probs{i}", 98304 + 4096 * i, [P, 1024]) for i in range(2)]
        pT = [mem.at(f"probsT{i}", 106496 + 4096 * i, [P, 1024]) for i in range(2)]
        on = [mem.at(f"mla_out{i}", 114688 + 2048 * i, [P, SBW]) for i in range(2)]
        mx = mem.at("row_max", 118784, [P, N])
        nm = mem.at("minus_max", 119168, [P, N])
        rs = mem.at("row_sum", 119552, [P, N])
        ri = mem.at("inverse_sum", 119936, [P, N])
        sp = [s.enter_context(nc.psum_tensor(f"score_ps{i}", [P, 1024], F32)) for i in range(2)]
        tp = s.enter_context(nc.psum_tensor("probsT_ps", [P, 1024], F32))
        op = s.enter_context(nc.psum_tensor("mla_out_ps", [P, 512], F32))
        oT = s.enter_context(nc.psum_tensor("mla_outT_ps", [P, 512], F32))
        s_done, masked, max_done, nm_done, p_done, t_done, t_copied, av_done, inv_done, on_done, oT_done, oT_copied, wo_in = sems(
            nc, s, "ms_done", "ms_masked", "max_done", "nm_done", "p_done", "t_done", "t_copied", "m_av_done",
            "m_inv", "on_done", "oT_done", "oT_copied", "wo_in")
        block = s.enter_context(nc.Block())

        @block.sync
        def _(sp):
            sp.dma_start(m["w_oa"][:], a["w_oa"].rearrange("(k p) c -> p k c", p=P)).then_inc(wo_in, 16)
            sp.dma_start(m["w_ob"][:], a["w_ob"].rearrange("(k p) c -> p k c", p=P)).then_inc(wo_in, 16)
            sp.wait_ge(wo_in, 32)

        @block.tensor
        def _(pe):
            for t in range(N + 3):
                if t < N:
                    i, h = items[t]
                    r = rows_of(i)
                    first, nk, _ = keys_of(i)
                    if t >= 2:
                        pe.wait_ge(p_done, t - 1)
                    for c in range(0, nk, 512):
                        w = min(512, nk - c)
                        mm = nc.tensor.matmul(sp[t % 2][0:r, c:c + w], m["mqT"][0:MD, h, P * i:P * i + r],
                                              m["mkT"][0:MD, h, first + c:first + c + w], start=True, stop=True)
                    mm.then_inc(s_done, 1)
                n = t - 1
                if 0 <= n < N:
                    i, h = items[n]
                    r = rows_of(i)
                    pe.wait_ge(p_done, n + 1)
                    if n >= 1:
                        pe.wait_ge(t_copied, n)
                    for x, (off, rows, vt) in enumerate(keys_of(i)[2]):
                        mm = nc.tensor.transpose(tp[0:rows, P * x:P * x + r], p[n % 2][0:r, off:off + rows], m["ident"][0:r, 0:r])
                    mm.then_inc(t_done, 1)
                n = t - 2
                if 0 <= n < N:
                    i, h = items[n]
                    r = rows_of(i)
                    pe.wait_ge(t_copied, n + 1)
                    if h == 0 and i >= 1:
                        pe.wait_ge(on_done, i)
                    tiles = keys_of(i)[2]
                    for x, (off, rows, vt) in enumerate(tiles):
                        mm = nc.tensor.matmul(op[0:r, HD * h:HD * (h + 1)], pT[n % 2][0:rows, P * x:P * x + r],
                                              m["mv"][0:rows, vt, HD * h:HD * (h + 1)], start=(x == 0), stop=(x == len(tiles) - 1),
                                              skip_group_check=True)
                    mm.then_inc(av_done, 1)
                n = t - 3
                if 0 <= n < N and items[n][1] == HEADS - 1:
                    i = items[n][0]
                    r = rows_of(i)
                    pe.wait_ge(on_done, i + 1)
                    if i >= 1:
                        pe.wait_ge(oT_copied, i)
                    for x in range(4):
                        mm = nc.tensor.transpose(oT[:, P * x:P * x + r], on[i % 2][0:r, P * x:P * (x + 1)], m["ident"][0:r, 0:r])
                    mm.then_inc(oT_done, 1)

        @block.scalar
        def _(act):
            for n, (i, h) in enumerate(items):
                r = rows_of(i)
                nk = keys_of(i)[1]
                act.wait_ge(nm_done, n + 1)
                if n >= 2:
                    act.wait_ge(t_done, n - 1)
                nc.scalar.activation(p[n % 2][0:r, 0:nk], sp[n % 2][0:r, 0:nk], ACT.Exp, bias=nm[0:r, n:n + 1],
                                     scale=MLA_SCALE, accum_out=rs[0:r, n:n + 1]).then_inc(p_done, 1)

        @block.vector
        def _(dve):
            for t in range(N + 3):
                if t < N:
                    i, h = items[t]
                    r = rows_of(i)
                    nk = keys_of(i)[1]
                    dve.wait_ge(s_done, t + 1)
                    if i < TILES:
                        nc.vector.memset(sp[t % 2][0:CHUNK, nk - CHUNK:nk], FAR).then_inc(masked, 1)
                        dve.wait_ge(masked, t + 1)
                    nc.vector.reduce_max(mx[0:r, t:t + 1], sp[t % 2][0:r, 0:nk], AX).then_inc(max_done, 1)
                    dve.wait_ge(max_done, t + 1)
                    nc.vector.tensor_scalar(nm[0:r, t:t + 1], mx[0:r, t:t + 1], -MLA_SCALE, None, ALU.mult).then_inc(nm_done, 1)
                n = t - 1
                if 0 <= n < N:
                    i, h = items[n]
                    r = rows_of(i)
                    tiles = keys_of(i)[2]
                    dve.wait_ge(t_done, n + 1)
                    if n >= 2:
                        dve.wait_ge(av_done, n - 1)
                    if i < TILES:
                        nc.vector.tensor_copy(pT[n % 2][:, 0:P * len(tiles)], tp[:, 0:P * len(tiles)]).then_inc(t_copied, 1)
                    else:
                        nc.vector.tensor_copy(pT[n % 2][0:NEW, 0:r], tp[0:NEW, 0:r]).then_inc(masked, 1)
                        for x in (1, 2):
                            ins = nc.vector.tensor_copy(pT[n % 2][:, P * x:P * x + r], tp[:, P * x:P * x + r])
                            ins.then_inc(t_copied if x == 2 else masked, 1)
                n = t - 2
                if 0 <= n < N and items[n][1] == HEADS - 1:
                    i = items[n][0]
                    r = rows_of(i)
                    dve.wait_ge(av_done, n + 1)
                    dve.wait_ge(p_done, n + 1)
                    at = slice(HEADS * i, HEADS * (i + 1))
                    nc.vector.reciprocal(ri[0:r, at], rs[0:r, at]).then_inc(inv_done, 1)
                    dve.wait_ge(inv_done, i + 1)
                    nc.vector.tensor_tensor(on[i % 2][0:r, :].rearrange("p (h d) -> p h d", h=HEADS),
                                            op[0:r, :].rearrange("p (h d) -> p h d", h=HEADS),
                                            ri[0:r, at].unsqueeze(2).broadcast_to([r, HEADS, HD]), ALU.mult).then_inc(on_done, 1)
                n = t - 3
                if 0 <= n < N and items[n][1] == HEADS - 1:
                    i = items[n][0]
                    r = rows_of(i)
                    dve.wait_ge(oT_done, i + 1)
                    nc.vector.tensor_copy(m["obT"][:, :, P * i:P * i + r],
                                          oT[:].rearrange("p (x q) -> p x q", x=4)[:, :, 0:r]).then_inc(oT_copied, 1)


def merge(nc, mem, a, m):
    with ExitStack() as s:
        sig = [mem.at(f"gates{i}", 32768 + 8448 * i, [P, 2, TOKENS]) for i in range(2)]
        part = [mem.at(f"gated{i}", 49664 + 1408 * i, [P, SPAN]) for i in range(4)]
        ps = banks(nc, s, "merge_ps", 8)
        next_in, filled, gated, merged = sems(nc, s, "next_weights_in", "g_filled", "g_gated", "g_merged")
        sig_in = sems(nc, s, "sig_in_a", "sig_in_b")
        plan = [(j, c) for j in range(KC) for c in range(SPANS)]
        block = s.enter_context(nc.Block())

        @block.sync
        def _(sp):
            for j in range(KC):
                if j >= 2:
                    sp.wait_ge(gated, 2 * SPANS * (j - 1))
                sp.dma_start(sig[j % 2][:], a["gatesT"].rearrange("(g k p) t -> k p g t", g=2, p=P)[j]).then_inc(sig_in[j % 2], 16)
                if j == 2:
                    sp.dma_start(m["w_out"][:], a["w_out"].rearrange("(k p) c -> p k c", p=P)).then_inc(next_in, 16)
                    sp.dma_start(m["ln1_g"][:], a["ln1_g"].partition_broadcast(P)).then_inc(next_in, 16)
            sp.wait_ge(next_in, 32)

        @block.tensor
        def _(pe):
            for n, (j, c) in enumerate(plan):
                if n >= 4:
                    pe.wait_ge(gated, 2 * (n - 3))
                for x, (w, o) in enumerate(((m["w_oa"], m["oaT"]), (m["w_ob"], m["obT"]))):
                    for k in range(4):
                        mm = nc.tensor.matmul(ps[2 * (n % 4) + x][:, 0:SPAN], w[:, k, P * j:P * (j + 1)],
                                              o[:, k, SPAN * c:SPAN * (c + 1)], start=(k == 0), stop=(k == 3))
                mm.then_inc(filled, 1)

        @block.vector
        def _(dve):
            for n, (j, c) in enumerate(plan):
                cols = slice(SPAN * c, SPAN * (c + 1))
                if c == 0:
                    dve.wait_ge(sig_in[j % 2], 16 * (j // 2 + 1))
                dve.wait_ge(filled, n + 1)
                if n >= 2:
                    dve.wait_ge(merged, n - 1)
                for x in range(2):
                    nc.vector.tensor_tensor(part[2 * (n % 2) + x][:], ps[2 * (n % 4) + x][:, 0:SPAN], sig[j % 2][:, x, cols],
                                            ALU.mult).then_inc(gated, 1)
                dve.wait_ge(gated, 2 * (n + 1))
                nc.vector.tensor_tensor(m["mergedT"][:, j, cols], part[2 * (n % 2)][:], part[2 * (n % 2) + 1][:],
                                        ALU.add).then_inc(merged, 1)


def first_norm(nc, mem, a, m):
    with ExitStack() as s:
        w_out, g = m["w_out"], m["ln1_g"]
        b = mem.at("ln1_b", 179200, [P, D])
        x = [mem.at(f"x_rows{i}", 183296 + 4096 * i, [P, D]) for i in range(2)]
        r_ = [mem.at(f"residual{i}", 191488 + 4096 * i, [P, D]) for i in range(2)]
        st = [mem.at(f"stats{i}", 199680 + 64 * i, [P, 16]) for i in range(2)]
        ps = banks(nc, s, "out_ps", 4)
        tp = banks(nc, s, "hT_ps", 4)
        gb_in, filled, res_done, step, root_done, inv_done, scaled, h_done, turned, t_copied = sems(
            nc, s, "gb_in", "n_filled", "n_res", "n_step", "n_root", "n_inverse", "n_scaled", "h_done", "h_turned", "hT_copied")
        x_in = sems(nc, s, "xr_in_a", "xr_in_b")
        block = s.enter_context(nc.Block())

        @block.sync
        def _(sp):
            for t in range(TILES + 1):
                r = rows_of(t)
                if t >= 2:
                    sp.wait_ge(res_done, 2 * (t - 1))
                sp.dma_start(x[t % 2][0:r, :], a["x"][P * t:P * t + r, :]).then_inc(x_in[t % 2], 16)
                if t == 0:
                    sp.dma_start(b[:], a["ln1_b"].partition_broadcast(P)).then_inc(gb_in, 16)

        @block.tensor
        def _(pe):
            for t in range(TILES + 2):
                if t <= TILES:
                    r = rows_of(t)
                    if t >= 2:
                        pe.wait_ge(res_done, 2 * (t - 1))
                    for c in range(2):
                        for k in range(KC):
                            mm = nc.tensor.matmul(ps[2 * (t % 2) + c][0:r, :], m["mergedT"][:, k, P * t:P * t + r],
                                                  w_out[:, k, 512 * c:512 * (c + 1)], start=(k == 0), stop=(k == KC - 1))
                        mm.then_inc(filled, 1)
                n = t - 1
                if n >= 0:
                    r = rows_of(n)
                    pe.wait_ge(h_done, n + 1)
                    if n >= 2:
                        pe.wait_ge(t_copied, 2 * (n - 1))
                    for k in range(KC):
                        mm = nc.tensor.transpose(tp[2 * (n % 2) + k // 4][:, P * (k % 4):P * (k % 4) + r],
                                                 m["h"][0:r, n, P * k:P * (k + 1)], m["ident"][0:r, 0:r])
                        if k % 4 == 3:
                            mm.then_inc(turned, 1)

        @block.scalar
        def _(act):
            for t in range(TILES + 2):
                if t <= TILES:
                    r = rows_of(t)
                    act.wait_ge(step, 3 * t + 3)
                    nc.scalar.activation(st[t % 2][0:r, 14:15], st[t % 2][0:r, 13:14], ACT.Sqrt, bias=m["eps"][0:r, :]).then_inc(root_done, 1)
                n = t - 1
                if n >= 0:
                    r = rows_of(n)
                    for y in range(2):
                        act.wait_ge(turned, 2 * n + y + 1)
                        nc.scalar.copy(m["hT"][:, 4 * y:4 * y + 4, P * n:P * n + r],
                                       tp[2 * (n % 2) + y][:].rearrange("p (x q) -> p x q", x=4)[:, :, 0:r]).then_inc(t_copied, 1)

        @block.vector
        def _(dve):
            for t in range(TILES + 1):
                r = rows_of(t)
                if t >= 2:
                    dve.wait_ge(h_done, t - 1)
                dve.wait_ge(x_in[t % 2], 16 * (t // 2 + 1))
                s_ = st[t % 2]
                for c in range(2):
                    cols = slice(512 * c, 512 * (c + 1))
                    dve.wait_ge(filled, 2 * t + c + 1)
                    nc.vector.scalar_tensor_tensor(r_[t % 2][0:r, cols], x[t % 2][0:r, cols], ALPHA, ps[2 * (t % 2) + c][0:r, :],
                                                   ALU.mult, ALU.add).then_inc(res_done, 1)
                for c in range(2):
                    dve.wait_ge(res_done, 2 * t + c + 1)
                    nc.vector.bn_stats(s_[0:r, 6 * c:6 * c + 6], r_[t % 2][0:r, 512 * c:512 * (c + 1)]).then_inc(step, 1)
                dve.wait_ge(step, 3 * t + 2)
                nc.vector.bn_aggr(s_[0:r, 12:14], s_[0:r, 0:12]).then_inc(step, 1)
                dve.wait_ge(root_done, t + 1)
                nc.vector.reciprocal(s_[0:r, 15:16], s_[0:r, 14:15]).then_inc(inv_done, 1)
                dve.wait_ge(inv_done, t + 1)
                hrow = m["h"][0:r, t, :]
                nc.vector.tensor_scalar(r_[t % 2][0:r, :], r_[t % 2][0:r, :], s_[0:r, 12:13], s_[0:r, 15:16],
                                        ALU.subtract, ALU.mult).then_inc(scaled, 1)
                dve.wait_ge(scaled, 2 * t + 1)
                nc.vector.tensor_tensor(r_[t % 2][0:r, :], r_[t % 2][0:r, :], g[0:r, :], ALU.mult).then_inc(scaled, 1)
                dve.wait_ge(scaled, 2 * t + 2)
                if t == 0:
                    dve.wait_ge(gb_in, 16)
                nc.vector.tensor_tensor(hrow, r_[t % 2][0:r, :], b[0:r, :], ALU.add).then_inc(h_done, 1)
            dve.wait_ge(h_done, TILES + 1)


def route_experts(nc, mem, a, m):
    with ExitStack() as s:
        T = TILES + 1
        qT = [mem.at(f"peer_qT{i}", 107520 + 8448 * i, [P, 2, TOKENS]) for i in range(2)]
        wq = mem.at("wq_head", 124416, [P, KC, 2 * PKEYS])
        sub = [mem.at(f"sub_keysT{i}", 132608 + 1024 * i, [P, 2, PKEYS]) for i in range(2)]
        gate = [mem.at(f"expert_gate{i}", 134656 + 576 * i, [P, T, TOPK]) for i in range(2)]
        flat = [mem.at(f"gate_address{i}", 135808 + 256 * i, [P, DENSE, TOPK], U32) for i in range(2)]
        iota_u = mem.at("rank_iota_u", 136320, [P, TOPK], U32)
        iota = mem.at("rank_iota", 136384, [P, TOPK])
        token_u = mem.at("dense_token_u", 136448, [P, DENSE], U32)
        token = mem.at("dense_token", 136480, [P, DENSE])
        mx = mem.at("gate_max", 136512, [P, T])
        sm = mem.at("gate_sum", 136576, [P, T])
        iv = mem.at("gate_inverse", 136640, [P, T])
        GROUPS = [(0, 1), (2, 3), (4, 5), (6, 7, 8)]
        SETS = 3

        def scratch(name, offset, shape, dtype=F32):
            return [mem.at(f"{name}{u}", 136704 + 4096 * u + offset, shape, dtype) for u in range(SETS)]

        best = scratch("best", 0, [P, 2, TOPK])
        besti = scratch("best_index", 128, [P, 2, TOPK], U32)
        bestf = scratch("best_index_f", 256, [P, 2, TOPK])
        pos = scratch("pair_position", 384, [P, TOPK], U32)
        ab = scratch("pair_ranks", 448, [P, 2, TOPK], U32)
        abf = scratch("pair_ranks_f", 576, [P, 2, TOPK])
        pick = scratch("picked", 704, [P, 2, TOPK])
        expert = scratch("expert_f", 832, [P, TOPK])
        left = scratch("scores_left", 1024, [P, 2, PKEYS])
        cand = scratch("pair_scores", 2048, [P, TOPK * TOPK])
        cand2 = scratch("pair_scores_left", 3072, [P, TOPK * TOPK])
        hot = scratch("one_hot", 2048, [P, 2, TOPK * TOPK])
        idx_all, gate_all = m["idx_all"], m["gate_all"]
        idx = [mem.at(f"picked_index{i}", 148992 + 320 * i, [P, GATHER + 1, TOPK], U32) for i in range(2)]
        idx_s = [mem.at(f"sample_index{i}", 149632 + 32 * i, [P, 4], U32) for i in range(2)]
        gate_s = [mem.at(f"sample_gate{i}", 149696 + 32 * i, [P, 4]) for i in range(2)]
        SL = 6
        dots = mem.at("early_dots", 149760, [P, SL])
        gel = mem.at("early_activated", 149792, [P, SL])
        coef = mem.at("early_coefficients", 149824, [P, SL])
        junk = mem.at("unused_early_products", 150016, [P, D], BF16)
        ring = mem.at("early_rows", 152064, [P, SL, 2 * D])
        keys = mem.at("key_columns", 50176, [P, 2, KC, P])
        acts = mem.at("dense_acts_stage", 58368, [P, 4, P * DENSE])
        qp = banks(nc, s, "peer_q_ps", 2)
        up = banks(nc, s, "dense_act_ps", 2)
        scp = banks(nc, s, "peer_score_ps", 4)
        (cleared, fine, norm, made, acc_set, q_filled, q_copied, scored, shifted, exped, gated, kept,
         packed, h_packed, dotted, gelud, weighed, used, act_filled, act_gelud) = sems(
            nc, s, "gates_cleared", "route_fine_step", "gate_norm_step", "r_made", "acc_set", "q_filled", "q_copied", "scored",
            "scores_shifted", "exp_done", "gates_ready", "gates_kept", "sample_packed",
            "sample_h_packed", "dotted", "gelu_done", "coef_done", "row_used", "dense_filled", "dense_gelu")
        got = sems(nc, s, *[f"row_in{i}" for i in range(SL)])
        keys_in = sems(nc, s, "key_columns_in_a", "key_columns_in_b")
        acts_out = sems(nc, s, *[f"dense_acts_out{i}" for i in range(4)])
        added = sems(nc, s, *[f"gates_added{t}" for t in range(DENSE)])
        wq_in, = sems(nc, s, "wq_in")
        sub_in = sems(nc, s, "sub_in_a", "sub_in_b")
        block = s.enter_context(nc.Block())
        QT = 2 * SPANS
        STAGES = [2, 4, 2, 3, 2, 2, 1, 1, 2, 1, 1, 2, 1, 1, 1]
        FINE_T = sum(STAGES)
        FINE = T * FINE_T
        PARTS = [slice(0, DENSE), slice(DENSE, T)]

        ROWS = EARLY * TOPK + 4
        BEATS = ROWS
        PACKS = 8
        ET = EXPERTS // P // HEADS
        UNITS = QT + ET

        def units_at(beat):
            return [j for j in range(UNITS) if j * BEATS // UNITS == beat]

        def tile_at(position):
            return (GATHER + position) if position < DENSE else (position - DENSE) if position < TILES else TILES

        def read_at(position):
            group = [g for g in GROUPS if position in g][0]
            return group[0] * FINE_T + len(group) * (STAGES[0] + STAGES[1])

        def is_head(h, n):
            return isinstance(h, int) and h == n

        def over_heads(eng, body):
            body(0, 0)
            body(1, 1)
            with eng.Fori(1, HEADS // 2 - 1) as pair:
                for par in range(2):
                    body(pair * 2 + par, par)
            body(HEADS - 2, 0)
            body(HEADS - 1, 1)

        def chosen(x, h, dims):
            return x[h] if isinstance(h, int) else x[bass.ds(h, 1)].rearrange(f"o {dims} -> (o {dims[0]}) {dims[2:]}")

        @block.sync
        def _(sp):
            wq_of = a["peer_wq"].rearrange("(k p) (h c) -> h p k c", p=P, h=HEADS)
            sub_of = a["sub_keysT"].rearrange("(h c p) n -> h p c n", h=HEADS, c=2)

            def query_weights(h, par):
                if not is_head(h, 0):
                    sp.wait_ge(q_filled, h * QT)
                sp.dma_start(wq[:], chosen(wq_of, h, "p k c")).then_inc(wq_in, 16)
                if not (isinstance(h, int) and h < 2):
                    sp.wait_ge(scored, h * T - T)
                sp.dma_start(sub[par][:], chosen(sub_of, h, "p c n")).then_inc(sub_in[par], 16)

            def keys_load(h, e):
                if not (is_head(h, 0) and e < 2):
                    sp.wait_ge(act_filled, h * ET + (e - 1))
                sp.dma_start(keys[:, e % 2, :, :], chosen(a["key_columns"], h * ET + e, "p k e")).then_inc(keys_in[e % 2], 16)

            def loads(h, par):
                if not is_head(h, 0):
                    for e in range(ET):
                        keys_load(h - 1, e)
                        if e == 3:
                            pack(h - 1, 1 - par)
                        if e == 13 and not (isinstance(h, int) and h >= HEADS - 2):
                            query_weights(h + 2, par)

            def pack(h, par):
                sp.wait_ge(gated, h * 2 + 2)
                for q in range(4):
                    part = slice(NEW * q, NEW * (q + 1))
                    sp.dma_start(idx_s[par][part, :], idx[par][0:NEW, GATHER, 4 * q:4 * q + 4]).then_inc(packed, 16)
                    sp.dma_start(gate_s[par][part, :], gate[par][0:NEW, TILES, 4 * q:4 * q + 4]).then_inc(packed, 16)

            for h in range(3):
                query_weights(h, h % 2)
            for q in range(1, 4):
                sp.dma_start(m["h"][NEW * q:NEW * (q + 1), TILES, :], m["h"][0:NEW, TILES, :]).then_inc(h_packed, 16)
            sp.wait_ge(acc_set, T)
            over_heads(sp, loads)
            for e in range(ET):
                keys_load(HEADS - 1, e)
                if e == 3:
                    pack(HEADS - 1, 1)
            sp.wait_ge(packed, 16 * PACKS * HEADS)
            sp.wait_ge(h_packed, 48)
            for x in range(4):
                sp.wait_ge(acts_out[x], 16 * HEADS * ET // 4)

        @block.gpsimd
        def _(pool):
            pool.iota(iota_u[:], pattern=[[1, TOPK]], base=0, channel_multiplier=0).then_inc(made, 1)
            pool.iota(token_u[:], pattern=[[P, DENSE]], base=0, channel_multiplier=1).then_inc(made, 1)
            pool.wait_ge(made, 2)
            pool.tensor_copy(iota[:], iota_u[:]).then_inc(made, 1)
            pool.tensor_copy(token[:], token_u[:]).then_inc(made, 1)

            def scatter(h, par, n):
                t, k = n // TOPK, n % TOPK
                if n == 0:
                    pool.wait_ge(gated, h * 2 + 1)
                    pool.nop(nofuse=True)
                if k == 0 and not is_head(h, 0):
                    pool.wait_ge(added[t], h * (16 * TOPK))
                    pool.nop(nofuse=True)
                pool.indirect_dma_start(a["gates_by_expert"], bass.IndirectOffsetOnAxis(ap=flat[par][:, t, k:k + 1], axis=0),
                                        gate[par][:, t, k:k + 1], None, compute_op=ALU.add).then_inc(added[t], 16)

            def gather(h, par, x):
                if x == 0:
                    pool.wait_ge(fine, h * FINE + FINE)
                    pool.nop(nofuse=True)
                if x == EARLY * TOPK:
                    pool.wait_ge(packed, h * (16 * PACKS) + 16 * PACKS)
                    pool.nop(nofuse=True)
                if not (is_head(h, 0) and x < SL):
                    pool.wait_ge(used, h * ROWS + (x - SL + 1))
                    pool.nop(nofuse=True)
                source = idx[par][:, x // TOPK, x % TOPK:x % TOPK + 1] if x < EARLY * TOPK else \
                    idx_s[par][:, x - EARLY * TOPK:x - EARLY * TOPK + 1]
                pool.indirect_dma_start(ring[:, x % SL, :], None, a["experts"],
                                        bass.IndirectOffsetOnAxis(ap=source, axis=0)).then_inc(got[x % SL], 16)

            half, turn = DENSE * TOPK // 2, 24

            def rest(h, par, beat):
                gather(h - 1, 1 - par, beat)
                if beat < turn:
                    for n in range(half * beat // turn, half * (beat + 1) // turn):
                        scatter(h - 1, 1 - par, half + n)

            def body(h, par):
                for beat in range(BEATS):
                    if not is_head(h, 0):
                        rest(h, par, beat)
                    if beat >= turn:
                        for n in range(half * (beat - turn) // (BEATS - turn), half * (beat - turn + 1) // (BEATS - turn)):
                            scatter(h, par, n)

            over_heads(pool, body)
            for beat in range(BEATS):
                rest(HEADS, 0, beat)
            for t in range(DENSE):
                pool.wait_ge(added[t], HEADS * 16 * TOPK)

        @block.tensor
        def _(pe):
            def queries(h, par, n):
                if n == 0:
                    pe.wait_ge(wq_in, h * 16 + 16)
                if n >= 2 or not is_head(h, 0):
                    pe.wait_ge(q_copied, h * QT + (n - 1))
                c, y = n // SPANS, n % SPANS
                for k in range(KC):
                    mm = nc.tensor.matmul(qp[n % 2][:, 0:SPAN], wq[:, k, PKEYS * c:PKEYS * (c + 1)],
                                          m["hT"][:, k, SPAN * y:SPAN * (y + 1)], start=(k == 0), stop=(k == KC - 1))
                mm.then_inc(q_filled, 1)

            def scores(h, par, ys):
                for y in ys:
                    t, r = tile_at(y), rows_of(tile_at(y))
                    if y == 0:
                        pe.wait_ge(sub_in[par], 16 * (h // 2 + 1) if isinstance(h, int) else (h - par) * 8 + 16)
                        pe.wait_ge(q_copied, h * QT + QT)
                    if y >= 4:
                        pe.wait_ge(fine, h * FINE + read_at(y - 4))
                    elif not is_head(h, 0):
                        last = max(v for v in range(T) if (v + 1 - par) % 4 == (y + par) % 4)
                        pe.wait_ge(fine, (h - 1) * FINE + read_at(last))
                    for c in range(2):
                        mm = nc.tensor.matmul(scp[(y + par) % 4][0:r, PKEYS * c:PKEYS * (c + 1)], qT[par][:, c, P * t:P * t + r],
                                              sub[par][:, c, :], start=True, stop=True)
                    mm.then_inc(scored, 1)

            def key_products(h, e):
                pe.wait_ge(keys_in[e % 2], h * (ET // 2 * 16) + 16 * (e // 2 + 1))
                if not (is_head(h, 0) and e < 2):
                    pe.wait_ge(act_gelud, h * ET + (e - 1))
                for k in range(KC):
                    mm = nc.tensor.matmul(up[e % 2][:], keys[:, e % 2, k, :], m["hT"][:, k, P * GATHER:SEQ], start=(k == 0), stop=(k == KC - 1))
                mm.then_inc(act_filled, 1)

            def body(h, par):
                for beat in range(BEATS):
                    for ys, at in (((4, 5), 3), ((6, 7), 12), ((8,), 21)):
                        if beat == at:
                            scores(h, par, ys)
                    if beat == 30 and not is_head(h, HEADS - 1):
                        scores(h + 1, 1 - par, range(4))
                    for j in units_at(beat):
                        if j >= QT:
                            if not is_head(h, 0):
                                key_products(h - 1, j - QT)
                        elif not is_head(h, HEADS - 1):
                            queries(h + 1, 1 - par, j)

            for n in range(QT):
                queries(0, 0, n)
            scores(0, 0, range(4))
            over_heads(pe, body)
            for e in range(ET):
                key_products(HEADS - 1, e)

        @block.scalar
        def _(act):
            acts_of = a["dense_acts"].rearrange("(n p) t -> n p t", p=P)

            def copy_queries(h, par, n):
                if n == 0 and not (isinstance(h, int) and h < 2):
                    act.wait_ge(scored, (h - 1) * T)
                act.wait_ge(q_filled, h * QT + (n + 1))
                nc.scalar.copy(qT[par][:, n // SPANS, SPAN * (n % SPANS):SPAN * (n % SPANS + 1)],
                               qp[n % 2][:, 0:SPAN]).then_inc(q_copied, 1)

            def activate(h, e):
                act.wait_ge(act_filled, h * ET + (e + 1))
                if not (is_head(h, 0) and e < 4):
                    act.wait_ge(acts_out[e % 4], h * (ET // 4 * 16) + 16 * (e // 4))
                nc.scalar.activation(acts[:, e % 4, :], up[e % 2][:], ACT.Gelu).then_inc(act_gelud, 1)
                act.wait_ge(act_gelud, h * ET + (e + 1))
                act.dma_start(chosen(acts_of, h * ET + e, "p t"), acts[:, e % 4, :]).then_inc(acts_out[e % 4], 16)

            def exponentials(h, par, x):
                act.wait_ge(shifted, h * 4 + (2 * x + 2))
                nc.scalar.activation(gate[par][:, PARTS[x], :], gate[par][:, PARTS[x], :], ACT.Exp).then_inc(exped, 1)

            def keep(h, par):
                act.wait_ge(gated, h * 2 + 2)
                nc.scalar.activation(gate_all[:, h, :, :] if isinstance(h, int) else
                                     gate_all[:, bass.ds(h, 1), :, :].rearrange("p o t k -> p (o t) k"),
                                     gate[par][:, DENSE + EARLY:TILES, :], ACT.Copy).then_inc(kept, 1)

            def weight(h, par, x):
                c = x % SL
                if x == EARLY * TOPK:
                    act.wait_ge(packed, h * (16 * PACKS) + 16 * PACKS)
                g = gate[par][:, DENSE + x // TOPK, x % TOPK:x % TOPK + 1] if x < EARLY * TOPK else \
                    gate_s[par][:, x - EARLY * TOPK:x - EARLY * TOPK + 1]
                act.wait_ge(dotted, h * ROWS + (x + 1))
                if not (is_head(h, 0) and x < SL):
                    act.wait_ge(used, h * ROWS + (x - SL + 1))
                nc.scalar.activation(gel[:, c:c + 1], dots[:, c:c + 1], ACT.Gelu).then_inc(gelud, 1)
                act.wait_ge(gelud, h * ROWS + (x + 1))
                nc.scalar.activation(coef[:, c:c + 1], gel[:, c:c + 1], ACT.Copy, scale=g).then_inc(weighed, 1)

            def body(h, par):
                for beat in range(BEATS):
                    if not is_head(h, 0):
                        if beat == 0:
                            exponentials(h - 1, 1 - par, 1)
                            keep(h - 1, 1 - par)
                        weight(h - 1, 1 - par, beat)
                    if beat == BEATS // 2:
                        exponentials(h, par, 0)
                    for j in units_at(beat):
                        if j >= QT:
                            if not is_head(h, 0):
                                activate(h - 1, j - QT)
                        elif not is_head(h, HEADS - 1):
                            copy_queries(h + 1, 1 - par, j)

            for n in range(QT):
                copy_queries(0, 0, n)
            for t in range(TILES):
                nc.scalar.mul(m["acc"][:, t, :], m["h"][:, t, :], ALPHA).then_inc(acc_set, 1)
            act.wait_ge(cleared, 3)
            nc.scalar.mul(m["acc"][0:NEW, TILES, :], m["h"][0:NEW, TILES, :], ALPHA).then_inc(acc_set, 1)
            act.wait_ge(acc_set, T)
            over_heads(act, body)
            exponentials(HEADS - 1, 1, 1)
            keep(HEADS - 1, 1)
            for x in range(ROWS):
                weight(HEADS - 1, 1, x)
                for e in range(ET * x // ROWS, ET * (x + 1) // ROWS):
                    activate(HEADS - 1, e)
            act.wait_ge(kept, HEADS)

        @block.vector
        def _(dve):
            nc.vector.memset(gate[0][:, T - 1, :], 0.0).then_inc(cleared, 1)
            nc.vector.memset(gate[1][:, T - 1, :], 0.0).then_inc(cleared, 1)
            nc.vector.memset(m["acc"][:, TILES, :], 0.0).then_inc(cleared, 1)
            dve.wait_ge(cleared, 3)
            dve.wait_ge(made, 4)

            def stage(n, u, y, h, par):
                r = rows_of(tile_at(y))
                sc = [scp[(y + par) % 4][0:r, PKEYS * x:PKEYS * (x + 1)] for x in range(2)]
                g = gate[par][0:r, y, :]
                oh = hot[u][0:r].rearrange("p x (k j) -> p (x k) j", j=TOPK)
                v = nc.vector
                if n == 0:
                    return [v.max(best[u][0:r, x, 0:8], sc[x]) for x in range(2)]
                if n == 1:
                    return ([v.match_replace(left[u][0:r, x, :], best[u][0:r, x, 0:8], sc[x], LOWEST) for x in range(2)]
                            + [v.max_index(besti[u][0:r, x, 0:8], best[u][0:r, x, 0:8], sc[x]) for x in range(2)])
                if n == 2:
                    return [v.max(best[u][0:r, x, 8:16], left[u][0:r, x, :]) for x in range(2)]
                if n == 3:
                    return ([v.max_index(besti[u][0:r, x, 8:16], best[u][0:r, x, 8:16], left[u][0:r, x, :]) for x in range(2)]
                            + [v.tensor_tensor(cand[u][0:r, :].rearrange("p (i j) -> p i j", i=TOPK),
                                               best[u][0:r, 0, :].unsqueeze(2).broadcast_to([r, TOPK, TOPK]),
                                               best[u][0:r, 1, :].unsqueeze(1).broadcast_to([r, TOPK, TOPK]), ALU.add)])
                if n == 4:
                    return [v.max(g[:, 0:8], cand[u][0:r, :]), v.tensor_copy(bestf[u][0:r], besti[u][0:r])]
                if n == 5:
                    return [v.match_replace(cand2[u][0:r, :], g[:, 0:8], cand[u][0:r, :], LOWEST),
                            v.max_index(pos[u][0:r, 0:8], g[:, 0:8], cand[u][0:r, :])]
                if n == 6:
                    return [v.max(g[:, 8:16], cand2[u][0:r, :])]
                if n == 7:
                    return [v.max_index(pos[u][0:r, 8:16], g[:, 8:16], cand2[u][0:r, :])]
                if n == 8:
                    return [v.tensor_scalar(ab[u][0:r, 0, :], pos[u][0:r, :], 4, None, ALU.logical_shift_right),
                            v.tensor_scalar(ab[u][0:r, 1, :], pos[u][0:r, :], 15, None, ALU.bitwise_and)]
                if n == 9:
                    return [v.tensor_copy(abf[u][0:r], ab[u][0:r])]
                if n == 10:
                    return [v.tensor_tensor(oh, abf[u][0:r].rearrange("p x k -> p (x k)").unsqueeze(2).broadcast_to([r, 2 * TOPK, TOPK]),
                                            iota[0:r, :].unsqueeze(1).broadcast_to([r, 2 * TOPK, TOPK]), ALU.is_equal)]
                if n == 11:
                    o3 = [hot[u][0:r, x, :].rearrange("p (k j) -> p k j", j=TOPK) for x in range(2)]
                    return [v.tensor_tensor(o3[x], o3[x], bestf[u][0:r, x, :].unsqueeze(1).broadcast_to([r, TOPK, TOPK]), ALU.mult)
                            for x in range(2)]
                if n == 12:
                    return [v.tensor_reduce(pick[u][0:r].rearrange("p x k -> p (x k)"), oh, AX, ALU.add)]
                if n == 13:
                    return [v.scalar_tensor_tensor(expert[u][0:r, :], pick[u][0:r, 0, :], float(PKEYS), pick[u][0:r, 1, :],
                                                   ALU.mult, ALU.add)]
                if y < DENSE:
                    return [v.tensor_scalar(flat[par][:, y, :], expert[u][:], float(P * DENSE), token[:, y:y + 1], ALU.mult, ALU.add)]
                if y < DENSE + EARLY or y == TILES:
                    return [v.tensor_copy(idx[par][0:r, y - DENSE, :], expert[u][0:r, :])]
                z = y - DENSE - EARLY
                return [v.tensor_copy(idx_all[0:r, h, z, :] if isinstance(h, int) else
                                      idx_all[0:r, bass.ds(h, 1), z, :].rearrange("p o k -> p (o k)"), expert[u][0:r, :])]

            def group_stages(h, par, group, stages, at, last):
                for n in stages:
                    for u, y in enumerate(group):
                        if last[u] > 0 or not is_head(h, 0):
                            dve.wait_ge(fine, h * FINE + last[u])
                            dve.nop(nofuse=True)
                        if n == 0:
                            dve.wait_ge(scored, h * T + (y + 1))
                            dve.nop(nofuse=True)
                        instructions = stage(n, u, y, h, par)
                        assert len(instructions) == STAGES[n]
                        for ins in instructions:
                            ins.then_inc(fine, 1)
                        at += STAGES[n]
                        last[u] = at
                return at

            def tile_of_row(x):
                return x // TOPK if x < EARLY * TOPK else TILES

            def dot(h, x):
                if not (is_head(h, 0) and x < SL):
                    dve.wait_ge(gelud, h * ROWS + (x - SL + 1))
                if not (is_head(h, 0) and x == 0):
                    dve.wait_ge(dotted, h * ROWS + x)
                if x == EARLY * TOPK:
                    dve.wait_ge(h_packed, 48)
                dve.wait_ge(got[x % SL], h * (16 * ROWS // SL) + 16 * (x // SL + 1))
                nc.vector.scalar_tensor_tensor(junk[:], ring[:, x % SL, 0:D], 1.0, m["h"][:, tile_of_row(x), :], ALU.mult, ALU.mult,
                                               accum_out=dots[:, x % SL:x % SL + 1]).then_inc(dotted, 1)

            def value(h, x):
                if not (is_head(h, 0) and x == 0):
                    dve.wait_ge(used, h * ROWS + x)
                dve.wait_ge(weighed, h * ROWS + (x + 1))
                sum_ = m["acc"][:, tile_of_row(x), :]
                nc.vector.scalar_tensor_tensor(sum_, ring[:, x % SL, D:2 * D], coef[:, x % SL:x % SL + 1], sum_,
                                               ALU.mult, ALU.add).then_inc(used, 1)

            def row(h, beat):
                dot(h, beat)
                if beat >= LAG:
                    value(h, beat - LAG)

            def shift(h, par, x):
                ys = PARTS[x]
                dve.wait_ge(fine, h * FINE + ys.stop * FINE_T)
                nc.vector.tensor_copy(mx[:, ys], gate[par][:, ys, 0]).then_inc(shifted, 1)
                dve.wait_ge(shifted, h * 4 + (2 * x + 1))
                nc.vector.tensor_tensor(gate[par][:, ys, :], gate[par][:, ys, :],
                                        mx[:, ys].unsqueeze(2).broadcast_to([P, ys.stop - ys.start, TOPK]), ALU.subtract).then_inc(shifted, 1)

            def normalise(h, par, x):
                ys = PARTS[x]
                dve.wait_ge(exped, h * 2 + (x + 1))
                nc.vector.tensor_reduce(sm[:, ys], gate[par][:, ys, :], AX, ALU.add).then_inc(norm, 1)
                dve.wait_ge(norm, h * 4 + (2 * x + 1))
                nc.vector.reciprocal(iv[:, ys], sm[:, ys]).then_inc(norm, 1)
                dve.wait_ge(norm, h * 4 + (2 * x + 2))
                nc.vector.tensor_tensor(gate[par][:, ys, :], gate[par][:, ys, :],
                                        iv[:, ys].unsqueeze(2).broadcast_to([P, ys.stop - ys.start, TOPK]), ALU.mult).then_inc(gated, 1)

            def route_head(h, par):
                if not (isinstance(h, int) and h < 2):
                    dve.wait_ge(kept, h - 1)
                    for t in range(DENSE):
                        dve.wait_ge(added[t], (h - 1) * (16 * TOPK))
                if not is_head(h, 0):
                    normalise(h - 1, 1 - par, 1)
                per = BEATS // len(GROUPS)
                for beat in range(BEATS):
                    group, part = GROUPS[beat // per], beat % per
                    if part == 0:
                        at = group[0] * FINE_T
                        last = [at] * len(group)
                    if beat == BEATS // 2:
                        shift(h, par, 0)
                    if beat == BEATS // 2 + 1:
                        normalise(h, par, 0)
                    N = len(STAGES)
                    at = group_stages(h, par, group, range(N * part // per, N * (part + 1) // per), at, last)
                    if not is_head(h, 0):
                        row(h - 1, beat)
                if not is_head(h, 0):
                    for x in range(ROWS - LAG, ROWS):
                        value(h - 1, x)
                shift(h, par, 1)

            over_heads(dve, route_head)
            normalise(HEADS - 1, 1, 1)
            dve.wait_ge(acc_set, T)
            for beat in range(ROWS):
                row(HEADS - 1, beat)
            for x in range(ROWS - LAG, ROWS):
                value(HEADS - 1, x)
            dve.wait_ge(gated, 2 * HEADS)
            dve.wait_ge(used, HEADS * ROWS)


class LastNorm:

    ORDER = [*range(EARLY), TILES, *range(EARLY, TILES)]
    FIRST = EARLY + 1

    def __init__(self, nc, mem, stack, m):
        self.nc, self.m = nc, m
        self.g = mem.at("ln2_g", 173056, [P, D])
        self.b = mem.at("ln2_b", 177152, [P, D])
        self.st = mem.at("stats_y", 50176, [P, TILES + 1, 16])
        (self.gb_in, self.step, self.root_done, self.inv_done, self.scaled, self.gained, self.y_done, self.out_done) = sems(
            nc, stack, "ln2_in", "y_step", "y_root", "y_inverse", "y_scaled", "y_gained", "y_done", "y_out")

    def tile(self, k):
        t = self.ORDER[k]
        return rows_of(t), self.st[0:rows_of(t), t, :], self.m["acc"][0:rows_of(t), t, :]

    def statistics(self, dve, k):
        r, st, row = self.tile(k)
        for c in range(2):
            self.nc.vector.bn_stats(st[:, 6 * c:6 * c + 6], row[:, 512 * c:512 * (c + 1)]).then_inc(self.step, 1)
        dve.wait_ge(self.step, 3 * k + 2)
        self.nc.vector.bn_aggr(st[:, 12:14], st[:, 0:12]).then_inc(self.step, 1)

    def root(self, act, k):
        r, st, row = self.tile(k)
        act.wait_ge(self.step, 3 * k + 3)
        self.nc.scalar.activation(st[:, 14:15], st[:, 13:14], ACT.Sqrt, bias=self.m["eps"][0:r, :]).then_inc(self.root_done, 1)

    def inverse(self, dve, k):
        r, st, row = self.tile(k)
        dve.wait_ge(self.root_done, k + 1)
        self.nc.vector.reciprocal(st[:, 15:16], st[:, 14:15]).then_inc(self.inv_done, 1)
        dve.wait_ge(self.inv_done, 2 * k + 1)
        self.nc.vector.tensor_scalar(st[:, 14:15], st[:, 12:13], st[:, 15:16], -1.0, ALU.mult, ALU.mult).then_inc(self.inv_done, 1)

    def scale(self, act, k):
        r, st, row = self.tile(k)
        act.wait_ge(self.inv_done, 2 * k + 2)
        self.nc.scalar.activation(row, row, ACT.Identity, bias=st[:, 14:15], scale=st[:, 15:16]).then_inc(self.scaled, 1)

    def gain(self, dve, k):
        r, st, row = self.tile(k)
        dve.wait_ge(self.scaled, k + 1)
        self.nc.vector.tensor_tensor(row, row, self.g[0:r, :], ALU.mult).then_inc(self.gained, 1)

    def offset(self, eng, k):
        r, st, row = self.tile(k)
        eng.wait_ge(self.gained, k + 1)
        eng.tensor_tensor(row, row, self.b[0:r, :], ALU.add).then_inc(self.y_done, 1)

    def load(self, sp, a):
        sp.dma_start(self.g[:], a["ln2_g"].partition_broadcast(P)).then_inc(self.gb_in, 16)
        sp.dma_start(self.b[:], a["ln2_b"].partition_broadcast(P)).then_inc(self.gb_in, 16)

    def store(self, sp, a, k):
        t = self.ORDER[k]
        r, st, row = self.tile(k)
        sp.wait_ge(self.y_done, k + 1)
        sp.dma_start(a["out_y"][P * t:P * t + r, :], row).then_inc(self.out_done, 16)


def apply_experts(nc, mem, a, m, norm):
    with ExitStack() as s:
        vals = mem.at("value_rows", 0, [P, 8, D])
        ring = mem.at("expert_rows", 107520, [P, SLOTS, 2 * D])
        gts = mem.at("dense_gates", 51200, [P, 4, P * DENSE])
        w = mem.at("dense_weights", 185344, [P, 8, P * DENSE])
        junk = mem.at("unused_products", 201728, [P, D], BF16)
        cur = mem.at("head_index", 209920, [P, GATHER - EARLY, TOPK], U32)
        curg = mem.at("head_gate", 210176, [P, GATHER - EARLY, TOPK])
        dots = mem.at("dots", 210432, [P, 8])
        gel = mem.at("activated", 210464, [P, 8])
        coef = mem.at("coefficients", 210496, [P, 8])
        vp = [s.enter_context(nc.psum_tensor(f"dense_out_ps{i}", [P, D], F32)) for i in range(2)]
        ss = s.enter_context(nc.psum_tensor("sample_sum_ps", [P, D], F32))
        (cur_set, dotted, gelud, weighed, used, act_gated, v_filled, v_added, summed, sample_set) = sems(
            nc, s, "head_index_set", "dotted", "gelu_done", "coef_done", "row_used",
            "dense_weighed", "dense_out_filled", "dense_out_added", "sample_summed", "sample_set")
        got = sems(nc, s, *[f"row_in{i}" for i in range(SLOTS)])
        tile_in = sems(nc, s, *[f"expert_tile_in{i}" for i in range(8)])
        gts_in = sems(nc, s, *[f"dense_gates_in{i}" for i in range(4)])
        block = s.enter_context(nc.Block())
        NT = GATHER - EARLY
        ROWS = NT * TOPK
        ET = 16
        PER = ROWS // ET
        GRP = 4

        def iterations(eng, body):
            body(0)
            with eng.Fori(1, HEADS) as i:
                body(i)

        def first(i):
            return isinstance(i, int) and i == 0

        norm_at = [GRP + 1 + 3 * k for k in range(norm.FIRST)]

        @block.sync
        def _(sp):
            acts_of = a["dense_acts"].rearrange("(n p) t -> n p t", p=P)
            table = a["experts"].rearrange("(n p) c -> n p c", p=P)
            dgates = a["gates_by_expert"].rearrange("(n p t) o -> n p (t o)", p=P, t=P * DENSE)

            def tile(src, n):
                return src[n] if isinstance(n, int) else src[bass.ds(n, 1)]

            def flatten(x, n, dims):
                return x if isinstance(n, int) else x.rearrange(f"o {dims} -> (o p) {dims[2:]}")

            def loads(i):
                for e in range(ET):
                    n = i * ET + e
                    if not (first(i) and e < 8):
                        sp.wait_ge(v_filled, i * ET + (e - e % GRP - GRP))
                    sp.dma_start(w[:, e % 8, :], flatten(tile(acts_of, n), n, "p t")).then_inc(tile_in[e % 8], 16)
                    if not (first(i) and e < 4):
                        sp.wait_ge(act_gated, n - 3)
                    sp.dma_start(gts[:, e % 4, :], flatten(tile(dgates, n), n, "p t")).then_inc(gts_in[e % 4], 16)
                    sp.dma_start(vals[:, e % 8, :], flatten(tile(table, n), n, "p c")[:, D:2 * D]).then_inc(tile_in[e % 8], 16)
                    if first(i) and e == 1:
                        norm.load(sp, a)


            iterations(sp, loads)
            for k in range(norm.FIRST):
                norm.store(sp, a, k)

        @block.gpsimd
        def _(pool):
            def gather(slot, source):
                pool.indirect_dma_start(ring[:, slot, :], None, a["experts"],
                                        bass.IndirectOffsetOnAxis(ap=source, axis=0)).then_inc(got[slot], 16)

            def head(i):
                for t in range(NT):
                    for k in range(TOPK):
                        x = TOPK * t + k
                        if not (first(i) and x < SLOTS):
                            pool.wait_ge(used, i * ROWS + (x - SLOTS + 1))
                            pool.nop(nofuse=True)
                        if k == 0:
                            for src, dst in ((m["idx_all"], cur), (m["gate_all"], curg)):
                                pool.tensor_copy(dst[:, t, :], src[:, i, t, :] if isinstance(i, int) else
                                                 src[:, bass.ds(i, 1), t, :].rearrange("p o k -> p (o k)")).then_inc(cur_set, 1)
                            pool.wait_ge(cur_set, i * (2 * NT) + 2 * (t + 1))
                            pool.nop(nofuse=True)
                        gather(x % SLOTS, cur[:, t, k:k + 1])

            iterations(pool, head)

        @block.tensor
        def _(pe):
            def add_values(i, e):
                tt = e % GRP
                g0 = (e - tt - GRP) % 8
                n = i * ET + e
                if tt == 0:
                    pe.wait_ge(act_gated, n)
                if not (first(i) and e < GRP + 2):
                    pe.wait_ge(v_added, i * (2 * ET) + 2 * (e - GRP - 1))
                for half in range(2):
                    for y in range(GRP):
                        mm = nc.tensor.matmul(vp[tt % 2][:, 512 * half:512 * (half + 1)], w[:, g0 + y, P * tt:P * (tt + 1)],
                                              vals[:, g0 + y, 512 * half:512 * (half + 1)], start=(y == 0), stop=(y == GRP - 1))
                mm.then_inc(v_filled, 1)

            def tiles(i):
                for e in range(ET):
                    if not (first(i) and e < GRP):
                        add_values(i, e)

            for half in range(2):
                for q in range(4):
                    mm = nc.tensor.matmul(ss[0:NEW, 512 * half:512 * (half + 1)], m["ident"][:, NEW * q:NEW * (q + 1)],
                                          m["acc"][:, TILES, 512 * half:512 * (half + 1)], start=(q == 0), stop=(q == 3))
            mm.then_inc(summed, 1)
            iterations(pe, tiles)
            for e in range(GRP):
                add_values(HEADS, e)

        @block.scalar
        def _(act):
            def weight(i, x, gate):
                c = x % 8
                act.wait_ge(dotted, i * ROWS + (x + 1))
                if not (first(i) and x < 8):
                    act.wait_ge(used, i * ROWS + (x - 7))
                nc.scalar.activation(gel[:, c:c + 1], dots[:, c:c + 1], ACT.Gelu).then_inc(gelud, 1)
                act.wait_ge(gelud, i * ROWS + (x + 1))
                nc.scalar.activation(coef[:, c:c + 1], gel[:, c:c + 1], ACT.Copy, scale=gate).then_inc(weighed, 1)

            def tiles(i):
                for x in range(ROWS):
                    weight(i, x, curg[:, x // TOPK, x % TOPK:x % TOPK + 1])
                    if first(i) and x % PER == PER - 1:
                        for k, at in enumerate(norm_at):
                            if at == x // PER + GRP:
                                norm.root(act, k)
                            if at + 1 == x // PER + GRP:
                                norm.scale(act, k)

            iterations(act, tiles)

        @block.vector
        def _(dve):
            def dot(i, x, h):
                slot = x % SLOTS
                dve.wait_ge(got[slot], i * (16 * ROWS // SLOTS) + 16 * (x // SLOTS + 1))
                if not (first(i) and x == 0):
                    dve.wait_ge(dotted, i * ROWS + x)
                if not (first(i) and x < 8):
                    dve.wait_ge(gelud, i * ROWS + (x - 7))
                nc.vector.scalar_tensor_tensor(junk[:], ring[:, slot, 0:D], 1.0, h, ALU.mult, ALU.mult,
                                               accum_out=dots[:, x % 8:x % 8 + 1]).then_inc(dotted, 1)

            def value(i, x, sum_):
                dve.wait_ge(weighed, i * ROWS + (x + 1))
                if not (first(i) and x == 0):
                    dve.wait_ge(used, i * ROWS + x)
                nc.vector.scalar_tensor_tensor(sum_, ring[:, x % SLOTS, D:2 * D], coef[:, x % 8:x % 8 + 1], sum_,
                                               ALU.mult, ALU.add).then_inc(used, 1)

            def add_dense(i, e):
                tt = e % GRP
                dve.wait_ge(v_filled, i * ET + (e - GRP + 1))
                for half in range(2):
                    cols = slice(512 * half, 512 * (half + 1))
                    sum_ = m["acc"][:, GATHER + tt, cols]
                    nc.vector.tensor_tensor(sum_, sum_, vp[tt % 2][:, cols], ALU.add).then_inc(v_added, 1)

            def rows(i, e):
                for x in range(PER * e, PER * (e + 1)):
                    t = EARLY + x // TOPK
                    dot(i, x, m["h"][:, t, :])
                    if x % TOPK >= LAG:
                        value(i, x - LAG, m["acc"][:, t, :])
                    if x % TOPK == TOPK - 1:
                        for z in range(x - LAG + 1, x + 1):
                            value(i, z, m["acc"][:, t, :])

            def tiles(i):
                for e in range(ET):
                    n = i * ET + e
                    dve.wait_ge(gts_in[e % 4], i * (ET // 4 * 16) + 16 * (e // 4 + 1))
                    dve.wait_ge(tile_in[e % 8], i * (ET // 8 * 32) + 32 * (e // 8 + 1))
                    nc.vector.tensor_tensor(w[:, e % 8, :], w[:, e % 8, :], gts[:, e % 4, :], ALU.mult).then_inc(act_gated, 1)
                    if e >= GRP:
                        rows(i, e - GRP)
                    elif not first(i):
                        rows(i - 1, e - GRP + ET)
                    if not (first(i) and e < GRP):
                        if not (first(i) and e < 2 * GRP):
                            dve.wait_ge(v_added, i * (2 * ET) + 2 * (e - 2 * GRP + 1))
                        add_dense(i, e)
                    for k, at in enumerate(norm_at):
                        if first(i) and at == e:
                            norm.statistics(dve, k)
                        if first(i) and at + 1 == e:
                            norm.inverse(dve, k)
                        if first(i) and at + 2 == e:
                            if k == 0:
                                dve.wait_ge(norm.gb_in, 32)
                            norm.gain(dve, k)
                            norm.offset(dve, k)

            dve.wait_ge(summed, 1)
            nc.vector.tensor_copy(m["acc"][0:NEW, TILES, :], ss[0:NEW, :]).then_inc(sample_set, 1)
            dve.wait_ge(sample_set, 1)
            iterations(dve, tiles)
            for e in range(GRP):
                rows(HEADS - 1, ET - GRP + e)
                dve.wait_ge(v_added, HEADS * 2 * ET + 2 * (e - 2 * GRP + 1))
                add_dense(HEADS, e)
            dve.wait_ge(used, HEADS * ROWS)
            dve.wait_ge(v_added, 2 * HEADS * ET)


def last_norm(nc, mem, a, m, norm):
    with ExitStack() as s:
        rest = range(norm.FIRST, TILES + 1)
        block = s.enter_context(nc.Block())

        @block.sync
        def _(sp):
            for k in rest:
                norm.store(sp, a, k)
            sp.wait_ge(norm.out_done, 16 * (TILES + 1))

        @block.scalar
        def _(act):
            for k in range(rest.start, rest.stop + 1):
                if k < rest.stop:
                    norm.root(act, k)
                if k > rest.start:
                    norm.scale(act, k - 1)

        @block.vector
        def _(dve):
            for k in range(rest.start, rest.stop + 2):
                if k < rest.stop:
                    norm.statistics(dve, k)
                if rest.start < k <= rest.stop:
                    norm.inverse(dve, k - 1)
                if k > rest.start + 1:
                    norm.gain(dve, k - 2)

        @block.gpsimd
        def _(pool):
            for k in rest:
                norm.offset(pool, k)


def kernel(x_prompt, x_sample, cache_sb_k, cache_sb_v, cache_mla_ckv, cache_mla_kpe, w_in, q_norm_g, w_uq, kv_norm_g,
           w_uk, w_uv, w_oa, w_ob, w_out, ln1_g, ln1_b, peer_wq, peer_sub_keys, peer_u, peer_v, ln2_g, ln2_b):
    import numpy as np
    import concourse.bacc as bacc
    from concourse.bass_utils import run_bass_kernel_spmd

    half = RD // 2
    swap = np.concatenate([np.arange(half, RD), np.arange(half)])
    x = np.concatenate([np.asarray(x_prompt)[0], np.asarray(x_sample)[0]], axis=0)
    w_in0, w_uq0 = np.asarray(w_in)[0], np.asarray(w_uq)[0]
    c_kr = 3 * SBW + QL + KVL
    positions = np.concatenate([np.arange(SEQ), PAST + np.arange(NEW)]).astype(np.float32)
    rates = (np.float32(10000.0) ** (-np.arange(half, dtype=np.float32) / np.float32(half))).astype(np.float32)
    angles = rates[:, None] * positions[None, :]
    cos, sin = np.cos(angles), np.sin(angles)
    arrays = {
        "x": x,
        "xT": x.T,
        "w_in": w_in0,
        "w_kr_swapped": w_in0[:, c_kr:c_kr + RD][:, swap],
        "past_sb_kT": np.asarray(cache_sb_k)[0, 0].reshape(PAST, SBW).T,
        "past_sb_v": np.asarray(cache_sb_v)[0, 0].reshape(PAST, SBW),
        "past_ckvT": np.asarray(cache_mla_ckv)[0, 0].T,
        "past_kpeT": np.asarray(cache_mla_kpe)[0, 0].T,
        "cosT": np.concatenate([cos, cos], axis=0),
        "sinT": np.concatenate([-sin, sin], axis=0),
        "norm_gains": np.concatenate([np.asarray(q_norm_g)[0], np.asarray(kv_norm_g)[0]]).reshape(QC + VC, P).T,
        "w_uq": w_uq0,
        "w_uq_swapped": w_uq0.reshape(QL, HEADS, MD)[:, :, HD:][:, :, swap].reshape(QL, HEADS * RD),
        "w_uk": np.asarray(w_uk)[0],
        "w_uv": np.asarray(w_uv)[0],
        "w_oa": np.asarray(w_oa)[0],
        "w_ob": np.asarray(w_ob)[0],
        "w_out": np.asarray(w_out)[0],
        "ln1_g": np.asarray(ln1_g)[0],
        "ln1_b": np.asarray(ln1_b)[0],
        "peer_wq": np.asarray(peer_wq)[0],
        "sub_keysT": np.asarray(peer_sub_keys)[0].transpose(0, 1, 3, 2).reshape(HEADS * 2 * PKEYS, PKEYS),
        "experts": np.concatenate([np.asarray(peer_u)[0], np.asarray(peer_v)[0]], axis=1),
        "key_columns": np.asarray(peer_u)[0].reshape(EXPERTS // P, P, KC, P).transpose(0, 3, 2, 1),
        "ln2_g": np.asarray(ln2_g)[0],
        "ln2_b": np.asarray(ln2_b)[0],
    }
    arrays = {k: np.ascontiguousarray(v) for k, v in arrays.items()}
    nc = bacc.Bacc("TRN2", target_bir_lowering=False, num_devices=1)
    a = {k: nc.dram_tensor(f"in_{k}", v.shape, F32, kind="ExternalInput").ap() for k, v in arrays.items()}
    a["gates_by_expert"] = nc.dram_tensor("gates_by_expert", (EXPERTS * P * DENSE, 1), F32).ap()
    a["dense_acts"] = nc.dram_tensor("dense_acts", (EXPERTS, P * DENSE), F32).ap()
    a["gatesT"] = nc.dram_tensor("gatesT", (2 * D, TOKENS), F32).ap()
    outs = {"out_y": (TOKENS, D), "out_kT": (SBW, TOKENS), "out_v": (TOKENS, SBW), "out_ckvT": (KVL, TOKENS), "out_kpeT": (RD, TOKENS)}
    for k, shape in outs.items():
        a[k] = nc.dram_tensor(k, shape, F32, kind="ExternalOutput").ap()
    hybrid_stream_step(nc, a)
    r = run_bass_kernel_spmd(nc, [{f"in_{k}": v for k, v in arrays.items()}], core_ids=[0]).results[0]
    y, v = r["out_y"], r["out_v"]
    k, ckv, kpe = (np.ascontiguousarray(r[n].T) for n in ("out_kT", "out_ckvT", "out_kpeT"))

    def state(z, rows, *tail):
        return z[rows].reshape(1, 1, -1, *tail)

    both = (slice(0, SEQ), slice(SEQ, TOKENS))
    new = [[state(k, w, HEADS, HD), state(v, w, HEADS, HD), state(ckv, w, KVL), state(kpe, w, RD)] for w in both]
    return (y[both[0]].reshape(1, SEQ, D), y[both[1]].reshape(1, NEW, D), *new[0], *new[1])
```
